# Optimizing a Trainium2 kernel written in Bass

```python
import jax, jax.numpy as jnp
from jax import lax
import numpy as np
import math

D_MODEL = 1024
BATCH = 1
SEQ = 512
DEPTH = 2

HEAD_DIM = 64
MIX_WIDTH = D_MODEL
ATT_Q_HEADS = (MIX_WIDTH // 2) // HEAD_DIM
ATT_KV_HEADS = 2
ATT_GROUP = ATT_Q_HEADS // ATT_KV_HEADS
ATT_WIDTH = ATT_Q_HEADS * HEAD_DIM
ATT_KV_WIDTH = ATT_KV_HEADS * HEAD_DIM
WINDOW = 128
BLOCK = 128
RWKV_HEADS = (MIX_WIDTH // 4) // HEAD_DIM
RWKV_WIDTH = RWKV_HEADS * HEAD_DIM
DECAY_LORA = 64
ICLR_LORA = 64
GATE_LORA = 128
RWKV_GN_EPS = 64e-5
CONV_WIDTH = MIX_WIDTH - ATT_WIDTH - RWKV_WIDTH
CONV_K = 3
ATT_PROJ_WIDTH = ATT_WIDTH + 2 * ATT_KV_WIDTH
RWKV_SIZES = (RWKV_WIDTH, RWKV_WIDTH, RWKV_WIDTH, DECAY_LORA, ICLR_LORA, GATE_LORA)
RWKV_PROJ_WIDTH = 3 * RWKV_WIDTH + DECAY_LORA + ICLR_LORA + GATE_LORA
CONV_PROJ_WIDTH = 3 * CONV_WIDTH
PROJ_WIDTH = ATT_PROJ_WIDTH + RWKV_PROJ_WIDTH + CONV_PROJ_WIDTH
D_FF = 2816
N_MOD = 9
EPS = 1e-6


def rms_norm(x, gain):
    xf = x.astype(jnp.float32)
    y = xf * lax.rsqrt(jnp.mean(xf * xf, axis=-1, keepdims=True) + EPS)
    return (y * gain.astype(jnp.float32)).astype(x.dtype)

def swiglu(x, w_in, w_out):
    gate, up = jnp.split(x @ w_in, 2, axis=-1)
    return (jax.nn.silu(gate) * up) @ w_out

def token_shift(p):
    return jnp.pad(p, ((0, 0), (1, 0), (0, 0)))[:, :-1]

def sliding_window_sink_attention(qkv, q_gain, k_gain, sinks):
    B, T, _ = qkv.shape
    nb = T // BLOCK
    q, k, v = jnp.split(qkv, [ATT_WIDTH, ATT_WIDTH + ATT_KV_WIDTH], axis=-1)
    q = rms_norm(q.reshape(B, T, ATT_Q_HEADS, HEAD_DIM), q_gain)
    k = rms_norm(k.reshape(B, T, ATT_KV_HEADS, HEAD_DIM), k_gain)
    v = v.reshape(B, T, ATT_KV_HEADS, HEAD_DIM)
    qb = q.reshape(B, nb, BLOCK, ATT_KV_HEADS, ATT_GROUP, HEAD_DIM)

    def band(z):
        zb = z.reshape(B, nb, BLOCK, ATT_KV_HEADS, HEAD_DIM)
        prev = jnp.pad(zb, ((0, 0), (1, 0), (0, 0), (0, 0), (0, 0)))[:, :-1]
        return jnp.concatenate([prev, zb], axis=2)

    kb, vb = band(k), band(v)
    scores = jnp.einsum('bnqhgd,bnkhd->bnhgqk', qb, kb).astype(jnp.float32) * (HEAD_DIM ** -0.5)
    blk = jnp.arange(nb)[:, None, None] * BLOCK
    q_pos = blk + jnp.arange(BLOCK)[None, :, None]
    k_pos = blk - BLOCK + jnp.arange(2 * BLOCK)[None, None, :]
    diff = q_pos - k_pos
    mask = (k_pos >= 0) & (diff >= 0) & (diff < WINDOW)
    scores = jnp.where(mask[None, :, None, None], scores, -jnp.inf)
    sink = sinks.astype(jnp.float32).reshape(ATT_KV_HEADS, ATT_GROUP)[None, None, :, :, None, None]
    sink = jnp.broadcast_to(sink, scores.shape[:-1] + (1,))
    probs = jax.nn.softmax(jnp.concatenate([scores, sink], axis=-1), axis=-1)[..., :-1]
    out = jnp.einsum('bnhgqk,bnkhd->bnqhgd', probs.astype(v.dtype), vb)
    return out.reshape(B, T, ATT_WIDTH)

def rwkv7_time_mix(p, mu, w0, w_w2, a0, w_a2, w_g2, k_k, k_a, r_k, gn_w, gn_b):
    B, T, _ = p.shape
    f32 = jnp.float32
    p = p + mu * (token_shift(p) - p)
    r, k, v, wd, ad, gd = jnp.split(p, np.cumsum(RWKV_SIZES)[:-1].tolist(), axis=-1)
    r, k, v = r.astype(f32), k.astype(f32), v.astype(f32)
    w_log = -jax.nn.softplus(-(w0 + jnp.tanh(wd) @ w_w2).astype(f32)) - 0.5
    decay = jnp.exp(-jnp.exp(w_log))
    a = jax.nn.sigmoid((a0 + ad @ w_a2).astype(f32))
    g = (jax.nn.sigmoid(gd) @ w_g2).astype(f32)
    kk = (k * k_k).reshape(B, T, RWKV_HEADS, HEAD_DIM)
    kk = kk / jnp.maximum(jnp.linalg.norm(kk, axis=-1, keepdims=True), 1e-12)
    k = k * (1.0 + (a - 1.0) * k_a)
    hs = lambda z: z.reshape(B, T, RWKV_HEADS, HEAD_DIM)
    r, k, v, a, decay = hs(r), hs(k), hs(v), hs(a), hs(decay)

    def step(S, inp):
        r_t, w_t, k_t, v_t, kk_t, a_t = inp
        s_kk = jnp.einsum('bhvk,bhk->bhv', S, kk_t)
        S = (S * w_t[:, :, None, :] - s_kk[..., None] * (kk_t * a_t)[:, :, None, :]
             + v_t[..., None] * k_t[:, :, None, :])
        return S, jnp.einsum('bhvk,bhk->bhv', S, r_t)

    xs = tuple(jnp.swapaxes(z, 0, 1) for z in (r, decay, k, v, kk, a))
    S0 = jnp.zeros((B, RWKV_HEADS, HEAD_DIM, HEAD_DIM), f32)
    _, y = lax.scan(step, S0, xs)
    y = jnp.swapaxes(y, 0, 1)
    mean = jnp.mean(y, axis=-1, keepdims=True)
    var = jnp.mean(jnp.square(y - mean), axis=-1, keepdims=True)
    y = ((y - mean) * lax.rsqrt(var + RWKV_GN_EPS)).reshape(B, T, RWKV_WIDTH) * gn_w + gn_b
    bonus = jnp.sum(r * k * r_k, axis=-1, keepdims=True) * v
    y = (y + bonus.reshape(B, T, RWKV_WIDTH)) * g
    return y.astype(p.dtype)

def short_conv_mix(p, conv_w):
    b_gate, c_gate, h = jnp.split(p, [CONV_WIDTH, 2 * CONV_WIDTH], axis=-1)
    u = c_gate * h
    y = lax.conv_general_dilated(u, conv_w[:, None, :].astype(u.dtype), window_strides=(1,),
                                 padding=[(CONV_K - 1, 0)], dimension_numbers=('NWC', 'WIO', 'NWC'),
                                 feature_group_count=CONV_WIDTH)
    return b_gate * y

def first_inputs(seed: int = 0) -> dict:
    key = jax.random.key(seed)
    ks = iter(jax.random.split(key, 32))
    nrm = lambda shape, s: jax.random.normal(next(ks), shape, jnp.float32) * s
    L, D = DEPTH, D_MODEL
    return {
        'x': nrm((BATCH, SEQ, D), 1.0),
        'c': nrm((BATCH, D), 1.0),
        'w_ada': nrm((L, D, N_MOD * D), 0.1 * D ** -0.5),
        'b_ada': nrm((L, N_MOD * D), 0.01),
        'g_ffn1': 1.0 + nrm((L, D), 0.05),
        'w_ffn1_in': nrm((L, D, 2 * D_FF), D ** -0.5),
        'w_ffn1_out': nrm((L, D_FF, D), D_FF ** -0.5),
        'g_mix': 1.0 + nrm((L, D), 0.05),
        'w_mix_in': nrm((L, D, PROJ_WIDTH), D ** -0.5),
        'w_mix_out': nrm((L, MIX_WIDTH, D), MIX_WIDTH ** -0.5),
        'att_q_gain': 1.0 + nrm((L, HEAD_DIM), 0.05),
        'att_k_gain': 1.0 + nrm((L, HEAD_DIM), 0.05),
        'att_sinks': nrm((L, ATT_Q_HEADS), 1.0),
        'rwkv_mu': jax.random.uniform(next(ks), (L, RWKV_PROJ_WIDTH), jnp.float32),
        'rwkv_w0': jax.random.uniform(next(ks), (L, RWKV_WIDTH), jnp.float32, -6.0, -1.0),
        'rwkv_w_w2': nrm((L, DECAY_LORA, RWKV_WIDTH), 0.1 * DECAY_LORA ** -0.5),
        'rwkv_a0': nrm((L, RWKV_WIDTH), 0.1),
        'rwkv_a_w2': nrm((L, ICLR_LORA, RWKV_WIDTH), 0.1 * ICLR_LORA ** -0.5),
        'rwkv_g_w2': nrm((L, GATE_LORA, RWKV_WIDTH), GATE_LORA ** -0.5),
        'rwkv_k_k': 1.0 + nrm((L, RWKV_WIDTH), 0.1),
        'rwkv_k_a': 1.0 + nrm((L, RWKV_WIDTH), 0.1),
        'rwkv_r_k': nrm((L, RWKV_HEADS, HEAD_DIM), 0.1),
        'rwkv_gn_w': 1.0 + nrm((L, RWKV_WIDTH), 0.05),
        'rwkv_gn_b': nrm((L, RWKV_WIDTH), 0.01),
        'conv_w': nrm((L, CONV_K, CONV_WIDTH), CONV_K ** -0.5),
        'g_ffn2': 1.0 + nrm((L, D), 0.05),
        'w_ffn2_in': nrm((L, D, 2 * D_FF), D ** -0.5),
        'w_ffn2_out': nrm((L, D_FF, D), D_FF ** -0.5),
    }

def first_block(x, c, w_ada, b_ada, g_ffn1, w_ffn1_in, w_ffn1_out, g_mix, w_mix_in, w_mix_out,
              att_q_gain, att_k_gain, att_sinks, rwkv_mu, rwkv_w0, rwkv_w_w2, rwkv_a0, rwkv_a_w2,
              rwkv_g_w2, rwkv_k_k, rwkv_k_a, rwkv_r_k, rwkv_gn_w, rwkv_gn_b, conv_w,
              g_ffn2, w_ffn2_in, w_ffn2_out):
    h = x
    B = x.shape[0]
    c_act = jax.nn.silu(c)
    for l in range(DEPTH):
        mod = (c_act @ w_ada[l] + b_ada[l]).reshape(B, N_MOD, D_MODEL)
        sh1, sc1, gt1, sh2, sc2, gt2, sh3, sc3, gt3 = [mod[:, i, None, :] for i in range(N_MOD)]
        hn = rms_norm(h, g_ffn1[l]) * (1.0 + sc1) + sh1
        h = h + 0.5 * (1.0 + gt1) * swiglu(hn, w_ffn1_in[l], w_ffn1_out[l])
        hn = rms_norm(h, g_mix[l]) * (1.0 + sc2) + sh2
        proj = hn @ w_mix_in[l]
        p_att, p_rwkv, p_conv = jnp.split(proj, [ATT_PROJ_WIDTH, ATT_PROJ_WIDTH + RWKV_PROJ_WIDTH], axis=-1)
        y_att = sliding_window_sink_attention(p_att, att_q_gain[l], att_k_gain[l], att_sinks[l])
        y_rwkv = rwkv7_time_mix(p_rwkv, rwkv_mu[l], rwkv_w0[l], rwkv_w_w2[l], rwkv_a0[l], rwkv_a_w2[l],
                                rwkv_g_w2[l], rwkv_k_k[l], rwkv_k_a[l], rwkv_r_k[l], rwkv_gn_w[l], rwkv_gn_b[l])
        y_conv = short_conv_mix(p_conv, conv_w[l])
        mixed = jnp.concatenate([y_att, y_rwkv, y_conv], axis=-1) @ w_mix_out[l]
        h = h + (1.0 + gt2) * mixed
        hn = rms_norm(h, g_ffn2[l]) * (1.0 + sc3) + sh3
        h = h + 0.5 * (1.0 + gt3) * swiglu(hn, w_ffn2_in[l], w_ffn2_out[l])
    return h


GRID_W = 64
CTX_LEN = 256
D_MIX = D_MODEL
MLSTM_HEADS = 4
MLSTM_WIDTH = D_MIX // 2
MLSTM_HD = MLSTM_WIDTH // MLSTM_HEADS
MLSTM_CHUNK = 64
SHORT_CONV = 3
N_GATES = 4 * MLSTM_HEADS
FOURIER_HEADS = 4
FOURIER_WIDTH = D_MIX // 4
FOURIER_HD = FOURIER_WIDTH // FOURIER_HEADS
CONV_WIDTH_2 = D_MIX - MLSTM_WIDTH - FOURIER_WIDTH
CONV_K_2 = 31
D_FF_2 = 4 * D_MODEL
Q_OFF = 0
K_OFF = MLSTM_WIDTH
V_OFF = 2 * MLSTM_WIDTH
O_OFF = 3 * MLSTM_WIDTH
G_OFF = 4 * MLSTM_WIDTH
MLSTM_COLS = 4 * MLSTM_WIDTH + N_GATES
F_OFF = MLSTM_COLS
C_OFF = F_OFF + FOURIER_WIDTH
P_IN = C_OFF + 2 * CONV_WIDTH_2
POS_BASE = 10000.0


def rmsnorm(x, g):
    xf = x.astype(jnp.float32)
    y = xf * lax.rsqrt(jnp.mean(xf * xf, axis=-1, keepdims=True) + EPS)
    return (y * g.astype(jnp.float32)).astype(x.dtype)

def layernorm(x, g, b):
    xf = x.astype(jnp.float32)
    mu = jnp.mean(xf, axis=-1, keepdims=True)
    var = jnp.mean(jnp.square(xf - mu), axis=-1, keepdims=True)
    y = (xf - mu) * lax.rsqrt(var + EPS)
    return (y * g.astype(jnp.float32) + b.astype(jnp.float32)).astype(x.dtype)

def modulate(h, shift, scale):
    return h * (1 + scale) + shift

def grid_sincos(rows, d):
    quarter = d // 4
    freq = jnp.exp(-math.log(POS_BASE) * jnp.arange(quarter, dtype=jnp.float32) / quarter)
    r = jnp.broadcast_to(jnp.arange(rows, dtype=jnp.float32)[:, None], (rows, GRID_W)).reshape(-1)
    col = jnp.broadcast_to(jnp.arange(GRID_W, dtype=jnp.float32)[None, :], (rows, GRID_W)).reshape(-1)
    ar = r[:, None] * freq
    ac = col[:, None] * freq
    return jnp.concatenate([jnp.sin(ar), jnp.cos(ar), jnp.sin(ac), jnp.cos(ac)], axis=-1)

def dwconv(u, w):
    k = w.shape[0]
    ch = u.shape[-1]
    return lax.conv_general_dilated(u, w[:, None, :], window_strides=(1,), padding=[(k // 2, k // 2)],
                                    dimension_numbers=('NWC', 'WIO', 'NWC'), feature_group_count=ch)

def mlstm_chunked(q, k, v, li, lf, state):
    b_, h_, t_, hd = q.shape
    nc = t_ // MLSTM_CHUNK
    L = MLSTM_CHUNK

    def to_chunks(a):
        return jnp.moveaxis(a.reshape(a.shape[:2] + (nc, L) + a.shape[3:]), 2, 0)

    tri = jnp.tril(jnp.ones((L, L), dtype=bool))

    def step(carry, inp):
        C, n, m = carry
        qc, kc, vc, lic, lfc = inp
        bcum = jnp.cumsum(lfc, axis=-1)
        a = bcum + m[..., None]
        D = bcum[..., :, None] - bcum[..., None, :] + lic[..., None, :]
        D = jnp.where(tri, D, -jnp.inf)
        m_t = jnp.maximum(a, jnp.max(D, axis=-1))
        w_inter = jnp.exp(a - m_t)
        S = jnp.einsum('bhld,bhsd->bhls', qc, kc) * jnp.exp(D - m_t[..., None])
        num = w_inter[..., None] * jnp.einsum('bhed,bhld->bhle', C, qc) + jnp.einsum('bhls,bhse->bhle', S, vc)
        den = w_inter * jnp.einsum('bhd,bhld->bhl', n, qc) + jnp.sum(S, axis=-1)
        h = num / jnp.maximum(jnp.abs(den), jnp.exp(-m_t))[..., None]
        bl = bcum[..., -1]
        g = bl[..., None] - bcum + lic
        m_new = jnp.maximum(bl + m, jnp.max(g, axis=-1))
        decay = jnp.exp(bl + m - m_new)
        ws = jnp.exp(g - m_new[..., None])
        C_new = decay[..., None, None] * C + jnp.einsum('bhs,bhse,bhsd->bhed', ws, vc, kc)
        n_new = decay[..., None] * n + jnp.einsum('bhs,bhsd->bhd', ws, kc)
        return (C_new, n_new, m_new), h

    final, hs = lax.scan(step, state, (to_chunks(q), to_chunks(k), to_chunks(v), to_chunks(li), to_chunks(lf)))
    h = jnp.moveaxis(hs, 0, 2).reshape(b_, h_, t_, hd)
    return h, final

def mlstm_heads(z, w_qk_conv, b_gate):
    b_, t_, _ = z.shape
    qk = dwconv(z[..., Q_OFF:V_OFF], w_qk_conv)

    def heads(a):
        return a.reshape(b_, t_, MLSTM_HEADS, MLSTM_HD).transpose(0, 2, 1, 3).astype(jnp.float32)

    q = heads(qk[..., :MLSTM_WIDTH])
    k = heads(qk[..., MLSTM_WIDTH:]) * (MLSTM_HD ** -0.5)
    v = heads(z[..., V_OFF:O_OFF])
    gates = (z[..., G_OFF:G_OFF + N_GATES].reshape(b_, t_, 4, MLSTM_HEADS) + b_gate).astype(jnp.float32)
    gates = gates.transpose(2, 0, 3, 1)
    fwd = (gates[0], jax.nn.log_sigmoid(gates[1]))
    bwd = (gates[2], jax.nn.log_sigmoid(gates[3]))
    return q, k, v, fwd, bwd

def mlstm_out(h, o_pre, g):
    b_, h_, t_, hd = h.shape
    mu = jnp.mean(h, axis=-1, keepdims=True)
    var = jnp.mean(jnp.square(h - mu), axis=-1, keepdims=True)
    hn = ((h - mu) * lax.rsqrt(var + EPS)).transpose(0, 2, 1, 3).reshape(b_, t_, h_ * hd)
    return (hn * g.astype(jnp.float32) * jax.nn.sigmoid(o_pre.astype(jnp.float32))).astype(o_pre.dtype)

def mlstm_mixer(zx, zc, w_qk_conv, b_gate, g_norm, need_ctx):
    qx, kx, vx, fx, bx = mlstm_heads(zx, w_qk_conv, b_gate)
    qc, kc, vc, fc, bc = mlstm_heads(zc, w_qk_conv, b_gate)
    bsz = zx.shape[0]
    zero = (jnp.zeros((bsz, MLSTM_HEADS, MLSTM_HD, MLSTM_HD), jnp.float32),
            jnp.zeros((bsz, MLSTM_HEADS, MLSTM_HD), jnp.float32),
            jnp.zeros((bsz, MLSTM_HEADS), jnp.float32))

    def fl(a):
        return jnp.flip(a, axis=2)

    hc_f, st_f = mlstm_chunked(qc, kc, vc, fc[0], fc[1], zero)
    hx_f, _ = mlstm_chunked(qx, kx, vx, fx[0], fx[1], st_f)
    hc_b, st_b = mlstm_chunked(fl(qc), fl(kc), fl(vc), fl(bc[0]), fl(bc[1]), zero)
    hx_b, _ = mlstm_chunked(fl(qx), fl(kx), fl(vx), fl(bx[0]), fl(bx[1]), st_b)
    yx = mlstm_out(hx_f + fl(hx_b), zx[..., O_OFF:G_OFF], g_norm)
    yc = mlstm_out(hc_f + fl(hc_b), zc[..., O_OFF:G_OFF], g_norm) if need_ctx else None
    return yx, yc

def fourier_mix(u):
    b_, t_, _ = u.shape
    uh = u.reshape(b_, t_, FOURIER_HEADS, FOURIER_HD).astype(jnp.float32)
    y = jnp.real(jnp.fft.fftn(uh, axes=(1, 3), norm='ortho'))
    return y.reshape(b_, t_, FOURIER_WIDTH).astype(u.dtype)

def conv_module(z, w_dw, b_dw, g_ln, b_ln):
    a, gt = z[..., :CONV_WIDTH_2], z[..., CONV_WIDTH_2:]
    u = a * jax.nn.sigmoid(gt)
    u = dwconv(u, w_dw) + b_dw
    return jax.nn.silu(layernorm(u, g_ln, b_ln))

def token_mixers(hx, hc, w_in, w_out, b_gate, w_qk_conv, g_mlstm_norm, w_dw, b_dw, g_conv_ln, b_conv_ln, need_ctx):
    zx = hx @ w_in
    zc = hc @ (w_in if need_ctx else w_in[:, :MLSTM_COLS])
    ym_x, ym_c = mlstm_mixer(zx, zc, w_qk_conv, b_gate, g_mlstm_norm, need_ctx)

    def merge(z, ym):
        yf = fourier_mix(z[..., F_OFF:C_OFF])
        yv = conv_module(z[..., C_OFF:P_IN], w_dw, b_dw, g_conv_ln, b_conv_ln)
        return jnp.concatenate([ym, yf, yv], axis=-1) @ w_out

    out_x = merge(zx, ym_x)
    out_c = merge(zc, ym_c) if need_ctx else None
    return out_x, out_c

def sq_relu_mlp(h, w1, w2):
    return jnp.square(jax.nn.relu(h @ w1)) @ w2

def second_inputs(seed: int = 0) -> dict:
    key = jax.random.key(seed)
    ks = jax.random.split(key, 24)
    f32 = jnp.float32
    L = DEPTH

    def nrm(k, shape, scale):
        return jax.random.normal(k, shape, f32) * scale

    def gain(k, shape):
        return 1.0 + nrm(k, shape, 0.05)

    return {
        'x': nrm(ks[0], (BATCH, SEQ, D_MODEL), 1.0),
        'c': nrm(ks[1], (BATCH, D_MODEL), 1.0),
        'ctx': nrm(ks[2], (BATCH, CTX_LEN, D_MODEL), 1.0),
        'c_ctx': nrm(ks[3], (D_MODEL,), 1.0),
        'w_ada': nrm(ks[4], (L, D_MODEL, 6 * D_MODEL), D_MODEL ** -0.5),
        'b_ada': nrm(ks[5], (L, 6 * D_MODEL), 0.02),
        'g_pre_mix': gain(ks[6], (L, D_MODEL)),
        'g_post_mix': gain(ks[7], (L, D_MODEL)),
        'g_pre_mlp': gain(ks[8], (L, D_MODEL)),
        'g_post_mlp': gain(ks[9], (L, D_MODEL)),
        'w_in': nrm(ks[10], (L, D_MODEL, P_IN), D_MODEL ** -0.5),
        'b_gate': jnp.array([0.0, 3.0, 0.0, 3.0], f32)[None, :, None] + nrm(ks[11], (L, 4, MLSTM_HEADS), 0.1),
        'w_qk_conv': nrm(ks[12], (L, SHORT_CONV, 2 * MLSTM_WIDTH), SHORT_CONV ** -0.5),
        'g_mlstm_norm': gain(ks[13], (L, MLSTM_WIDTH)),
        'w_dw': nrm(ks[14], (L, CONV_K_2, CONV_WIDTH_2), CONV_K_2 ** -0.5),
        'b_dw': nrm(ks[15], (L, CONV_WIDTH_2), 0.02),
        'g_conv_ln': gain(ks[16], (L, CONV_WIDTH_2)),
        'b_conv_ln': nrm(ks[17], (L, CONV_WIDTH_2), 0.02),
        'w_out': nrm(ks[18], (L, D_MIX, D_MODEL), D_MIX ** -0.5),
        'w_mlp1': nrm(ks[19], (L, D_MODEL, D_FF_2), D_MODEL ** -0.5),
        'w_mlp2': nrm(ks[20], (L, D_FF_2, D_MODEL), D_FF_2 ** -0.5),
    }

def second_block(x, c, ctx, c_ctx, w_ada, b_ada, g_pre_mix, g_post_mix, g_pre_mlp, g_post_mlp, w_in, b_gate,
              w_qk_conv, g_mlstm_norm, w_dw, b_dw, g_conv_ln, b_conv_ln, w_out, w_mlp1, w_mlp2):
    n_tok = x.shape[1]
    rows = n_tok // GRID_W
    x = x + grid_sincos(rows, x.shape[-1]).astype(x.dtype)[None]
    for l in range(DEPTH):
        need_ctx = l < DEPTH - 1
        mx = jnp.split((jax.nn.silu(c) @ w_ada[l] + b_ada[l])[:, None, :], 6, axis=-1)
        mc = jnp.split((jax.nn.silu(c_ctx) @ w_ada[l] + b_ada[l])[None, None, :], 6, axis=-1)
        hx = modulate(rmsnorm(x, g_pre_mix[l]), mx[0], mx[1])
        hc = modulate(rmsnorm(ctx, g_pre_mix[l]), mc[0], mc[1])
        out_x, out_c = token_mixers(hx, hc, w_in[l], w_out[l], b_gate[l], w_qk_conv[l], g_mlstm_norm[l],
                                    w_dw[l], b_dw[l], g_conv_ln[l], b_conv_ln[l], need_ctx)
        x = x + mx[2] * rmsnorm(out_x, g_post_mix[l])
        hx = modulate(rmsnorm(x, g_pre_mlp[l]), mx[3], mx[4])
        x = x + mx[5] * rmsnorm(sq_relu_mlp(hx, w_mlp1[l], w_mlp2[l]), g_post_mlp[l])
        if need_ctx:
            ctx = ctx + mc[2] * rmsnorm(out_c, g_post_mix[l])
            hc = modulate(rmsnorm(ctx, g_pre_mlp[l]), mc[3], mc[4])
            ctx = ctx + mc[5] * rmsnorm(sq_relu_mlp(hc, w_mlp1[l], w_mlp2[l]), g_post_mlp[l])
    return x


def setup_inputs(seed=0):
    out = dict(first_inputs(seed))
    for name, value in second_inputs(seed + 1).items():
        if name != "x":
            out[name + "_2"] = value
    return out


def reference(
    x, c, w_ada, b_ada, g_ffn1, w_ffn1_in, w_ffn1_out, g_mix, w_mix_in, w_mix_out, att_q_gain,
    att_k_gain, att_sinks, rwkv_mu, rwkv_w0, rwkv_w_w2, rwkv_a0, rwkv_a_w2, rwkv_g_w2, rwkv_k_k,
    rwkv_k_a, rwkv_r_k, rwkv_gn_w, rwkv_gn_b, conv_w, g_ffn2, w_ffn2_in, w_ffn2_out, c_2, ctx_2,
    c_ctx_2, w_ada_2, b_ada_2, g_pre_mix_2, g_post_mix_2, g_pre_mlp_2, g_post_mlp_2, w_in_2,
    b_gate_2, w_qk_conv_2, g_mlstm_norm_2, w_dw_2, b_dw_2, g_conv_ln_2, b_conv_ln_2, w_out_2,
    w_mlp1_2, w_mlp2_2,
):
    x = first_block(
        x, c, w_ada, b_ada, g_ffn1, w_ffn1_in, w_ffn1_out, g_mix, w_mix_in, w_mix_out,
        att_q_gain, att_k_gain, att_sinks, rwkv_mu, rwkv_w0, rwkv_w_w2, rwkv_a0, rwkv_a_w2,
        rwkv_g_w2, rwkv_k_k, rwkv_k_a, rwkv_r_k, rwkv_gn_w, rwkv_gn_b, conv_w, g_ffn2,
        w_ffn2_in, w_ffn2_out,
    )
    return second_block(
        x, c_2, ctx_2, c_ctx_2, w_ada_2, b_ada_2, g_pre_mix_2, g_post_mix_2, g_pre_mlp_2,
        g_post_mlp_2, w_in_2, b_gate_2, w_qk_conv_2, g_mlstm_norm_2, w_dw_2, b_dw_2,
        g_conv_ln_2, b_conv_ln_2, w_out_2, w_mlp1_2, w_mlp2_2,
    )


_drawn_inputs = setup_inputs


def setup_inputs(seed=0):
    import zlib

    import numpy as np

    out = dict(_drawn_inputs(seed))
    spreads = {}
    factors = {'att_q_gain': 5.88,
     'att_k_gain': 6.168,
     'att_sinks': 10.823,
     'rwkv_w_w2': 8.0,
     'rwkv_a0': 2.925,
     'rwkv_a_w2': 3.176,
     'rwkv_gn_w': 2.806,
     'rwkv_gn_b': 8.0,
     'g_mlstm_norm_2': 12.375,
     'b_dw_2': 8.0,
     'g_conv_ln_2': 12.567,
     'b_conv_ln_2': 33.431,
     'g_post_mix_2': 2.802,
     'g_pre_mlp_2': 2.76,
     'g_post_mlp_2': 2.88}
    for name, (base, spread) in spreads.items():
        noise = np.random.default_rng([zlib.crc32(name.encode()), seed]).standard_normal(out[name].shape)
        drawn = base * np.exp(spread * noise) if base else spread * noise
        out[name] = __import__('jax').numpy.asarray(drawn.astype(out[name].dtype))
    for name, factor in factors.items():
        out[name] = (out[name] * factor).astype(out[name].dtype)
    return out
```

```python
from contextlib import ExitStack, contextmanager

import numpy as np
import concourse.bass as bass
from concourse import mybir

F32 = mybir.dt.float32
F32R = mybir.dt.float32r
ALU = mybir.AluOpType
ACT = mybir.ActivationFunctionType
AX = mybir.AxisListType
ds = bass.ds

P = 128
D = 1024
T = 512
TC = 256
TT = TC + T
KD = D // P
DEPTH = 2
EPS = 1e-6
D_FF = 2816
FT = D_FF // P
PROJ1 = 2560
NP1 = PROJ1 // P
HD = 64
QH = 8
GN_EPS = 64e-5
DECAY_SCALE = float(np.exp(-0.5))
D_FF2 = 4096
MH = 4
G_OFF = 2048
F_OFF = 2064
C_OFF = F_OFF + 256
K2 = 31
BASE = 16
SLOTS = 4
AHEAD = 2
DEBUG = False

COLS1 = {}
COLS2 = {}


def _layout(table, items):
    at = 0
    for name, n in items:
        table[name] = (at, n)
        at += n
    return at


NC1 = _layout(COLS1, [("b_ada", 72), ("g_ffn1", 8), ("g_mix", 8), ("g_ffn2", 8), ("q_gain", 1), ("k_gain", 1),
                      ("sinks", 8), ("mu", 8), ("w0", 2), ("a0", 2), ("k_k", 2), ("k_a", 2), ("r_k", 2),
                      ("gn_w", 2), ("gn_b", 2), ("conv", 6)])
NC2 = _layout(COLS2, [("b_ada", 48), ("g_pre_mix", 8), ("g_post_mix", 8), ("g_pre_mlp", 8), ("g_post_mlp", 8),
                      ("qk_conv", 24), ("g_mlstm", 4), ("w_dw", 62), ("b_dw", 2), ("g_ln", 2), ("b_ln", 2),
                      ("b_gate", 1)])
CONST = {}
NCONST = _layout(CONST, [("ident", 128), ("blk", 128), ("attmask", 512), ("levels", 7 * 128), ("level0T", 128),
                         ("upper", 128), ("upper_eq", 128), ("lower_eq", 128), ("c64", 128), ("s64", 128),
                         ("sel", 512), ("cc", 24)])
RW_LEVELS = 7


class Counter:

    def __init__(self, sem, name, base):
        self.sem, self.name, self.const, self.terms = sem, name, base, []

    def now(self, more=0):
        return (self, self.const + more, tuple(self.terms))


class Queue:

    def __init__(self, eng, progress, chained):
        self.eng, self.progress, self.chained = eng, progress, chained
        self.last = None
        self.seen = {}

    def wait(self, *tokens):
        for t in tokens:
            if t is None:
                continue
            counter, const, terms = t
            key = (counter.name, tuple(id(i) for i, _ in terms))
            if self.seen.get(key, 0) >= const:
                continue
            self.seen[key] = const
            value = const
            for i, k in terms:
                if k:
                    value = i * k + value
            self.eng.wait_ge(counter.sem, value)

    def __call__(self, fn, *args, after=(), inc=None, **kw):
        self.wait(*after)
        if self.chained:
            self.wait(self.last)
        counter = inc or self.progress
        fn(*args, **kw).then_inc(counter.sem, 1)
        counter.const += 1
        self.last = counter.now()
        return self.last


class Program:
    def __init__(self, nc, per_loop):
        self.nc = nc
        self.per_loop = per_loop
        self.recorded = {}
        self.counters = []
        self.pe = Queue(nc.tensor, self.counter("pe"), False)
        self.act = Queue(nc.scalar, self.counter("act"), True)
        self.dve = Queue(nc.vector, self.counter("dve"), True)
        self.pool = Queue(nc.gpsimd, self.counter("pool"), True)
        self.sp = Queue(nc.sync, self.counter("sp"), False)
        self.queues = [self.pe, self.act, self.dve, self.pool, self.sp]
        self.entered = nc.alloc_semaphore("s_entered")

    def counter(self, name, base=BASE):
        c = Counter(self.nc.alloc_semaphore("s_" + name), name, base)
        if base:
            self.nc.sync.sem_inc(c.sem, base)
        self.counters.append(c)
        return c

    def mm(self, out, lhsT, rhs, start, stop, after=(), inc=None, done=False):
        self.pe.wait(*after)
        ins = self.nc.tensor.matmul(out, lhsT, rhs, start=start, stop=stop)
        return self._pe_done(ins, inc, done)

    def transpose(self, out, in_, ident, after=(), inc=None, done=False):
        self.pe.wait(*after)
        return self._pe_done(self.nc.tensor.transpose(out, in_, ident), inc, done)

    def _pe_done(self, ins, inc, done):
        if inc is None and not done:
            return None
        counter = inc or self.pe.progress
        ins.then_inc(counter.sem, 1)
        counter.const += 1
        self.pe.last = counter.now()
        return self.pe.last

    def dma(self, queue, out, in_, counter, after=()):
        queue.wait(*after)
        queue.eng.dma_start(out, in_).then_inc(counter.sem, 16)
        counter.const += 16
        return counter.now()

    def by_half(self, heads, one_head):
        for half in range(2):
            mine = [h for h in heads if h % 2 == half]
            for h in mine:
                one_head(h, h == mine[-1])
            self.pe.wait(self.pe.last)
        return self.pe.last

    def barrier(self):
        work = [self.pe, self.act, self.dve, self.pool]
        for q in work:
            for other in work:
                if other is not q:
                    q.wait(other.last)

    @contextmanager
    def loop(self, name, n):
        for q in self.queues:
            if q.chained:
                q.wait(q.last)
            q.seen = {}
        outside = {q: q.last for q in self.queues}
        for q in self.queues:
            q.last = None
        for q in (self.pe, self.dve, self.pool):
            q.eng.sem_inc(self.entered, 1)
        start = {c: c.const for c in self.counters}
        per = self.per_loop.get(name, {})
        with self.nc.Fori(0, n) as i:
            for c in self.counters:
                c.terms.append((i, per.get(c.name, 0)))
            yield i
            for q in self.queues:
                if q.chained:
                    q.wait(q.last)
            for c in self.counters:
                c.terms.pop()
        self.recorded[name] = {c.name: c.const - start[c] for c in self.counters}
        for c in self.counters:
            c.const = start[c] + n * (c.const - start[c])
        for q in self.queues:
            q.seen = {}
            q.last = q.last[0].now() if q.last else outside[q]


def build(nc, a, per_loop):
    prog = Program(nc, per_loop)
    pe, act, dve, pool, sp = prog.pe, prog.act, prog.dve, prog.pool, prog.sp
    mm = prog.mm
    v, s_, g_ = nc.vector, nc.scalar, nc.gpsimd

    top = [(nc.sbuf_base + 63) // 64 * 64]

    def fixed(name, shape, dt=F32):
        off = top[0]
        top[0] += (int(np.prod(shape[1:])) * 4 + 31) // 32 * 32
        return nc.alloc_sbuf_tensor_at(name, list(shape), dt, offset=off)

    const = fixed("const", [P, NCONST])
    ones = fixed("ones", [P, P])
    cols1_all = fixed("cols1_all", [P, DEPTH * NC1])
    cols2_all = fixed("cols2_all", [P, DEPTH * NC2])
    cols1 = fixed("cols1", [P, NC1])
    cols2 = fixed("cols2", [P, NC2])
    mod1 = fixed("mod1", [P, 72])
    mod2 = fixed("mod2", [P, DEPTH * 2 * 48])
    small = fixed("small", [P, 48])
    csil = fixed("csil", [P, 3, 8])
    csig = fixed("csig", [P, 3, 8])
    lora = fixed("lora", [P, 2, 256])
    XC = fixed("XC", [P, KD, TT])
    stage_at = top[0]
    stage = fixed("stage", [P, SLOTS, 8, P])
    WL = nc.alloc_sbuf_tensor_at("WL", [P, SLOTS, 8, P], F32R, offset=stage_at)
    WH = fixed("WH", [P, SLOTS, 8, P], F32R)
    tmpf = fixed("tmpf", [P, 4, T])
    R0 = top[0]
    RN = (nc.sbuf_usable_end - R0) // 32 * 8
    print("RN", RN, "free after G0", RN - 2 * KD * TT) if DEBUG else None
    used = set()

    def region(name, off, shape, dt=F32):
        assert off + int(np.prod(shape[1:])) <= RN, (name, off, shape, RN)
        assert name not in used
        used.add(name)
        return nc.alloc_sbuf_tensor_at(name, list(shape), dt, offset=R0 + 4 * off)

    HH = region("HH", 0, [P, KD, TT], F32R)
    HL = region("HL", KD * TT, [P, KD, TT], F32R)
    G0 = 2 * KD * TT
    H1H = region("H1H", 0, [P, KD, T], F32R)
    H1L = region("H1L", KD * TT, [P, KD, T], F32R)
    GH = region("GH", G0, [P, 8, TT], F32R)
    GL = region("GL", G0 + 8 * TT, [P, 8, TT], F32R)
    ADA0 = RN - 2 * 2048 - 512
    ada_w = region("ada_w", ADA0, [P, 2, 8, 256])
    ada_acc = region("ada_acc", ADA0 + 4096, [P, 2, 256])
    bank = [nc.alloc_psum_tensor(f"bank{j}", [P, 512], F32) for j in range(8)]

    def k_(name, n=None):
        o, w = CONST[name]
        return const[:, o:o + (n or w)]

    ident, blk = k_("ident"), k_("blk")

    stage_full = [prog.counter(f"stage_full{i}") for i in range(SLOTS)]
    split_done = [prog.counter(f"split_done{i}") for i in range(SLOTS)]
    unit_done = [prog.counter(f"unit_done{i}") for i in range(SLOTS)]
    bank_free = [prog.counter(f"bank_free{i}") for i in range(8)]
    ada_full = [prog.counter(f"ada_full{i}", 0) for i in range(2)]
    ada_ready = [prog.counter(f"ada_ready{i}") for i in range(2)]
    in_lora = prog.counter("in_lora")
    in_table = prog.counter("in_table")
    gates_in = prog.counter("gates_in")
    out_done = prog.counter("out_done")
    in_misc = prog.counter("in_misc")

    prog.dma(act, const[:], a["const"], in_misc)
    prog.dma(act, cols1_all[:], a["cols1"], in_misc)
    prog.dma(act, cols2_all[:], a["cols2"], in_misc)
    t_const = prog.dma(act, XC[:, :, TC:TT], a["xT"], in_misc)
    t_const = prog.dma(act, XC[:, :, 0:TC], a["ctxT"], in_misc)
    dve(v.memset, ones[:], 1.0)
    one_row = ones[:, 0:1]
    eps_col, gn_eps_col = small[:, 46:47], small[:, 47:48]
    dve(v.memset, eps_col, EPS)
    dve(v.memset, gn_eps_col, GN_EPS)

    cc = k_("cc").rearrange("p (a k) -> p a k", a=3)
    act(s_.activation, csig[:], cc, ACT.Sigmoid, after=[t_const])
    t_csil = dve(v.tensor_tensor, csil[:], cc, csig[:], ALU.mult, after=[act.last, t_const])

    state = {"n": 0, "split": 0, "ada": 0}

    def split_next():
        st = state["split"] % SLOTS
        state["split"] += 1
        t = act(s_.copy, WH[:, st], stage[:, st], after=[stage_full[st].now(16)])
        dve(v.tensor_tensor, WL[:, st], stage[:, st], WH[:, st].bitcast(F32), ALU.subtract,
            after=[t, stage_full[st].now(16)], inc=split_done[st])

    def load(src):
        st = state["n"] % SLOTS
        prog.dma(sp, stage[:, st], src, stage_full[st], after=[unit_done[st].now()])
        return st

    def unit(src, kt, segs, hi, lo, evict, ada=None):
        s = load(src)
        split_next()
        if ada and ada[0] == "begin":
            ada_begin(*ada[1:])
        outs = []
        pe.wait(split_done[s].now(), bank_free[s].now())
        for gi, (bo, t0, nt) in enumerate(segs):
            ps = bank[s + bo][:, 0:nt]
            for k in range(kt):
                passes = [(WH, hi), (WH, lo), (WL, hi)]
                for pi, (w, x) in enumerate(passes):
                    lastmm = k == kt - 1 and pi == 2
                    end = lastmm and gi == len(segs) - 1
                    mm(ps, w[:, s, KD - kt + k, :], x[:, k, t0:t0 + nt], k == 0 and pi == 0, lastmm,
                       inc=unit_done[s] if end else None)
            outs.append(ps)
        evict(outs, pe.last, bank_free[s])
        if ada and ada[0] == "finish":
            ada_finish(*ada[1:])
        state["n"] += 1

    def ada_begin(src, streams, *_):
        x = state["ada"] % 2
        state["ada"] += 1
        t = prog.dma(pool, ada_w[:, x], src, ada_full[x], after=[ada_ready[x].now()])
        for j, c in enumerate(streams):
            for k in range(KD):
                end = k == KD - 1 and j == len(streams) - 1
                inc = ada_ready[x] if end else None
                if k == 0:
                    dve(v.tensor_scalar, ada_acc[:, j], ada_w[:, x, 0], csil[:, c, 0:1], None, ALU.mult,
                        after=[t, t_csil], inc=inc)
                else:
                    dve(v.scalar_tensor_tensor, ada_acc[:, j], ada_w[:, x, k], csil[:, c, k:k + 1], ada_acc[:, j],
                        ALU.mult, ALU.add, inc=inc)

    def ada_finish(src, streams, out, bias):
        pe.wait(ada_ready[(state["ada"] - 1) % 2].now(), bank_free[7].now())
        for j in range(len(streams)):
            for h in range(2):
                mm(bank[7][:, 2 * j + h:2 * j + h + 1], ada_acc[:, j, h * P:(h + 1) * P], one_row, True, True,
                   done=(j == len(streams) - 1 and h == 1))
        t = pe.last
        for j in range(len(streams)):
            dve(v.tensor_tensor, out[j], bank[7][:, 2 * j:2 * j + 2], bias, ALU.add, after=[t],
                inc=bank_free[7] if j == len(streams) - 1 else None)

    wada1 = a["w_ada"].rearrange("l (k p) n -> l p k n", p=P)
    wada2 = a["w_ada_2"].rearrange("l (k p) n -> l p k n", p=P)

    def ada1(l, u):
        bias = cols1_all[:, ds(u * 2 + (l * NC1 + COLS1["b_ada"][0]), 2)]
        return wada1[l][:, :, ds(u * 256, 256)], (0,), [mod1[:, ds(u * 2, 2)]], bias

    def ada2(l, u):
        bias = cols2_all[:, ds(u * 2 + (l * NC2 + COLS2["b_ada"][0]), 2)]
        return (wada2[l][:, :, ds(u * 256, 256)], (1, 2),
                [mod2[:, ds(u * 2 + (l * 96 + 48 * j), 2)] for j in range(2)], bias)

    sq = tmpf

    def norm_sum(src_of, nt, bk, scale=1.0):
        for k in range(KD):
            b = k % 2
            t = act(s_.activation, sq[:, b, 0:nt], src_of(k), ACT.Square, scale=scale,
                    after=[pe.last, dve.last] if k < 2 else [tok[b]])
            if k == 0:
                tok = {}
                pe.wait(bank_free[bk].now())
            tok[b] = mm(bank[bk][:, 0:nt], ones[:], sq[:, b, 0:nt], k == 0, k == KD - 1, after=[t], done=True)
        return pe.last

    def rstd(out, ps, after, n_mean, eps, inc=None):
        act(s_.activation, out, ps, ACT.Ln, scale=1.0 / n_mean, bias=eps, after=[after, dve.last], inc=inc)
        return act(s_.activation, out, out, ACT.Exp, scale=-0.5)

    def split_store(hi, lo, exact, after=(), inc=None):
        t = act(s_.copy, hi, exact, after=[*after, dve.last])
        return dve(v.tensor_tensor, lo, exact, hi.bitcast(F32), ALU.subtract, after=[t], inc=inc)

    def norm_mod(hi, lo, segs):
        for t0, h0, nt, g, sft in segs:
            t = norm_sum(lambda k: XC[:, k, t0:t0 + nt], nt, 4)
            t = rstd(tmpf[:, 3, 0:nt], bank[4][:, 0:nt], t, D, eps_col, inc=bank_free[4])
            for k in range(KD):
                b = k % 2
                y = tmpf[:, b, 0:nt]
                dve(v.scalar_tensor_tensor, y, XC[:, k, t0:t0 + nt], g[:, k:k + 1], tmpf[:, 3, 0:nt],
                    ALU.mult, ALU.mult, after=[t, act.last, pe.last])
                dve(v.tensor_scalar, y, y, sft[:, k:k + 1], None, ALU.add)
                split_store(hi[:, k, h0:h0 + nt], lo[:, k, h0:h0 + nt], y)

    X1 = [(0, 0, T)]
    X0 = [(0, TC, T)]
    XB = [(0, TC, T), (4, 0, TC)]

    wf_in = [a[n].rearrange("l (k p) n -> l p k n", p=P) for n in ("w_ffn1_in", "w_ffn2_in")]
    wf_out = [a[n].rearrange("l (k p) n -> l p k n", p=P) for n in ("w_ffn1_out", "w_ffn2_out")]
    wmix_in = a["w_mix_in"].rearrange("l (k p) n -> l p k n", p=P)
    wmix_out = a["w_mix_out"].rearrange("l (k p) n -> l p k n", p=P)

    def c1(name):
        o, w = COLS1[name]
        return cols1[:, o:o + w]

    def c2(name):
        o, w = COLS2[name]
        return cols2[:, o:o + w]

    def evict_add(n, coef):
        def go(ps, t, free):
            xa = XC[:, ds(n, 1), TC:TT].rearrange("p a n -> p (a n)")
            dve(v.scalar_tensor_tensor, xa, ps[0], coef[:, ds(n, 1)], xa, ALU.mult, ALU.add, after=[t], inc=free)
        return go

    def ffn(l, which, ada_in, ada_out):
        w_in, w_out = wf_in[which][l], wf_out[which][l]
        coef = small[:, 8:16]
        pe.wait(dve.last)
        for c, (j0, nj) in enumerate([(0, 8), (8, 8), (16, 6)]):
            with prog.loop(f"ffn{which}_in{c}", nj // 2) as i:
                for q in range(2):
                    col = (i * 2 + (j0 + q)) * P

                    def ev_gate(ps, t, free, q=q):
                        act(s_.activation, tmpf[:, q, :], ps[0], ACT.Silu, after=[t], inc=free)

                    def ev_up(ps, t, free, q=q):
                        y = tmpf[:, q, :]
                        dve(v.tensor_tensor, y, y, ps[0], ALU.mult, after=[t, act.last])
                        hi = GH[:, ds(i * 2 + q, 1), 0:T].rearrange("p a n -> p (a n)")
                        lo = GL[:, ds(i * 2 + q, 1), 0:T].rearrange("p a n -> p (a n)")
                        split_store(hi, lo, y, inc=free)

                    job = ada_in(c, i * 2 + q) if which == 0 else ada_in(c, i if c == 1 else i * 2 + q, q)
                    unit(w_in[:, :, ds(col, P)], KD, X1, H1H, H1L, ev_gate, ada=job and ("begin", *job))
                    unit(w_in[:, :, ds(col + D_FF, P)], KD, X1, H1H, H1L, ev_up, ada=job and ("finish", *job))
            pe.wait(bank_free[1].now(), bank_free[3].now())
            with prog.loop(f"ffn{which}_out{c}", 2) as i:
                for q in range(4):
                    job = ada_out(c, i * 2 + q // 2)
                    unit(w_out[:, j0 + nj - KD:j0 + nj, ds((i * 4 + q) * P, P)], nj, X1, GH, GL,
                         evict_add(i * 4 + q, coef), ada=job and (("begin", "finish")[q % 2], *job))

    def stage_cols(g, i):
        sc, gt = mod1[:, (i + 1) * 8:(i + 2) * 8], mod1[:, (i + 2) * 8:(i + 3) * 8]
        dve(v.tensor_scalar, small[:, 0:8], sc, 1.0, None, ALU.add)
        dve(v.tensor_tensor, small[:, 0:8], small[:, 0:8], g, ALU.mult)
        half = 1.0 if i == 3 else 0.5
        dve(v.tensor_scalar, small[:, 8:16], gt, half, half, ALU.mult, ALU.add)
        return mod1[:, i * 8:(i + 1) * 8]

    PJ = region("PJ", G0, [P, NP1, T + 2])
    S_FREE = G0 + NP1 * (T + 2)
    HT, LT = KD * T, KD * TT + KD * T
    att_s = region("att_s", HT, [P, QH, 256])
    att_pt = region("att_pt", LT, [P, 2 * QH, P])
    kdup = region("kdup", S_FREE, [P, 2, P + T])
    vnat = region("vnat", S_FREE + 1280, [P, 5, P])
    att_y = region("att_y", S_FREE + 1920, [P, 2, T])
    kd_in = prog.counter("kd_in")

    def heads_rms(tile_ap, gain_col, b):
        act(s_.activation, tmpf[:, b, :], tile_ap, ACT.Square, after=[dve.last, pe.last])
        t = mm(bank[4 + b][:], blk, tmpf[:, b, :], True, True, after=[act.last, dve.last], done=True)
        t = rstd(tmpf[:, b, :], bank[4 + b][:], t, HD, eps_col)
        dve(v.scalar_tensor_tensor, tile_ap, tile_ap, gain_col, tmpf[:, b, :], ALU.mult, ALU.mult, after=[t])

    def attention():
        for i in range(5):
            heads_rms(PJ[:, i, 2:2 + T], c1("q_gain") if i < 4 else c1("k_gain"), i % 2)
        dve(v.memset, kdup[:, :, 0:P], 0.0)
        dve(v.memset, vnat[:, 0, :], 0.0)
        for h in range(2):
            for half in range(2):
                t_kd = prog.dma(act, kdup[64 * half:64 * half + 64, h, P:P + T],
                                PJ[64 * h:64 * h + 64, 4, 2:2 + T], kd_in, after=[dve.last])
        for b in range(4):
            prog.transpose(bank[6][:, b * P:(b + 1) * P], PJ[:, 5, 2 + b * P:2 + (b + 1) * P], ident,
                           after=[dve.last], done=b == 3)
        dve(v.tensor_copy, vnat[:, 1:5, :], bank[6][:].rearrange("p (b n) -> p b n", b=4), after=[pe.last])
        m, e1, den = small[:, 16:24], small[:, 24:32], small[:, 32:40]
        for b in range(4):
            pe.wait(t_kd, dve.last)

            def score(h, done):
                pr = 64 * (h % 2)
                mm(bank[h // 2][:, (h % 2) * 256:(h % 2) * 256 + 256],
                   PJ[pr:pr + 64, h // 2, 2 + b * P:2 + (b + 1) * P],
                   kdup[pr:pr + 64, h // 4, b * P:b * P + 256], True, True, done=done)
            prog.by_half(range(QH), score)
            msk = k_("attmask")[:, (0 if b == 0 else 256):(0 if b == 0 else 256) + 256]
            for h in range(QH):
                dve(v.scalar_tensor_tensor, att_s[:, h, :], bank[h // 2][:, (h % 2) * 256:(h % 2) * 256 + 256],
                    HD ** -0.5, msk, ALU.mult, ALU.add, after=[pe.last])
            dve(v.tensor_reduce, m, att_s[:], AX.X, ALU.max)
            dve(v.tensor_tensor, m, m, c1("sinks"), ALU.max)
            dve(v.tensor_tensor, att_s[:], att_s[:], m.unsqueeze(2).broadcast_to([P, QH, 256]), ALU.subtract)
            dve(v.tensor_tensor, e1, c1("sinks"), m, ALU.subtract)
            act(s_.activation, att_s[:], att_s[:], ACT.Exp, after=[dve.last])
            act(s_.activation, e1, e1, ACT.Exp)
            dve(v.tensor_reduce, den, att_s[:], AX.X, ALU.add, after=[act.last])
            dve(v.tensor_tensor, den, den, e1, ALU.add)
            dve(v.reciprocal, den, den)
            dve(v.tensor_tensor, att_s[:], att_s[:], den.unsqueeze(2).broadcast_to([P, QH, 256]), ALU.mult)
            t_p = dve.last
            for h in range(QH):
                for x in range(2):
                    i = 2 * h + x
                    prog.transpose(bank[4 + i // 4][:, (i % 4) * P:(i % 4 + 1) * P],
                                   att_s[:, h, x * P:(x + 1) * P], ident, after=[t_p], done=i % 4 == 3)
                    if i % 4 == 3:
                        q = i // 4
                        f = (dve, v.tensor_copy) if q % 2 else (act, s_.copy)
                        f[0](f[1], att_pt[:, 4 * q:4 * q + 4, :],
                             bank[4 + q][:].rearrange("p (b n) -> p b n", b=4), after=[pe.last])
            for h in range(QH):
                pr = 64 * (h % 2)
                for x in range(2):
                    mm(bank[h % 2][pr:pr + 64, (h // 2) * P:(h // 2 + 1) * P],
                       vnat[:, b + x, 64 * (h // 4):64 * (h // 4) + 64],
                       att_pt[:, 2 * h + x, :], x == 0, x == 1, after=[act.last, dve.last], done=h == QH - 1 and x == 1)
            y = att_y[:, b % 2, :]
            act(s_.copy, y[0:64, :], bank[0][0:64, :], after=[pe.last, dve.last])
            dve(v.tensor_copy, y[64:128, :], bank[1][64:128, :], after=[pe.last, act.last])
            y4 = y.rearrange("p (b n) -> p b n", b=4)
            split_store(H1H[:, 0:4, b * P:(b + 1) * P], H1L[:, 0:4, b * P:(b + 1) * P], y4)

    PR = [region("PRa", HT, [P, 4, T]), region("PRb", LT, [P, 4, T])]

    def conv1():
        w = c1("conv")
        for i in range(2):
            u = PJ[:, 18 + i, :]
            dve(v.tensor_tensor, u, u, PJ[:, 16 + i, :], ALU.mult)
            y = tmpf[:, 2, :]
            dve(v.tensor_scalar, y, u[:, 0:T], w[:, 3 * i:3 * i + 1], None, ALU.mult, after=[act.last])
            for k in (1, 2):
                dve(v.scalar_tensor_tensor, y, u[:, k:k + T], w[:, 3 * i + k:3 * i + k + 1], y, ALU.mult, ALU.add)
            dve(v.tensor_tensor, y, y, PJ[:, 14 + i, 2:2 + T], ALU.mult)
            split_store(H1H[:, 6 + i, :], H1L[:, 6 + i, :], y)

    names = ["gg", "lw", "aa", "kk", "cm", "ee", "bonus"]
    rw = {n: region("rw_" + n, G0 + 1024 * i, [P, 2, T]) for i, n in enumerate(names)}
    r1 = G0 + 7 * 1024
    rw_nat = region("rw_nat", r1, [P, 3, 2, P])
    rw_L = region("rw_L", r1 + 768, [P, 2, MH, P])
    rw_T = region("rw_T", r1 + 768 + 1024, [P, 2, MH, P])
    rw_Z = region("rw_Z", r1 + 768 + 2048, [P, 2, MH, P])
    rw_M = region("rw_M", r1 + 768 + 3072, [P, 3, MH, P])
    rw_W = region("rw_W", r1 + 768 + 3072 + 1536, [P, 256])
    rw_U = region("rw_U", r1 + 768 + 3072 + 1792, [P, 256])
    rw_X = region("rw_X", r1 + 768 + 3072 + 2048, [P, 2, HD])
    assert 768 + 3072 + 2048 + 128 + 7 * 1024 <= ADA0 - G0
    rw_Q = [region("rw_Qa", 4 * T, [P, 2, MH, P]), region("rw_Qb", KD * TT + 4 * T, [P, 2, MH, P])]

    def rwkv_shift():
        for i in range(8):
            src = PJ[:, 6 + i, :]
            dst = PR[i // 4][:, i % 4, :]
            dve(v.tensor_tensor, dst, src[:, 1:1 + T], src[:, 2:2 + T], ALU.subtract)
            dve(v.scalar_tensor_tensor, dst, dst, c1("mu")[:, i:i + 1], src[:, 2:2 + T], ALU.mult, ALU.add)

    def rwkv():
        tile = lambda i: PR[i // 4][:, i % 4, :]
        r, k, vv = PR[0][:, 0:2, :], PR[0][:, 2:4, :], PR[1][:, 0:2, :]
        wad, gd = tile(6), tile(7)
        gg, lw, aa, kk, cm, ee, bonus = (rw[n] for n in names)
        act(s_.activation, wad[0:64, :], wad[0:64, :], ACT.Tanh, after=[dve.last])
        t_in = act(s_.activation, gd, gd, ACT.Sigmoid)
        for i in range(2):
            mm(bank[i][:], lora[0:64, 0, i * P:(i + 1) * P], wad[0:64, :], True, True, after=[t_in, dve.last])
            mm(bank[2 + i][:], lora[64:128, 0, i * P:(i + 1) * P], wad[64:128, :], True, True)
            mm(bank[4 + i][:], lora[:, 1, i * P:(i + 1) * P], gd, True, True, done=True)
        for i in range(2):
            act(s_.activation, lw[:, i, :], bank[i][:], ACT.Sigmoid, bias=c1("w0")[:, i:i + 1], after=[pe.last])
            act(s_.activation, aa[:, i, :], bank[2 + i][:], ACT.Sigmoid, bias=c1("a0")[:, i:i + 1])
            act(s_.copy, gg[:, i, :], bank[4 + i][:])
        dve(v.tensor_scalar, lw[:], lw[:], -DECAY_SCALE, None, ALU.mult, after=[act.last])
        for i in range(2):
            dve(v.tensor_scalar, kk[:, i, :], k[:, i, :], c1("k_k")[:, i:i + 1], None, ALU.mult)
            act(s_.activation, ee[:, i, :], kk[:, i, :], ACT.Square, after=[dve.last])
            mm(bank[6 + i][:], blk, ee[:, i, :], True, True, after=[act.last], done=True)
        for i in range(2):
            act(s_.activation, ee[:, i, :], bank[6 + i][:], ACT.Sqrt, after=[pe.last])
        dve(v.tensor_scalar, ee[:], ee[:], 1e-12, None, ALU.max, after=[act.last])
        dve(v.reciprocal, ee[:], ee[:])
        dve(v.tensor_tensor, kk[:], kk[:], ee[:], ALU.mult)
        for i in range(2):
            dve(v.tensor_scalar, ee[:, i, :], aa[:, i, :], -1.0, c1("k_a")[:, i:i + 1], ALU.add, ALU.mult)
            dve(v.scalar_tensor_tensor, k[:, i, :], ee[:, i, :], 1.0, k[:, i, :], ALU.add, ALU.mult)
            dve(v.scalar_tensor_tensor, ee[:, i, :], r[:, i, :], c1("r_k")[:, i:i + 1], k[:, i, :],
                ALU.mult, ALU.mult)
            mm(bank[6 + i][:], blk, ee[:, i, :], True, True, after=[dve.last], done=True)
            dve(v.tensor_tensor, bonus[:, i, :], bank[6 + i][:], vv[:, i, :], ALU.mult, after=[pe.last])
        dve(v.tensor_tensor, aa[:], aa[:], kk[:], ALU.mult)
        for i in range(2):
            for c in range(4):
                dve(v.tensor_tensor_scan, cm[:, i, c * P:(c + 1) * P], ones[:], lw[:, i, c * P:(c + 1) * P], 0.0,
                    ALU.mult, ALU.add)
        mid, end = small[:, 16:24], small[:, 24:32]
        cm4 = cm[:].rearrange("p i (c n) -> p (i c) n", c=4)
        dve(v.tensor_copy, mid, cm4[:, :, 63])
        dve(v.tensor_tensor, cm4, cm4, mid.unsqueeze(2).broadcast_to([P, 8, P]), ALU.subtract)
        dve(v.tensor_copy, end, cm4[:, :, P - 1])
        m8, e8 = mid.rearrange("p (i c) -> p i c", i=2), end.rearrange("p (i c) -> p i c", i=2)
        dve(v.tensor_tensor, e8[:, :, 0:3], e8[:, :, 0:3], m8[:, :, 1:4], ALU.add)
        t_end = act(s_.activation, end, end, ACT.Exp, after=[dve.last])
        act(s_.activation, ee[:], cm[:], ACT.Exp)
        dve(v.tensor_tensor, r, r, ee[:], ALU.mult, after=[act.last])
        dve(v.tensor_tensor, lw[:], cm[:], lw[:], ALU.subtract)
        act(s_.activation, lw[:], lw[:], ACT.Exp, after=[dve.last])
        dve(v.tensor_tensor, kk[:], kk[:], lw[:], ALU.mult, after=[act.last])
        act(s_.activation, ee[:], cm[:], ACT.Exp, scale=-1.0, after=[dve.last])
        dve(v.tensor_tensor, aa[:], aa[:], ee[:], ALU.mult, after=[act.last])
        dve(v.tensor_tensor, k, k, ee[:], ALU.mult)

        def hs(x, h, c):
            return x[64 * (h % 2):64 * (h % 2) + 64, h // 2, c * P:(c + 1) * P]

        def hb(j):
            return bank[j][:].rearrange("p (h n) -> p h n", h=MH)

        def wide(m):
            return m.unsqueeze(1).broadcast_to([P, MH, P])

        for pair in range(2):
            Q = rw_Q[pair]
            t_in = dve.last
            for x in range(2):
                c = 2 * pair + x
                pe.wait(t_in)

                def gram(h, done):
                    mm(bank[x][:, h * P:(h + 1) * P], hs(kk, h, c), hs(aa, h, c), True, True)
                    mm(bank[2 + x][:, h * P:(h + 1) * P], hs(aa, h, c), hs(kk, h, c), True, True, done=done)
                prog.by_half(range(MH), gram)
            for x in range(2):
                dve(v.tensor_copy, rw_L[:, x], hb(x), after=[pe.last])
                dve(v.tensor_tensor, rw_T[:, x], rw_L[:, x], wide(k_("levels")[:, 0:P]), ALU.mult)
                dve(v.tensor_tensor, rw_T[:, x], rw_T[:, x], wide(ident), ALU.add)
                dve(v.tensor_tensor, Q[:, x], hb(2 + x), wide(k_("level0T")), ALU.mult)
                dve(v.tensor_tensor, Q[:, x], Q[:, x], wide(ident), ALU.add)
            for lv in range(1, RW_LEVELS):
                more = lv < RW_LEVELS - 1
                t_z = [None, None]
                for x in range(2):
                    m = tmpf[:, x, :].rearrange("p (h n) -> p h n", h=MH)
                    dve(v.tensor_tensor, m, rw_L[:, x], wide(k_("levels")[:, lv * P:(lv + 1) * P]), ALU.mult)
                    for h in range(MH):
                        t_z[x] = mm(bank[x][:, h * P:(h + 1) * P], m[:, h, :], Q[:, x, h, :], True, True,
                                    after=[dve.last], done=h == MH - 1)
                for x in range(2):
                    act(s_.copy, rw_Z[:, x], hb(x), after=[t_z[x]])
                    for h in range(MH):
                        if more:
                            mm(bank[4 + x][:, h * P:(h + 1) * P], rw_Z[:, x, h, :], rw_T[:, x, h, :], True, True,
                               after=[act.last])
                        t_z[x] = mm(bank[2 + x][:, h * P:(h + 1) * P], rw_T[:, x, h, :], rw_Z[:, x, h, :],
                                    True, True, after=[act.last], done=h == MH - 1)
                for x in range(2):
                    dve(v.tensor_tensor, Q[:, x], Q[:, x], hb(2 + x), ALU.add, after=[t_z[x]])
                    if more:
                        dve(v.tensor_tensor, rw_T[:, x], rw_T[:, x], hb(4 + x), ALU.add)
        for c in range(4):
            Q = rw_Q[c // 2][:, c % 2]
            t_in = [dve.last, act.last]
            for j, src in enumerate((aa, k, vv)):
                for i in range(2):
                    n = 2 * j + i
                    prog.transpose(bank[4 + n // 4][:, (n % 4) * P:(n % 4 + 1) * P],
                                   src[:, i, c * P:(c + 1) * P], ident, after=t_in, done=n == 5)
            act(s_.copy, rw_nat[:, 0:2], bank[4][:].rearrange("p (j i n) -> p j i n", j=2, i=2), after=[pe.last])
            t_nat = act(s_.copy, rw_nat[:, 2], bank[5][:, 0:256].rearrange("p (i n) -> p i n", i=2))
            nat = lambda j, h: rw_nat[:, j, h // 2, 64 * (h % 2):64 * (h % 2) + 64]
            for j, (lh, rh) in enumerate(((k, kk), (aa, r), (k, r))):
                prog.by_half(range(MH), lambda h, done: mm(bank[j][:, h * P:(h + 1) * P], hs(lh, h, c), hs(rh, h, c),
                                                           True, True, done=done))
                dve(v.tensor_tensor, rw_M[:, j], hb(j), wide(k_("upper" if j == 0 else "upper_eq")), ALU.mult,
                    after=[pe.last, t_nat])
            pe.wait(dve.last)

            def w_head(h, done):
                o = bank[3][:, 64 * h:64 * h + 64]
                pr = 64 * (h % 2)
                if c:
                    mm(o, hs(kk, h, c), rw_X[pr:pr + 64, h // 2, :], True, False)
                mm(o, rw_M[:, 0, h, :], nat(2, h), c == 0, True, done=done)
            prog.by_half(range(MH), w_head)
            dve(v.tensor_copy, rw_W[:], bank[3][:, 0:256], after=[pe.last])
            for h in range(MH):
                mm(bank[3][:, 256 + 64 * h:320 + 64 * h], Q[:, h, :], rw_W[:, 64 * h:64 * h + 64], True, True,
                   after=[dve.last], done=h == MH - 1)
            dve(v.tensor_scalar, rw_U[:], bank[3][:, 256:512], -1.0, None, ALU.mult, after=[pe.last])
            for h in range(MH):
                pr = 64 * (h % 2)
                o = bank[6 + h % 2][pr:pr + 64, (h // 2) * P:(h // 2 + 1) * P]
                if c:
                    mm(o, rw_X[pr:pr + 64, h // 2, :], hs(r, h, c), True, False)
                mm(o, nat(2, h), rw_M[:, 2, h, :], c == 0, False)
                mm(o, rw_U[:, 64 * h:64 * h + 64], rw_M[:, 1, h, :], False, True, after=[dve.last],
                   done=h == MH - 1)
            for x in range(2):
                pr = 64 * x
                act(s_.copy, lw[pr:pr + 64, :, c * P:(c + 1) * P],
                    bank[6 + x][pr:pr + 64, 0:256].rearrange("p (i n) -> p i n", i=2), after=[pe.last])
            if c < 3:
                for h in range(MH):
                    pr = 64 * (h % 2)
                    o = bank[4 + h % 2][pr:pr + 64, 64 * (h // 2):64 * (h // 2) + 64]
                    mm(o, nat(1, h), nat(2, h), True, False)
                    mm(o, nat(0, h), rw_U[:, 64 * h:64 * h + 64], False, True, done=h == MH - 1)
                for x in range(2):
                    pr = 64 * x
                    for i in range(2):
                        o, ps = rw_X[pr:pr + 64, i, :], bank[4 + x][pr:pr + 64, 64 * i:64 * i + 64]
                        e = e8[pr:pr + 64, i, c:c + 1]
                        if c:
                            dve(v.tensor_tensor, o, o, ps, ALU.add, after=[pe.last])
                            dve(v.tensor_scalar, o, o, e, None, ALU.mult)
                        else:
                            dve(v.tensor_scalar, o, ps, e, None, ALU.mult, after=[pe.last, t_end])
        for i in range(2):
            y, d2, rs = lw[:, i, :], tmpf[:, 0, :], tmpf[:, 1, :]
            mm(bank[0][:], blk, y, True, True, after=[act.last, dve.last], done=True)
            dve(v.scalar_tensor_tensor, y, bank[0][:], -1.0 / HD, y, ALU.mult, ALU.add, after=[pe.last])
            act(s_.activation, d2, y, ACT.Square, after=[dve.last])
            t = mm(bank[1][:], blk, d2, True, True, after=[act.last], done=True)
            rstd(rs, bank[1][:], t, HD, gn_eps_col)
            dve(v.tensor_tensor, y, y, rs, ALU.mult, after=[act.last])
            dve(v.tensor_scalar, y, y, c1("gn_w")[:, i:i + 1], c1("gn_b")[:, i:i + 1], ALU.mult, ALU.add)
            dve(v.tensor_tensor, y, y, bonus[:, i, :], ALU.add)
            dve(v.tensor_tensor, y, y, gg[:, i, :], ALU.mult)
            split_store(H1H[:, 4 + i, :], H1L[:, 4 + i, :], y)

    def mix1(l):
        pe.wait(dve.last)
        with prog.loop("mix_in", NP1 // 4) as i:
            for q in range(4):
                def ev(ps, t, free, q=q):
                    o = PJ[:, ds(i * 4 + q, 1), 2:2 + T].rearrange("p a n -> p (a n)")
                    act(s_.copy, o, ps[0], after=[t], inc=free)
                unit(wmix_in[l][:, :, ds((i * 4 + q) * P, P)], KD, X1, H1H, H1L, ev)
        prog.barrier()
        dve(v.memset, PJ[:, :, 0:2], 0.0)
        attention()
        prog.barrier()
        rwkv_shift()
        conv1()
        prog.barrier()
        rwkv()
        prog.barrier()
        pe.wait(dve.last)
        with prog.loop("mix_out", 2) as i:
            for q in range(4):
                unit(wmix_out[l][:, :, ds((i * 4 + q) * P, P)], KD, X1, H1H, H1L,
                     evict_add(i * 4 + q, small[:, 8:16]))

    with prog.loop("ada_first", 7) as u:
        for j in range(2):
            ada_begin(*ada1(0, u * 2 + j))
            ada_finish(*ada1(0, u * 2 + j))
    for _ in range(AHEAD):
        split_next()

    with prog.loop("layers1", DEPTH) as l:
        prog.dma(act, lora[:], a["lora"][l], in_lora)
        dve(v.tensor_copy, cols1[:], cols1_all[:, ds(l * NC1, NC1)])
        pe.wait(in_lora.now())
        shift = stage_cols(c1("g_ffn1"), 0)
        norm_mod(H1H, H1L, [(TC, 0, T, small[:, 0:8], shift)])
        ffn(l, 0, lambda c, j: ada1(l, j + (14 + 8 * c)), lambda c, j: ada2(l, j + 4 * c))
        prog.barrier()
        shift = stage_cols(c1("g_mix"), 3)
        norm_mod(H1H, H1L, [(TC, 0, T, small[:, 0:8], shift)])
        mix1(l)
        prog.barrier()
        shift = stage_cols(c1("g_ffn2"), 6)
        norm_mod(H1H, H1L, [(TC, 0, T, small[:, 0:8], shift)])

        def ada_in(c, j, q):
            if c == 0:
                return ada2(l, j + 12)
            if c == 1:
                return ada2(l, 20 + j) if q == 0 else ada1(1, j)
            return ada1(1, j + 4)
        ffn(l, 1, ada_in, lambda c, j: ada1(1, j + 10) if c == 0 else None)
        prog.barrier()

    QK = region("QK", G0, [P, 8, TT])
    SO = region("SO", G0 + 6144, [P, MH, TT])
    VN = region("VN", G0 + 9216, [P, TT // P, 512])
    CUW = TT + 4 * 15
    CU = region("CU", G0 + 12288, [P, 2, CUW])
    UT = region("UT", G0 + 12288 + 2 * CUW, [P, 2, TT])
    GR = region("GR", G0 + 15480, [P, TT])
    RAW = region("RAW", G0 + 16248, [P, 2, TT + 4])
    VF = region("VF", G0 + 16248, [P, TT // P, 4, P])
    DFT = [region("DFT_cos", 0, [P, 4, T]), region("DFT_sin", KD * TT, [P, 4, T])]
    DFTC = [region("DFTC_cos", 2048, [P, 2, TC]), region("DFTC_sin", KD * TT + 2048, [P, 2, TC])]
    CA = region("CA", 0, [P, 2, TT])
    GI = region("GI", G0 + 16248, [4, 4, TT])
    MC = region("MC", G0 + 12288, [4, 2, TT])
    GS = region("GS", G0 + 13824, [P, TT // P, 2, MH])
    WT = region("WT", G0 + 13944, [P, 2, T])
    HA = region("HA", G0 + 14968, [P, T])
    OUT = region("OUT", G0 + 12288, [P, KD, TT])
    POS = region("POS", G0, [P, KD, T])
    assert 16248 + 3072 <= RN - G0

    w_in2 = a["w_in_2"].rearrange("l (k p) n -> l p k n", p=P)
    w_out2 = a["w_out_2"].rearrange("l (k p) n -> l p k n", p=P)
    w_mlp1 = a["w_mlp1_2"].rearrange("l (k p) n -> l p k n", p=P)
    w_mlp2 = a["w_mlp2_2"].rearrange("l (k p) n -> l p k n", p=P)
    
    def m2(l, stream, row):
        o = l * 96 + stream * 48 + row * 8
        return mod2[:, o:o + 8]

    def tile_evict(dst):
        def go(ps, t, free):
            act(s_.copy, dst[:, TC:TT], ps[0], after=[t], inc=None if len(ps) > 1 else free)
            if len(ps) > 1:
                act(s_.copy, dst[:, 0:TC], ps[1], inc=free)
        return go

    def unit_nat(src, tile, nt, evict):
        s = load(src)
        split_next()
        pe.wait(split_done[s].now(), bank_free[s].now())
        for b in range(nt):
            ps = bank[s + 4 * (b // 4)][:, (b % 4) * P:(b % 4 + 1) * P]
            for k in range(KD):
                passes = [(HH, WH), (HL, WH), (HH, WL)]
                for pi, (x, w) in enumerate(passes):
                    mm(ps, x[:, k, b * P:(b + 1) * P], w[:, s, k, :], k == 0 and pi == 0, k == KD - 1 and pi == 2,
                       inc=unit_done[s] if (b, k, pi) == (nt - 1, KD - 1, 2) else None)
        t = pe.last
        act(s_.copy, VN[:, 0:4, tile * P:(tile + 1) * P], bank[s][:].rearrange("p (b n) -> p b n", b=4), after=[t])
        act(s_.copy, VN[:, 4:6, tile * P:(tile + 1) * P], bank[s + 4][:, 0:256].rearrange("p (b n) -> p b n", b=2),
            inc=bank_free[s])
        state["n"] += 1

    def project(l, ctx):
        both = XB if ctx else X0
        pe.wait(dve.last)

        def cols_of(at):
            return w_in2[l][:, :, ds(at, P)]

        dve(v.memset, CU[:], 0.0)
        for i in range(2):
            def ev_gate(ps, t, free):
                act(s_.activation, tmpf[:, 0, :], ps[0], ACT.Sigmoid, after=[t, dve.last],
                    inc=None if len(ps) > 1 else free)
                if len(ps) > 1:
                    act(s_.activation, tmpf[:, 1, 0:TC], ps[1], ACT.Sigmoid, inc=free)

            def ev_a(ps, t, free, i=i):
                dve(v.tensor_tensor, CU[:, i, TC + 45:TC + 45 + T], ps[0], tmpf[:, 0, :], ALU.mult,
                    after=[t, act.last], inc=None if len(ps) > 1 else free)
                if len(ps) > 1:
                    dve(v.tensor_tensor, CU[:, i, 15:15 + TC], ps[1], tmpf[:, 1, 0:TC], ALU.mult, inc=free)
            unit(cols_of(C_OFF + 256 + i * P), KD, both, HH, HL, ev_gate)
            unit(cols_of(C_OFF + i * P), KD, both, HH, HL, ev_a)
        for i in range(2):
            unit(cols_of(F_OFF + i * P), KD, both, HH, HL, tile_evict(UT[:, i, :]))
        unit(cols_of(G_OFF), KD, XB, HH, HL, tile_evict(GR[:, :]))
        for i in range(4):
            unit_nat(cols_of(1024 + i * P), i, TT // P, None)
        for q in range(4):
            def ev_o(ps, t, free, q=q):
                act(s_.activation, SO[:, q, TC:TT], ps[0], ACT.Sigmoid, after=[t],
                    inc=None if len(ps) > 1 else free)
                if len(ps) > 1:
                    act(s_.activation, SO[:, q, 0:TC], ps[1], ACT.Sigmoid, inc=free)
            unit(cols_of(1536 + q * P), KD, both, HH, HL, ev_o)
        dve(v.memset, RAW[:], 0.0)
        wq = cols2[:, COLS2["qk_conv"][0]:COLS2["qk_conv"][0] + 24]
        dve(v.tensor_scalar, wq[:, 12:24], wq[:, 12:24], 128.0 ** -0.5, None, ALU.mult)
        act.wait(dve.last)
        for half in range(2):
            segs = XB if half or ctx else X0
            for q in range(4):
                def ev(ps, t, free, q=q, half=half):
                    r = RAW[:, q % 2, :]
                    act(s_.copy, r[:, TC + 3:TC + 3 + T], ps[0], after=[t, dve.last],
                        inc=None if len(ps) > 1 else free)
                    if len(ps) > 1:
                        act(s_.copy, r[:, 1:1 + TC], ps[1], inc=free)
                    for r0, t0, nt in [(TC + 2, TC, T), (0, 0, TC)][:len(ps)]:
                        o = QK[:, 4 * half + q, t0:t0 + nt]
                        w = wq[:, 12 * half + 3 * q:12 * half + 3 * q + 3]
                        dve(v.tensor_scalar, o, r[:, r0:r0 + nt], w[:, 0:1], None, ALU.mult, after=[act.last])
                        for k in (1, 2):
                            dve(v.scalar_tensor_tensor, o, r[:, r0 + k:r0 + k + nt], w[:, k:k + 1], o,
                                ALU.mult, ALU.add)
                unit(cols_of(half * 512 + q * P), KD, segs, HH, HL, ev)

    def fourier(ctx):
        t_tab = None
        for j, n in enumerate(("cos", "sin")):
            t_tab = prog.dma(act, DFT[j][:], a["dft_" + n], in_table)
            t_tab = prog.dma(act, DFTC[j][:], a["dftc_" + n], in_table)
        blocks = range(0 if ctx else 2, TT // P)
        for b in blocks:
            for x, m in enumerate((k_("c64"), k_("s64"))):
                for i in range(2):
                    mm(bank[b % 4][:, (2 * x + i) * P:(2 * x + i + 1) * P], UT[:, i, b * P:(b + 1) * P], m,
                       True, True, after=[act.last] if b - blocks[0] >= 4 else (), done=x == 1 and i == 1)
            act(s_.copy, VF[:, b].rearrange("p x n -> p (x n)"), bank[b % 4][:], after=[pe.last])
        pe.wait(act.last, t_tab)
        for b0, nb, t0, nt, tab in [(2, 4, TC, T, DFT), (0, 2, 0, TC, DFTC)][:2 if ctx else 1]:
            for i in range(2):
                n = 0
                for x in range(2):
                    for b in range(nb):
                        mm(bank[4 + i + (0 if b0 else 2)][:, 0:nt], VF[:, b0 + b, 2 * x + i, :], tab[x][:, b, :], n == 0,
                           n == 2 * nb - 1, done=n == 2 * nb - 1)
                        n += 1
                y = tmpf[:, i, 0:nt]
                act(s_.copy, y, bank[4 + i + (0 if b0 else 2)][:, 0:nt], after=[pe.last, dve.last])
                split_store(HH[:, 4 + i, t0:t0 + nt], HL[:, 4 + i, t0:t0 + nt], y)

    def layer_norm_over_partitions(tiles, nt, n_mean, mat, bk, b):
        pe.wait(dve.last, act.last)
        for j, y in enumerate(tiles):
            mm(bank[bk][:, 0:nt], mat, y, j == 0, j == len(tiles) - 1, done=True)
        for y in tiles:
            dve(v.scalar_tensor_tensor, y, bank[bk][:, 0:nt], -1.0 / n_mean, y, ALU.mult, ALU.add, after=[pe.last])
        for j, y in enumerate(tiles):
            act(s_.activation, tmpf[:, b, 0:nt], y, ACT.Square, after=[dve.last, pe.last])
            mm(bank[bk + 1][:, 0:nt], mat, tmpf[:, b, 0:nt], j == 0, j == len(tiles) - 1, after=[act.last], done=True)
        rstd(tmpf[:, b, 0:nt], bank[bk + 1][:, 0:nt], pe.last, n_mean, eps_col)
        return tmpf[:, b, 0:nt]

    def conv31(l, ctx):
        w = c2("w_dw")
        parts = [(TC, T, TC + 30), (0, TC, 0)][:2 if ctx else 1]
        for i in range(2):
            for t0, nt, u0 in parts:
                dve(v.tensor_scalar, CA[:, i, t0:t0 + nt], CU[:, i, u0:u0 + nt], w[:, K2 * i:K2 * i + 1],
                    c2("b_dw")[:, i:i + 1], ALU.mult, ALU.add)
        with prog.loop(f"conv31_{l}", K2 - 1) as k:
            for i in range(2):
                for t0, nt, u0 in parts:
                    o = CA[:, i, t0:t0 + nt]
                    dve(v.scalar_tensor_tensor, o, CU[:, i, ds(k + (u0 + 1), nt)], w[:, ds(k + (K2 * i + 1), 1)], o,
                        ALU.mult, ALU.add)
        for t0, nt, _ in parts:
            tiles = [CA[:, i, t0:t0 + nt] for i in range(2)]
            rs = layer_norm_over_partitions(tiles, nt, 256, ones[:], 0, 0)
            for i, y in enumerate(tiles):
                dve(v.tensor_tensor, y, y, rs, ALU.mult, after=[act.last])
                dve(v.tensor_scalar, y, y, c2("g_ln")[:, i:i + 1], c2("b_ln")[:, i:i + 1], ALU.mult, ALU.add)
                act(s_.activation, y, y, ACT.Silu, after=[dve.last])
                split_store(HH[:, 6 + i, t0:t0 + nt], HL[:, 6 + i, t0:t0 + nt], y)

    def rows(x):
        return [x[0:4, :], x[4:8, :], x[8:12, :], x[12:16, :]]

    def gates():
        g16 = GR[0:16, :]
        dve(v.tensor_scalar, g16, g16, c2("b_gate")[0:16, :], None, ALU.add)
        for j in range(4):
            t = prog.dma(act, GI[:, j, :], GR[4 * j:4 * j + 4, :], gates_in, after=[dve.last])
        for d in range(2):
            f, m = GI[:, 2 * d + 1, :], MC[:, d, :]
            act(s_.activation, m, f, ACT.Abs, after=[t])
            act(s_.activation, m, m, ACT.Exp, scale=-1.0)
            act(s_.activation, m, m, ACT.Ln, bias=ones[0:4, 0:1])
            dve(v.scalar_tensor_tensor, f, f, 0.0, m, ALU.min, ALU.subtract, after=[act.last])
            g = GI[:, 2 * d, :]
            one = ones[0:4, 0:1].broadcast_to([4, TT])

            def scan(out, inp, op):
                if d == 0:
                    dve(v.tensor_tensor_scan, out, one, inp, 0.0, ALU.mult, op)
                else:
                    dve(v.tensor_tensor_scan, out[:, 0:TC][:, ::-1], one[:, 0:TC], inp[:, 0:TC][:, ::-1], 0.0,
                        ALU.mult, op)
                    dve(v.tensor_tensor_scan, out[:, TC:TT][:, ::-1], one[:, 0:T], inp[:, TC:TT][:, ::-1],
                        out[:, 0:1], ALU.mult, op)
            scan(m, f, ALU.add)
            dve(v.tensor_copy, f, m)
            dve(v.tensor_tensor, g, g, f, ALU.subtract)
            scan(m, g, ALU.max)
            dve(v.tensor_tensor, f, f, m, ALU.add)
        for b in range(TT // P):
            for d in range(2):
                at = (2 * b + d) * MH
                prog.transpose(bank[6][:, at:at + MH], GI[:, 2 * d, b * P:(b + 1) * P], ident[0:4, 0:4],
                               after=[dve.last], done=True)
        dve(v.tensor_copy, GS[:].rearrange("p b d h -> p (b d h)"), bank[6][:, 0:TT // P * 2 * MH], after=[pe.last])

    def mlstm_query(h, q0, nt, sources):
        sel = k_("sel")[0:4, h * P:(h + 1) * P]
        bc = [tmpf[:, 0, 0:nt], tmpf[:, 1, 0:nt]]
        for d in range(2):
            mm(bank[4 + d][:, 0:nt], sel, MC[:, d, q0:q0 + nt], True, True, after=[dve.last, act.last], done=True)
        for d in range(2):
            act(s_.copy, bc[d], bank[4 + d][:, 0:nt], after=[pe.last, dve.last])
        n = 0
        for ji, (j, rel) in enumerate(sources):
            sb = bank[4 + ji % 2]
            mm(sb[:, 0:nt], QK[:, 4 + h, j * P:(j + 1) * P], QK[:, h, q0:q0 + nt], True, True,
               after=[dve.last, act.last], done=True)
            t_s = pe.last
            first, last = ji == 0, ji == len(sources) - 1
            for d in range(2):
                lo, hi_ = (0, nt) if rel is None else ((rel * P, nt) if d == 0 else (0, (rel + 1) * P))
                w = WT[:, d, lo:hi_]
                dve(v.tensor_scalar, w, bc[d][:, lo:hi_], GS[:, j, d, h:h + 1], 0.0, ALU.add, ALU.min,
                    after=[act.last, pe.last])
                act(s_.activation, w, w, ACT.Exp, after=[dve.last])
                dve(v.tensor_tensor, w, w, sb[:, lo:hi_], ALU.mult, after=[act.last, t_s])
                if rel is not None:
                    wd = WT[:, d, rel * P:(rel + 1) * P]
                    dve(v.tensor_tensor, wd, wd, k_("upper_eq" if d == 0 else "lower_eq"), ALU.mult)
                if first and hi_ < nt:
                    dve(v.memset, WT[:, d, hi_:nt], 0.0)
                    hi_ = nt
                w = WT[:, d, lo:hi_]
                mm(bank[d][:, lo:hi_], VN[:, j, h * P:(h + 1) * P], w, first, last, after=[dve.last])
                mm(bank[2 + d][:, lo:hi_], ones[:], w, first, last, done=True)
        y = HA[:, 0:nt]
        for d in range(2):
            mm(bank[4 + d][:, 0:nt], sel, GI[:, 2 * d + 1, q0:q0 + nt], True, True, after=[dve.last], done=True)
            fl = tmpf[:, 2 + d, 0:nt]
            act(s_.activation, fl, bank[4 + d][:, 0:nt], ACT.Exp, after=[pe.last, dve.last])
            w = WT[:, d, 0:nt]
            act(s_.activation, w, bank[2 + d][:, 0:nt], ACT.Abs)
            dve(v.tensor_tensor, w, w, fl, ALU.max, after=[act.last])
            dve(v.reciprocal, w, w)
            if d == 0:
                dve(v.tensor_tensor, y, w, bank[d][:, 0:nt], ALU.mult)
            else:
                dve(v.tensor_tensor, w, w, bank[d][:, 0:nt], ALU.mult)
                dve(v.tensor_tensor, y, y, w, ALU.add)
        rs = layer_norm_over_partitions([y], nt, P, ones[:], 6, 0)
        dve(v.tensor_tensor, y, y, rs, ALU.mult, after=[act.last])
        dve(v.scalar_tensor_tensor, y, y, c2("g_mlstm")[:, h:h + 1], SO[:, h, q0:q0 + nt], ALU.mult, ALU.mult)
        split_store(HH[:, h, q0:q0 + nt], HL[:, h, q0:q0 + nt], y)

    def post_norm_add(l, segs, g, row):
        for stream, t0, nt in segs:
            gg = small[:, 16:24]
            dve(v.tensor_tensor, gg, g, m2(l, stream, row), ALU.mult)
            t = norm_sum(lambda k: OUT[:, k, t0:t0 + nt], nt, 4)
            t = rstd(tmpf[:, 3, 0:nt], bank[4][:, 0:nt], t, D, eps_col, inc=bank_free[4])
            for k in range(KD):
                o = OUT[:, k, t0:t0 + nt]
                dve(v.scalar_tensor_tensor, o, o, gg[:, k:k + 1], tmpf[:, 3, 0:nt], ALU.mult, ALU.mult, after=[t])
                dve(v.tensor_tensor, XC[:, k, t0:t0 + nt], XC[:, k, t0:t0 + nt], o, ALU.add)

    def mod_norm(l, segs, g, row):
        items = []
        for stream, t0, nt in segs:
            gs = small[:, 8 * stream:8 * stream + 8]
            dve(v.tensor_scalar, gs, m2(l, stream, row + 1), 1.0, None, ALU.add)
            dve(v.tensor_tensor, gs, gs, g, ALU.mult)
            items.append((t0, t0, nt, gs, m2(l, stream, row)))
        norm_mod(HH, HL, items)

    def out_evict(n, first):
        def go(ps, t, free):
            for j, (t0, nt) in enumerate([(TC, T), (0, TC)][:len(ps)]):
                inc = free if j == len(ps) - 1 else None
                o = OUT[:, ds(n, 1), t0:t0 + nt].rearrange("p a n -> p (a n)")
                if first:
                    dve(v.tensor_copy, o, ps[j], after=[t], inc=inc)
                else:
                    dve(v.tensor_tensor, o, o, ps[j], ALU.add, after=[t], inc=inc)
        return go

    def mlp(l, ctx, final):
        both = XB if ctx else X0
        for c in range(4):
            pe.wait(dve.last)
            with prog.loop(f"mlp{l}_in{c}", 2) as i:
                for q in range(4):
                    def ev(ps, t, free, q=q):
                        for j, (t0, nt) in enumerate([(TC, T), (0, TC)][:len(ps)]):
                            y = tmpf[:, q % 2 + 2 * j, 0:nt]
                            hi, lo = (g[:, ds(i * 4 + q, 1), t0:t0 + nt].rearrange("p a n -> p (a n)")
                                      for g in (GH, GL))
                            act(s_.activation, y, ps[j], ACT.Relu, after=[t])
                            dve(v.tensor_tensor, y, y, ps[j], ALU.mult, after=[act.last])
                            split_store(hi, lo, y, inc=free if j == len(ps) - 1 else None)
                    unit(w_mlp1[l][:, :, ds((i * 4 + (q + 8 * c)) * P, P)], KD, both, HH, HL, ev)
            pe.wait(*[b.now() for b in bank_free[0:4]])
            with prog.loop(f"mlp{l}_out{c}", 2) as i:
                for q in range(4):
                    unit(w_mlp2[l][:, 8 * c:8 * c + 8, ds((i * 4 + q) * P, P)], KD, both, GH, GL,
                         out_evict(i * 4 + q, c == 0))
        if final:
            for _ in range(AHEAD):
                load(a["const"][:, 0:KD * P].rearrange("p (k n) -> p k n", k=KD))
                state["n"] += 1

    def block2(l):
        ctx = l < DEPTH - 1
        segs = [(0, TC, T), (1, 0, TC)]
        kept = segs if ctx else segs[:1]
        dve(v.tensor_copy, cols2[:], cols2_all[:, l * NC2:(l + 1) * NC2])
        mod_norm(l, segs, c2("g_pre_mix"), 0)
        prog.barrier()
        project(l, ctx)
        prog.barrier()
        fourier(ctx)
        prog.barrier()
        conv31(l, ctx)
        prog.barrier()
        gates()
        prog.barrier()
        for h in range(MH):
            mlstm_query(h, TC, T, [(0, None), (1, None)] + [(2 + r, r) for r in range(4)])
            if ctx:
                mlstm_query(h, 0, TC, [(0, 0), (1, 1)])
        prog.barrier()
        pe.wait(dve.last)
        with prog.loop(f"out{l}", 2) as i:
            for q in range(4):
                unit(w_out2[l][:, :, ds((i * 4 + q) * P, P)], KD, XB if ctx else X0, HH, HL,
                     out_evict(i * 4 + q, True))
        prog.barrier()
        post_norm_add(l, kept, c2("g_post_mix"), 2)
        mod_norm(l, kept, c2("g_pre_mlp"), 3)
        prog.barrier()
        mlp(l, ctx, not ctx)
        prog.barrier()
        post_norm_add(l, kept, c2("g_post_mlp"), 5)
        prog.barrier()

    t_pos = prog.dma(act, POS[:], a["posT"], in_table)
    dve(v.tensor_tensor, XC[:, :, TC:TT], XC[:, :, TC:TT], POS[:], ALU.add, after=[t_pos])
    prog.barrier()
    for l in range(DEPTH):
        block2(l)
    prog.dma(sp, a["outT"], XC[:, :, TC:TT], out_done, after=[dve.last])
    sp.wait(out_done.now())
    return prog.recorded


def _columns(parts, table, total):
    out = np.zeros((DEPTH, P, total), np.float32)
    for name, (o, w) in table.items():
        out[:, :, o:o + w] = parts[name]
    return np.ascontiguousarray(out.transpose(1, 0, 2).reshape(P, DEPTH * total))


def _vec(x):
    x = np.asarray(x).reshape(DEPTH, -1, P)
    return x.transpose(0, 2, 1)


def _taps(x):
    x = np.asarray(x)
    k = x.shape[1]
    return x.reshape(DEPTH, k, -1, P).transpose(0, 3, 2, 1).reshape(DEPTH, P, -1)


def _shape_constants():
    p, f = np.arange(P)[:, None], np.arange(P)[None, :]
    out = np.zeros((P, NCONST), np.float32)

    def put(name, x):
        o, w = CONST[name]
        out[:x.shape[0], o:o + w] = x

    put("ident", (p == f).astype(np.float32))
    put("blk", (p // HD == f // HD).astype(np.float32))
    q, k = np.arange(P)[:, None], np.arange(2 * P)[None, :] - P
    open_ = (q - k >= 0) & (q - k < P)
    put("attmask", np.concatenate([np.where(open_ & (k >= 0), 0, -1e30), np.where(open_, 0, -1e30)], 1))
    levels = []
    for j in range(RW_LEVELS):
        w = 1 << j
        same = (p // (2 * w)) == (f // (2 * w))
        levels.append(-(same & (p // w % 2 == 1) & (f // w % 2 == 0)).astype(np.float32))
    put("levels", np.concatenate(levels, 1))
    put("level0T", levels[0].T)
    put("upper", (p < f).astype(np.float32))
    put("upper_eq", (p <= f).astype(np.float32))
    put("lower_eq", (p >= f).astype(np.float32))
    ang = 2 * np.pi * ((p % HD) * (f % HD) % HD) / HD
    same = p // HD == f // HD
    put("c64", np.where(same, np.cos(ang), 0))
    put("s64", np.where(same, -np.sin(ang), 0))
    sel = np.zeros((4, 4, P), np.float32)
    for h in range(4):
        sel[h, h] = -1
    put("sel", sel.reshape(4, -1))
    return out


def _dft(n):
    i = np.arange(n)
    ang = 2 * np.pi * (i[:, None] * i[None, :] % n) / n
    scale = 1 / np.sqrt(n * 64)
    lay = lambda x: np.ascontiguousarray((x * scale).astype(np.float32).reshape(n // P, P, n).transpose(1, 0, 2))
    return lay(np.cos(ang)), lay(np.sin(ang))


def _positions():
    quarter = D // 4
    f32 = np.float32
    freq = np.exp(f32(-np.log(10000.0)) * np.arange(quarter, dtype=f32) / f32(quarter))
    r = np.repeat(np.arange(T // 64, dtype=f32), 64)[:, None] * freq
    c = np.tile(np.arange(64, dtype=f32), T // 64)[:, None] * freq
    pos = np.concatenate([np.sin(r), np.cos(r), np.sin(c), np.cos(c)], -1).astype(f32)
    return _transposed(pos)


def _transposed(x):
    return np.ascontiguousarray(x.T.reshape(KD, P, -1).transpose(1, 0, 2))


def host_arrays(i):
    i = {k: np.asarray(x) for k, x in i.items()}
    const = _shape_constants()
    o, w = CONST["cc"]
    for j, n in enumerate(("c", "c_2", "c_ctx_2")):
        const[:, o + 8 * j:o + 8 * j + 8] = i[n].reshape(KD, P).T
    twice = lambda x: np.concatenate([x, x], 1)[:, :, None]
    cols1 = _columns({
        "b_ada": _vec(i["b_ada"]), "g_ffn1": _vec(i["g_ffn1"]), "g_mix": _vec(i["g_mix"]),
        "g_ffn2": _vec(i["g_ffn2"]), "q_gain": twice(i["att_q_gain"]), "k_gain": twice(i["att_k_gain"]),
        "sinks": np.broadcast_to(i["att_sinks"][:, None, :], (DEPTH, P, QH)), "mu": _vec(i["rwkv_mu"]),
        "w0": _vec(i["rwkv_w0"]), "a0": _vec(i["rwkv_a0"]), "k_k": _vec(i["rwkv_k_k"]), "k_a": _vec(i["rwkv_k_a"]),
        "r_k": _vec(i["rwkv_r_k"]), "gn_w": _vec(i["rwkv_gn_w"]), "gn_b": _vec(i["rwkv_gn_b"]),
        "conv": _taps(i["conv_w"])}, COLS1, NC1)
    bg = np.zeros((DEPTH, P, 1), np.float32)
    bg[:, :16, 0] = i["b_gate_2"].reshape(DEPTH, 16)
    cols2 = _columns({
        "b_ada": _vec(i["b_ada_2"]), "g_pre_mix": _vec(i["g_pre_mix_2"]), "g_post_mix": _vec(i["g_post_mix_2"]),
        "g_pre_mlp": _vec(i["g_pre_mlp_2"]), "g_post_mlp": _vec(i["g_post_mlp_2"]),
        "qk_conv": _taps(i["w_qk_conv_2"]), "g_mlstm": _vec(i["g_mlstm_norm_2"]), "w_dw": _taps(i["w_dw_2"]),
        "b_dw": _vec(i["b_dw_2"]), "g_ln": _vec(i["g_conv_ln_2"]), "b_ln": _vec(i["b_conv_ln_2"]),
        "b_gate": bg}, COLS2, NC2)
    lora = np.zeros((DEPTH, P, 2, 256), np.float32)
    lora[:, 0:64, 0] = i["rwkv_w_w2"]
    lora[:, 64:128, 0] = i["rwkv_a_w2"]
    lora[:, :, 1] = i["rwkv_g_w2"]
    dc, dsn = _dft(T)
    cc, cs = _dft(TC)
    arrays = {"const": const, "cols1": cols1, "cols2": cols2, "lora": lora, "xT": _transposed(i["x"][0]),
              "ctxT": _transposed(i["ctx_2"][0]), "posT": _positions(), "dft_cos": dc, "dft_sin": dsn,
              "dftc_cos": cc, "dftc_sin": cs}
    for n in ("w_ada", "w_ffn1_in", "w_ffn1_out", "w_ffn2_in", "w_ffn2_out", "w_mix_in", "w_mix_out", "w_ada_2",
              "w_in_2", "w_out_2", "w_mlp1_2", "w_mlp2_2"):
        arrays[n] = np.ascontiguousarray(i[n])
    return arrays


def kernel(**inputs):
    import concourse.bacc as _bacc
    from concourse.bass_utils import run_bass_kernel_spmd as _run
    arrays = host_arrays(inputs)
    per_loop = {}
    for _ in range(2):
        nc = _bacc.Bacc("TRN2", target_bir_lowering=False, num_devices=1)
        a = {n: nc.dram_tensor("in_" + n, x.shape, F32, kind="ExternalInput").ap() for n, x in arrays.items()}
        a["outT"] = nc.dram_tensor("outT", (P, KD, T), F32, kind="ExternalOutput").ap()
        per_loop = build(nc, a, per_loop)
    r = _run(nc, [{"in_" + n: x for n, x in arrays.items()}], core_ids=[0])
    out = r.results[0]["outT"]
    return np.ascontiguousarray(out.transpose(1, 0, 2).reshape(D, T).T)[None]
```

```python
from contextlib import ExitStack, contextmanager

import numpy as np
import concourse.bass as bass
from concourse import mybir

F32 = mybir.dt.float32
F32R = mybir.dt.float32r
ALU = mybir.AluOpType
ACT = mybir.ActivationFunctionType
AX = mybir.AxisListType
ds = bass.ds

P = 128
D = 1024
T = 512
TC = 256
TT = TC + T
KD = D // P
DEPTH = 2
EPS = 1e-6
D_FF = 2816
FT = D_FF // P
PROJ1 = 2560
NP1 = PROJ1 // P
HD = 64
QH = 8
GN_EPS = 64e-5
DECAY_SCALE = float(np.exp(-0.5))
D_FF2 = 4096
MH = 4
G_OFF = 2048
F_OFF = 2064
C_OFF = F_OFF + 256
K2 = 31
BASE = 16
SLOTS = 4
AHEAD = 2
DEBUG = False

COLS1 = {}
COLS2 = {}


def _layout(table, items):
    at = 0
    for name, n in items:
        table[name] = (at, n)
        at += n
    return at


NC1 = _layout(COLS1, [("b_ada", 72), ("g_ffn1", 8), ("g_mix", 8), ("g_ffn2", 8), ("q_gain", 1), ("k_gain", 1),
                      ("sinks", 8), ("mu", 8), ("w0", 2), ("a0", 2), ("k_k", 2), ("k_a", 2), ("r_k", 2),
                      ("gn_w", 2), ("gn_b", 2), ("conv", 6)])
NC2 = _layout(COLS2, [("b_ada", 48), ("g_pre_mix", 8), ("g_post_mix", 8), ("g_pre_mlp", 8), ("g_post_mlp", 8),
                      ("qk_conv", 24), ("g_mlstm", 4), ("w_dw", 62), ("b_dw", 2), ("g_ln", 2), ("b_ln", 2),
                      ("b_gate", 1)])
CONST = {}
NCONST = _layout(CONST, [("ident", 128), ("blk", 128), ("attmask", 512), ("levels", 7 * 128), ("level0T", 128),
                         ("upper", 128), ("upper_eq", 128), ("lower_eq", 128), ("c64", 128), ("s64", 128),
                         ("sel", 512), ("cc", 24)])
RW_LEVELS = 7


class Counter:

    def __init__(self, sem, name, base):
        self.sem, self.name, self.const, self.terms = sem, name, base, []

    def now(self, more=0):
        return (self, self.const + more, tuple(self.terms))


class Queue:

    def __init__(self, eng, progress, chained):
        self.eng, self.progress, self.chained = eng, progress, chained
        self.last = None
        self.latest = None
        self.seen = {}

    def wait(self, *tokens):
        for t in tokens:
            if t is None:
                continue
            counter, const, terms = t
            key = (counter.name, tuple(id(i) for i, _ in terms))
            if self.seen.get(key, 0) >= const:
                continue
            self.seen[key] = const
            value = const
            for i, k in terms:
                if k:
                    value = i * k + value
            self.eng.wait_ge(counter.sem, value)

    def __call__(self, fn, *args, after=(), inc=None, **kw):
        self.wait(*after)
        if self.chained:
            self.wait(self.last)
        counter = inc or self.progress
        fn(*args, **kw).then_inc(counter.sem, 1)
        counter.const += 1
        self.last = self.latest = counter.now()
        return self.last


class Program:
    def __init__(self, nc, per_loop):
        self.nc = nc
        self.per_loop = per_loop
        self.recorded = {}
        self.counters = []
        self.pe = Queue(nc.tensor, self.counter("pe"), False)
        self.act = Queue(nc.scalar, self.counter("act"), True)
        self.dve = Queue(nc.vector, self.counter("dve"), True)
        self.pool = Queue(nc.gpsimd, self.counter("pool"), True)
        self.sp = Queue(nc.sync, self.counter("sp"), False)
        self.queues = [self.pe, self.act, self.dve, self.pool, self.sp]
        self.entered = nc.alloc_semaphore("s_entered")

    def counter(self, name, base=BASE):
        c = Counter(self.nc.alloc_semaphore("s_" + name), name, base)
        if base:
            self.nc.sync.sem_inc(c.sem, base)
        self.counters.append(c)
        return c

    def mm(self, out, lhsT, rhs, start, stop, after=(), inc=None, done=False):
        self.pe.wait(*after)
        ins = self.nc.tensor.matmul(out, lhsT, rhs, start=start, stop=stop)
        return self._pe_done(ins, inc, done)

    def transpose(self, out, in_, ident, after=(), inc=None, done=False):
        self.pe.wait(*after)
        return self._pe_done(self.nc.tensor.transpose(out, in_, ident), inc, done)

    def _pe_done(self, ins, inc, done):
        if inc is None and not done:
            return None
        counter = inc or self.pe.progress
        ins.then_inc(counter.sem, 1)
        counter.const += 1
        self.pe.last = self.pe.latest = counter.now()
        return self.pe.last

    def dma(self, queue, out, in_, counter, after=()):
        queue.wait(*after)
        queue.eng.dma_start(out, in_).then_inc(counter.sem, 16)
        counter.const += 16
        return counter.now()

    def by_half(self, heads, one_head):
        for half in range(2):
            mine = [h for h in heads if h % 2 == half]
            for h in mine:
                one_head(h, h == mine[-1])
            self.pe.wait(self.pe.last)
        return self.pe.last

    def interleave(self, *chains):
        last = {c: {q: q.last for q in self.queues} for c in chains}
        live = list(chains)
        while live:
            for c in list(live):
                for q in self.queues:
                    q.last = last[c][q]
                if next(c, self) is self:
                    live.remove(c)
                last[c] = {q: q.last for q in self.queues}
        for q in self.queues:
            q.last = q.latest

    def barrier(self):
        work = [self.pe, self.act, self.dve, self.pool]
        for q in work:
            for other in work:
                if other is not q:
                    q.wait(other.last)

    @contextmanager
    def loop(self, name, n):
        for q in self.queues:
            if q.chained:
                q.wait(q.last)
            q.seen = {}
        outside = {q: q.last for q in self.queues}
        for q in self.queues:
            q.last = None
        for q in (self.pe, self.dve, self.pool):
            q.eng.sem_inc(self.entered, 1)
        start = {c: c.const for c in self.counters}
        per = self.per_loop.get(name, {})
        with self.nc.Fori(0, n) as i:
            for c in self.counters:
                c.terms.append((i, per.get(c.name, 0)))
            yield i
            for q in self.queues:
                if q.chained:
                    q.wait(q.last)
            for c in self.counters:
                c.terms.pop()
        self.recorded[name] = {c.name: c.const - start[c] for c in self.counters}
        for c in self.counters:
            c.const = start[c] + n * (c.const - start[c])
        for q in self.queues:
            q.seen = {}
            q.last = q.latest = q.last[0].now() if q.last else outside[q]


def build(nc, a, per_loop):
    prog = Program(nc, per_loop)
    pe, act, dve, pool, sp = prog.pe, prog.act, prog.dve, prog.pool, prog.sp
    mm = prog.mm
    v, s_, g_ = nc.vector, nc.scalar, nc.gpsimd

    top = [(nc.sbuf_base + 63) // 64 * 64]

    def fixed(name, shape, dt=F32):
        off = top[0]
        top[0] += (int(np.prod(shape[1:])) * 4 + 31) // 32 * 32
        return nc.alloc_sbuf_tensor_at(name, list(shape), dt, offset=off)

    const = fixed("const", [P, NCONST])
    ones = fixed("ones", [P, P])
    cols1_all = fixed("cols1_all", [P, DEPTH * NC1])
    cols2_all = fixed("cols2_all", [P, DEPTH * NC2])
    cols1 = fixed("cols1", [P, NC1])
    cols2 = fixed("cols2", [P, NC2])
    mod1 = fixed("mod1", [P, 72])
    mod2 = fixed("mod2", [P, DEPTH * 2 * 48])
    small = fixed("small", [P, 48])
    csil = fixed("csil", [P, 3, 8])
    csig = fixed("csig", [P, 3, 8])
    lora = fixed("lora", [P, 2, 256])
    XC = fixed("XC", [P, KD, TT])
    stage_at = top[0]
    stage = fixed("stage", [P, SLOTS, 8, P])
    WL = nc.alloc_sbuf_tensor_at("WL", [P, SLOTS, 8, P], F32R, offset=stage_at)
    WH = fixed("WH", [P, SLOTS, 8, P], F32R)
    tmpf = fixed("tmpf", [P, 4, T])
    R0 = top[0]
    RN = (nc.sbuf_usable_end - R0) // 32 * 8
    print("RN", RN, "free after G0", RN - 2 * KD * TT) if DEBUG else None
    used = set()

    def region(name, off, shape, dt=F32):
        assert off + int(np.prod(shape[1:])) <= RN, (name, off, shape, RN)
        assert name not in used
        used.add(name)
        return nc.alloc_sbuf_tensor_at(name, list(shape), dt, offset=R0 + 4 * off)

    HH = region("HH", 0, [P, KD, TT], F32R)
    HL = region("HL", KD * TT, [P, KD, TT], F32R)
    G0 = 2 * KD * TT
    H1H = region("H1H", 0, [P, KD, T], F32R)
    H1L = region("H1L", KD * TT, [P, KD, T], F32R)
    GH = region("GH", G0, [P, 8, TT], F32R)
    GL = region("GL", G0 + 8 * TT, [P, 8, TT], F32R)
    ADA0 = RN - 2 * 2048 - 512
    ada_w = region("ada_w", ADA0, [P, 2, 8, 256])
    ada_acc = region("ada_acc", ADA0 + 4096, [P, 2, 256])
    bank = [nc.alloc_psum_tensor(f"bank{j}", [P, 512], F32) for j in range(8)]

    def k_(name, n=None):
        o, w = CONST[name]
        return const[:, o:o + (n or w)]

    ident, blk = k_("ident"), k_("blk")

    stage_full = [prog.counter(f"stage_full{i}") for i in range(SLOTS)]
    split_done = [prog.counter(f"split_done{i}") for i in range(SLOTS)]
    unit_done = [prog.counter(f"unit_done{i}") for i in range(SLOTS)]
    bank_free = [prog.counter(f"bank_free{i}") for i in range(8)]
    ada_full = [prog.counter(f"ada_full{i}", 0) for i in range(2)]
    ada_ready = [prog.counter(f"ada_ready{i}") for i in range(2)]
    in_lora = prog.counter("in_lora")
    in_table = prog.counter("in_table")
    gates_in = prog.counter("gates_in")
    out_done = prog.counter("out_done")
    in_misc = prog.counter("in_misc")

    prog.dma(act, const[:], a["const"], in_misc)
    prog.dma(act, cols1_all[:], a["cols1"], in_misc)
    prog.dma(act, cols2_all[:], a["cols2"], in_misc)
    t_const = prog.dma(act, XC[:, :, TC:TT], a["xT"], in_misc)
    t_const = prog.dma(act, XC[:, :, 0:TC], a["ctxT"], in_misc)
    dve(v.memset, ones[:], 1.0)
    one_row = ones[:, 0:1]
    eps_col, gn_eps_col = small[:, 46:47], small[:, 47:48]
    dve(v.memset, eps_col, EPS)
    dve(v.memset, gn_eps_col, GN_EPS)

    cc = k_("cc").rearrange("p (a k) -> p a k", a=3)
    act(s_.activation, csig[:], cc, ACT.Sigmoid, after=[t_const])
    t_csil = dve(v.tensor_tensor, csil[:], cc, csig[:], ALU.mult, after=[act.last, t_const])

    state = {"n": 0, "split": 0, "ada": 0}

    def split_next():
        st = state["split"] % SLOTS
        state["split"] += 1
        t = act(s_.copy, WH[:, st], stage[:, st], after=[stage_full[st].now(16)])
        dve(v.tensor_tensor, WL[:, st], stage[:, st], WH[:, st].bitcast(F32), ALU.subtract,
            after=[t, stage_full[st].now(16)], inc=split_done[st])

    def load(src):
        st = state["n"] % SLOTS
        prog.dma(sp, stage[:, st], src, stage_full[st], after=[unit_done[st].now()])
        return st

    def unit(src, kt, segs, hi, lo, evict, ada=None):
        s = load(src)
        split_next()
        if ada and ada[0] == "begin":
            ada_begin(*ada[1:])
        outs = []
        pe.wait(split_done[s].now(), bank_free[s].now())
        for gi, (bo, t0, nt) in enumerate(segs):
            ps = bank[s + bo][:, 0:nt]
            for k in range(kt):
                passes = [(WH, hi), (WH, lo), (WL, hi)]
                for pi, (w, x) in enumerate(passes):
                    lastmm = k == kt - 1 and pi == 2
                    end = lastmm and gi == len(segs) - 1
                    mm(ps, w[:, s, KD - kt + k, :], x[:, k, t0:t0 + nt], k == 0 and pi == 0, lastmm,
                       inc=unit_done[s] if end else None)
            outs.append(ps)
        evict(outs, pe.last, bank_free[s])
        if ada and ada[0] == "finish":
            ada_finish(*ada[1:])
        state["n"] += 1

    def ada_begin(src, streams, *_):
        x = state["ada"] % 2
        state["ada"] += 1
        t = prog.dma(pool, ada_w[:, x], src, ada_full[x], after=[ada_ready[x].now()])
        for j, c in enumerate(streams):
            for k in range(KD):
                end = k == KD - 1 and j == len(streams) - 1
                inc = ada_ready[x] if end else None
                if k == 0:
                    dve(v.tensor_scalar, ada_acc[:, j], ada_w[:, x, 0], csil[:, c, 0:1], None, ALU.mult,
                        after=[t, t_csil], inc=inc)
                else:
                    dve(v.scalar_tensor_tensor, ada_acc[:, j], ada_w[:, x, k], csil[:, c, k:k + 1], ada_acc[:, j],
                        ALU.mult, ALU.add, inc=inc)

    def ada_finish(src, streams, out, bias):
        pe.wait(ada_ready[(state["ada"] - 1) % 2].now(), bank_free[7].now())
        for j in range(len(streams)):
            for h in range(2):
                mm(bank[7][:, 2 * j + h:2 * j + h + 1], ada_acc[:, j, h * P:(h + 1) * P], one_row, True, True,
                   done=(j == len(streams) - 1 and h == 1))
        t = pe.last
        for j in range(len(streams)):
            dve(v.tensor_tensor, out[j], bank[7][:, 2 * j:2 * j + 2], bias, ALU.add, after=[t],
                inc=bank_free[7] if j == len(streams) - 1 else None)

    wada1 = a["w_ada"].rearrange("l (k p) n -> l p k n", p=P)
    wada2 = a["w_ada_2"].rearrange("l (k p) n -> l p k n", p=P)

    def ada1(l, u):
        bias = cols1_all[:, ds(u * 2 + (l * NC1 + COLS1["b_ada"][0]), 2)]
        return wada1[l][:, :, ds(u * 256, 256)], (0,), [mod1[:, ds(u * 2, 2)]], bias

    def ada2(l, u):
        bias = cols2_all[:, ds(u * 2 + (l * NC2 + COLS2["b_ada"][0]), 2)]
        return (wada2[l][:, :, ds(u * 256, 256)], (1, 2),
                [mod2[:, ds(u * 2 + (l * 96 + 48 * j), 2)] for j in range(2)], bias)

    sq = tmpf

    NORM_X = [tmpf[:, 0, :], tmpf[:, 1, :], tmpf[:, 3, :]]
    c_buf = tmpf[:, 2, 0:TC]
    NORM_C = [c_buf, c_buf, tmpf[:, 2, TC:2 * TC]]

    def norm_sum(src_of, nt, bk, buf):
        read = [pe.last, pe.last]
        act.wait(dve.last)
        for k in range(KD):
            y = buf[k % 2][:, 0:nt]
            t = act(s_.activation, y, src_of(k), ACT.Square, after=[read[k % 2]])
            if k == 0:
                pe.wait(bank_free[bk].now())
            read[k % 2] = mm(bank[bk][:, 0:nt], ones[:], y, k == 0, k == KD - 1, after=[t], done=True)
            if buf[0] is buf[1]:
                read = [pe.last, pe.last]
            yield

    def rstd(out, ps, after, n_mean, eps, inc=None):
        act(s_.activation, out, ps, ACT.Ln, scale=1.0 / n_mean, bias=eps, after=[after, dve.last], inc=inc)
        return act(s_.activation, out, out, ACT.Exp, scale=-0.5)

    def split_store(hi, lo, exact, after=(), inc=None):
        t = act(s_.copy, hi, exact, after=[*after, dve.last])
        return dve(v.tensor_tensor, lo, exact, hi.bitcast(F32), ALU.subtract, after=[t], inc=inc)

    def norm_chain(hi, lo, t0, h0, nt, g, shift, bk, buf):
        yield from norm_sum(lambda k: XC[:, k, t0:t0 + nt], nt, bk, buf)
        r = buf[2][:, 0:nt]
        t = rstd(r, bank[bk][:, 0:nt], pe.last, D, eps_col, inc=bank_free[bk])
        ahead = 0 if buf[0] is buf[1] else 1
        t_y = []
        for k in range(KD):
            y = buf[k % 2][:, 0:nt]
            while len(t_y) < min(k + ahead + 1, KD):
                i = len(t_y)
                t_y.append(dve(v.tensor_tensor, buf[i % 2][:, 0:nt], XC[:, i, t0:t0 + nt], r, ALU.mult,
                               after=[t, pe.last]))
            act(s_.activation, y, y, ACT.Identity, scale=g[:, k:k + 1], bias=shift[:, k:k + 1], after=[t_y[k]])
            split_store(hi[:, k, h0:h0 + nt], lo[:, k, h0:h0 + nt], y)
            yield

    def norm_mod(hi, lo, segs):
        prog.interleave(*[norm_chain(hi, lo, *seg, bk, buf)
                          for seg, bk, buf in zip(segs, (4, 5), (NORM_X, NORM_C))])

    X1 = [(0, 0, T)]
    X0 = [(0, TC, T)]
    XB = [(0, TC, T), (4, 0, TC)]

    wf_in = [a[n].rearrange("l (k p) n -> l p k n", p=P) for n in ("w_ffn1_in", "w_ffn2_in")]
    wf_out = [a[n].rearrange("l (k p) n -> l p k n", p=P) for n in ("w_ffn1_out", "w_ffn2_out")]
    wmix_in = a["w_mix_in"].rearrange("l (k p) n -> l p k n", p=P)
    wmix_out = a["w_mix_out"].rearrange("l (k p) n -> l p k n", p=P)

    def c1(name):
        o, w = COLS1[name]
        return cols1[:, o:o + w]

    def c2(name):
        o, w = COLS2[name]
        return cols2[:, o:o + w]

    def evict_add(n, coef):
        def go(ps, t, free):
            xa = XC[:, ds(n, 1), TC:TT].rearrange("p a n -> p (a n)")
            dve(v.scalar_tensor_tensor, xa, ps[0], coef[:, ds(n, 1)], xa, ALU.mult, ALU.add, after=[t], inc=free)
        return go

    def ffn(l, which, ada_in, ada_out):
        w_in, w_out = wf_in[which][l], wf_out[which][l]
        coef = small[:, 8:16]
        pe.wait(dve.last)
        for c, (j0, nj) in enumerate([(0, 8), (8, 8), (16, 6)]):
            with prog.loop(f"ffn{which}_in{c}", nj // 2) as i:
                for q in range(2):
                    col = (i * 2 + (j0 + q)) * P

                    def ev_gate(ps, t, free, q=q):
                        act(s_.activation, tmpf[:, q, :], ps[0], ACT.Silu, after=[t], inc=free)

                    def ev_up(ps, t, free, q=q):
                        y = tmpf[:, q, :]
                        dve(v.tensor_tensor, y, y, ps[0], ALU.mult, after=[t, act.last])
                        hi = GH[:, ds(i * 2 + q, 1), 0:T].rearrange("p a n -> p (a n)")
                        lo = GL[:, ds(i * 2 + q, 1), 0:T].rearrange("p a n -> p (a n)")
                        split_store(hi, lo, y, inc=free)

                    job = ada_in(c, i * 2 + q) if which == 0 else ada_in(c, i if c == 1 else i * 2 + q, q)
                    unit(w_in[:, :, ds(col, P)], KD, X1, H1H, H1L, ev_gate, ada=job and ("begin", *job))
                    unit(w_in[:, :, ds(col + D_FF, P)], KD, X1, H1H, H1L, ev_up, ada=job and ("finish", *job))
            pe.wait(bank_free[1].now(), bank_free[3].now())
            with prog.loop(f"ffn{which}_out{c}", 2) as i:
                for q in range(4):
                    job = ada_out(c, i * 2 + q // 2)
                    unit(w_out[:, j0 + nj - KD:j0 + nj, ds((i * 4 + q) * P, P)], nj, X1, GH, GL,
                         evict_add(i * 4 + q, coef), ada=job and (("begin", "finish")[q % 2], *job))

    def stage_cols(g, i):
        sc, gt = mod1[:, (i + 1) * 8:(i + 2) * 8], mod1[:, (i + 2) * 8:(i + 3) * 8]
        dve(v.tensor_scalar, small[:, 0:8], sc, 1.0, None, ALU.add)
        dve(v.tensor_tensor, small[:, 0:8], small[:, 0:8], g, ALU.mult)
        half = 1.0 if i == 3 else 0.5
        dve(v.tensor_scalar, small[:, 8:16], gt, half, half, ALU.mult, ALU.add)
        return mod1[:, i * 8:(i + 1) * 8]

    PJ = region("PJ", G0, [P, NP1, T + 2])
    S_FREE = G0 + NP1 * (T + 2)
    HT, LT = KD * T, KD * TT + KD * T
    att_s = region("att_s", HT, [P, 2, 4, 256])
    att_pt = region("att_pt", LT, [P, 2, 8, P])
    kdup = region("kdup", S_FREE, [P, 2, P + T])
    vnat = region("vnat", S_FREE + 1280, [P, 5, P])
    att_y = region("att_y", S_FREE + 1920, [P, 2, 2, P])
    kd_in = prog.counter("kd_in")

    def heads_rms(tiles):
        act.wait(dve.last, pe.last)
        buf = [tmpf[:, i, :] for i in range(4)] + [att_s[:, 0].rearrange("p h n -> p (h n)")[:, 0:T]]
        t_b = []
        for i, (x, _) in enumerate(tiles):
            act(s_.activation, buf[i], x, ACT.Square)
            t_b.append(mm(bank[i][:], blk, buf[i], True, True, after=[act.last], done=True))
        for i in range(len(tiles)):
            act(s_.activation, buf[i], bank[i][:], ACT.Ln, scale=1.0 / HD, bias=eps_col, after=[t_b[i]])
        for i, (x, gain) in enumerate(tiles):
            act(s_.activation, buf[i], buf[i], ACT.Exp, scale=-0.5)
            dve(v.scalar_tensor_tensor, x, x, gain, buf[i], ALU.mult, ALU.mult, after=[act.last])

    def attention():
        heads_rms([(PJ[:, i, 2:2 + T], c1("q_gain") if i < 4 else c1("k_gain")) for i in (4, 0, 1, 2, 3)])
        dve(v.memset, kdup[:, :, 0:P], 0.0)
        dve(v.memset, vnat[:, 0, :], 0.0)
        for h in range(2):
            for half in range(2):
                t_kd = prog.dma(act, kdup[64 * half:64 * half + 64, h, P:P + T],
                                PJ[64 * h:64 * h + 64, 4, 2:2 + T], kd_in, after=[dve.last])
        for b in range(4):
            prog.transpose(bank[6][:, b * P:(b + 1) * P], PJ[:, 5, 2 + b * P:2 + (b + 1) * P], ident,
                           after=[dve.last], done=b == 3)
        dve(v.tensor_copy, vnat[:, 1:5, :], bank[6][:].rearrange("p (b n) -> p b n", b=4), after=[pe.last])
        prog.interleave(*[attention_group(kv, t_kd, [dve.last, act.last]) for kv in range(2)], conv1())

    def attention_group(kv, t_kd, t_v):
        b0 = 4 * kv
        S, PT = att_s[:, kv], att_pt[:, kv]
        m, e1, den = (small[:, o + 4 * kv:o + 4 * kv + 4] for o in (16, 24, 32))
        sinks = c1("sinks")[:, 4 * kv:4 * kv + 4]
        for b in range(4):
            pe.wait(t_kd, *t_v, act.last, dve.last)

            def score(h, done):
                pr = 64 * (h % 2)
                mm(bank[b0 + h // 2][:, (h % 2) * 256:(h % 2) * 256 + 256],
                   PJ[pr:pr + 64, 2 * kv + h // 2, 2 + b * P:2 + (b + 1) * P],
                   kdup[pr:pr + 64, kv, b * P:b * P + 256], True, True, done=done)
            prog.by_half(range(4), score)
            yield
            msk = k_("attmask")[:, (0 if b == 0 else 256):(0 if b == 0 else 256) + 256]
            for h in range(4):
                dve(v.scalar_tensor_tensor, S[:, h, :], bank[b0 + h // 2][:, (h % 2) * 256:(h % 2) * 256 + 256],
                    HD ** -0.5, msk, ALU.mult, ALU.add, after=[pe.last])
            yield
            dve(v.tensor_reduce, m, S, AX.X, ALU.max)
            dve(v.tensor_tensor, m, m, sinks, ALU.max)
            dve(v.tensor_tensor, S, S, m.unsqueeze(2).broadcast_to([P, 4, 256]), ALU.subtract)
            dve(v.tensor_tensor, e1, sinks, m, ALU.subtract)
            yield
            act(s_.activation, S, S, ACT.Exp, after=[dve.last])
            act(s_.activation, e1, e1, ACT.Exp)
            yield
            dve(v.tensor_reduce, den, S, AX.X, ALU.add, after=[act.last])
            dve(v.tensor_tensor, den, den, e1, ALU.add)
            dve(v.reciprocal, den, den)
            dve(v.tensor_tensor, S, S, den.unsqueeze(2).broadcast_to([P, 4, 256]), ALU.mult)
            t_p = dve.last
            yield
            for q in range(2):
                for i in range(4 * q, 4 * q + 4):
                    prog.transpose(bank[b0 + 2 + q][:, (i % 4) * P:(i % 4 + 1) * P],
                                   S[:, i // 2, (i % 2) * P:(i % 2 + 1) * P], ident, after=[t_p], done=i % 4 == 3)
                f = (dve, v.tensor_copy) if q else (act, s_.copy)
                f[0](f[1], PT[:, 4 * q:4 * q + 4, :], bank[b0 + 2 + q][:].rearrange("p (b n) -> p b n", b=4),
                     after=[pe.last])
            yield
            pe.wait(act.last, dve.last)
            for h in range(4):
                pr = 64 * (h % 2)
                for x in range(2):
                    mm(bank[b0 + h % 2][pr:pr + 64, (h // 2) * P:(h // 2 + 1) * P],
                       vnat[:, b + x, 64 * kv:64 * kv + 64], PT[:, 2 * h + x, :], x == 0, x == 1,
                       done=h == 3 and x == 1)
            yield
            y = att_y[:, kv]
            src = [bank[b0 + x][64 * x:64 * x + 64, 0:256].rearrange("p (i n) -> p i n", i=2) for x in range(2)]
            act(s_.copy, y[0:64], src[0], after=[pe.last, dve.last])
            dve(v.tensor_copy, y[64:128], src[1], after=[pe.last])
            split_store(H1H[:, 2 * kv:2 * kv + 2, b * P:(b + 1) * P], H1L[:, 2 * kv:2 * kv + 2, b * P:(b + 1) * P],
                        y, after=[act.last])
            yield

    PR = [region("PRa", HT, [P, 4, T]), region("PRb", LT, [P, 4, T])]

    def conv1():
        w = c1("conv")
        for i in range(2):
            u = PJ[:, 18 + i, :]
            dve(v.tensor_tensor, u, u, PJ[:, 16 + i, :], ALU.mult)
            y = tmpf[:, 2, :]
            yield
            dve(v.tensor_scalar, y, u[:, 0:T], w[:, 3 * i:3 * i + 1], None, ALU.mult, after=[act.last])
            yield
            for k in (1, 2):
                dve(v.scalar_tensor_tensor, y, u[:, k:k + T], w[:, 3 * i + k:3 * i + k + 1], y, ALU.mult, ALU.add)
            yield
            dve(v.tensor_tensor, y, y, PJ[:, 14 + i, 2:2 + T], ALU.mult)
            split_store(H1H[:, 6 + i, :], H1L[:, 6 + i, :], y)
            yield

    names = ["gg", "lw", "aa", "kk", "cm", "ee", "bonus"]
    rw = {n: region("rw_" + n, G0 + 1024 * i, [P, 2, T]) for i, n in enumerate(names)}
    r1 = G0 + 7 * 1024
    rw_nat = region("rw_nat", r1, [P, 3, 2, P])
    rw_L = region("rw_L", r1 + 768, [P, 2, MH, P])
    rw_T = region("rw_T", r1 + 768 + 1024, [P, 2, MH, P])
    rw_Z = region("rw_Z", r1 + 768 + 2048, [P, 2, MH, P])
    rw_M = region("rw_M", r1 + 768 + 3072, [P, 3, MH, P])
    rw_W = region("rw_W", r1 + 768 + 3072 + 1536, [P, 256])
    rw_U = region("rw_U", r1 + 768 + 3072 + 1792, [P, 256])
    rw_X = region("rw_X", r1 + 768 + 3072 + 2048, [P, 2, HD])
    assert 768 + 3072 + 2048 + 128 + 7 * 1024 <= ADA0 - G0
    rw_Q = [region("rw_Qa", 4 * T, [P, 2, MH, P]), region("rw_Qb", KD * TT + 4 * T, [P, 2, MH, P])]

    def rwkv_shift():
        for i in range(8):
            src = PJ[:, 6 + i, :]
            dst = PR[i // 4][:, i % 4, :]
            dve(v.tensor_tensor, dst, src[:, 1:1 + T], src[:, 2:2 + T], ALU.subtract)
            dve(v.scalar_tensor_tensor, dst, dst, c1("mu")[:, i:i + 1], src[:, 2:2 + T], ALU.mult, ALU.add)

    def rwkv():
        tile = lambda i: PR[i // 4][:, i % 4, :]
        r, k, vv = PR[0][:, 0:2, :], PR[0][:, 2:4, :], PR[1][:, 0:2, :]
        wad, gd = tile(6), tile(7)
        gg, lw, aa, kk, cm, ee, bonus = (rw[n] for n in names)
        act(s_.activation, wad[0:64, :], wad[0:64, :], ACT.Tanh, after=[dve.last])
        t_in = act(s_.activation, gd, gd, ACT.Sigmoid)
        for i in range(2):
            mm(bank[i][:], lora[0:64, 0, i * P:(i + 1) * P], wad[0:64, :], True, True, after=[t_in, dve.last])
            mm(bank[2 + i][:], lora[64:128, 0, i * P:(i + 1) * P], wad[64:128, :], True, True)
            mm(bank[4 + i][:], lora[:, 1, i * P:(i + 1) * P], gd, True, True, done=True)
        for i in range(2):
            act(s_.activation, lw[:, i, :], bank[i][:], ACT.Sigmoid, bias=c1("w0")[:, i:i + 1], after=[pe.last])
            act(s_.activation, aa[:, i, :], bank[2 + i][:], ACT.Sigmoid, bias=c1("a0")[:, i:i + 1])
            act(s_.copy, gg[:, i, :], bank[4 + i][:])
        dve(v.tensor_scalar, lw[:], lw[:], -DECAY_SCALE, None, ALU.mult, after=[act.last])
        for i in range(2):
            dve(v.tensor_scalar, kk[:, i, :], k[:, i, :], c1("k_k")[:, i:i + 1], None, ALU.mult)
            act(s_.activation, ee[:, i, :], kk[:, i, :], ACT.Square, after=[dve.last])
            mm(bank[6 + i][:], blk, ee[:, i, :], True, True, after=[act.last], done=True)
        for i in range(2):
            act(s_.activation, ee[:, i, :], bank[6 + i][:], ACT.Sqrt, after=[pe.last])
        dve(v.tensor_scalar, ee[:], ee[:], 1e-12, None, ALU.max, after=[act.last])
        dve(v.reciprocal, ee[:], ee[:])
        dve(v.tensor_tensor, kk[:], kk[:], ee[:], ALU.mult)
        for i in range(2):
            dve(v.tensor_scalar, ee[:, i, :], aa[:, i, :], -1.0, c1("k_a")[:, i:i + 1], ALU.add, ALU.mult)
            dve(v.scalar_tensor_tensor, k[:, i, :], ee[:, i, :], 1.0, k[:, i, :], ALU.add, ALU.mult)
            dve(v.scalar_tensor_tensor, ee[:, i, :], r[:, i, :], c1("r_k")[:, i:i + 1], k[:, i, :],
                ALU.mult, ALU.mult)
            mm(bank[6 + i][:], blk, ee[:, i, :], True, True, after=[dve.last], done=True)
            dve(v.tensor_tensor, bonus[:, i, :], bank[6 + i][:], vv[:, i, :], ALU.mult, after=[pe.last])
        dve(v.tensor_tensor, aa[:], aa[:], kk[:], ALU.mult)
        for i in range(2):
            for c in range(4):
                dve(v.tensor_tensor_scan, cm[:, i, c * P:(c + 1) * P], ones[:], lw[:, i, c * P:(c + 1) * P], 0.0,
                    ALU.mult, ALU.add)
        mid, end = small[:, 16:24], small[:, 24:32]
        cm4 = cm[:].rearrange("p i (c n) -> p (i c) n", c=4)
        dve(v.tensor_copy, mid, cm4[:, :, 63])
        dve(v.tensor_tensor, cm4, cm4, mid.unsqueeze(2).broadcast_to([P, 8, P]), ALU.subtract)
        dve(v.tensor_copy, end, cm4[:, :, P - 1])
        m8, e8 = mid.rearrange("p (i c) -> p i c", i=2), end.rearrange("p (i c) -> p i c", i=2)
        dve(v.tensor_tensor, e8[:, :, 0:3], e8[:, :, 0:3], m8[:, :, 1:4], ALU.add)
        t_end = act(s_.activation, end, end, ACT.Exp, after=[dve.last])
        act(s_.activation, ee[:], cm[:], ACT.Exp)
        dve(v.tensor_tensor, r, r, ee[:], ALU.mult, after=[act.last])
        dve(v.tensor_tensor, lw[:], cm[:], lw[:], ALU.subtract)
        act(s_.activation, lw[:], lw[:], ACT.Exp, after=[dve.last])
        dve(v.tensor_tensor, kk[:], kk[:], lw[:], ALU.mult, after=[act.last])
        act(s_.activation, ee[:], cm[:], ACT.Exp, scale=-1.0, after=[dve.last])
        dve(v.tensor_tensor, aa[:], aa[:], ee[:], ALU.mult, after=[act.last])
        dve(v.tensor_tensor, k, k, ee[:], ALU.mult)

        def hs(x, h, c):
            return x[64 * (h % 2):64 * (h % 2) + 64, h // 2, c * P:(c + 1) * P]

        def hb(j):
            return bank[j][:].rearrange("p (h n) -> p h n", h=MH)

        def wide(m):
            return m.unsqueeze(1).broadcast_to([P, MH, P])

        for pair in range(2):
            Q = rw_Q[pair]
            t_in = dve.last
            for x in range(2):
                c = 2 * pair + x
                pe.wait(t_in)

                def gram(h, done):
                    mm(bank[x][:, h * P:(h + 1) * P], hs(kk, h, c), hs(aa, h, c), True, True)
                    mm(bank[2 + x][:, h * P:(h + 1) * P], hs(aa, h, c), hs(kk, h, c), True, True, done=done)
                prog.by_half(range(MH), gram)
            for x in range(2):
                dve(v.tensor_copy, rw_L[:, x], hb(x), after=[pe.last])
                dve(v.tensor_tensor, rw_T[:, x], rw_L[:, x], wide(k_("levels")[:, 0:P]), ALU.mult)
                dve(v.tensor_tensor, rw_T[:, x], rw_T[:, x], wide(ident), ALU.add)
                dve(v.tensor_tensor, Q[:, x], hb(2 + x), wide(k_("level0T")), ALU.mult)
                dve(v.tensor_tensor, Q[:, x], Q[:, x], wide(ident), ALU.add)
            for lv in range(1, RW_LEVELS):
                more = lv < RW_LEVELS - 1
                t_z = [None, None]
                for x in range(2):
                    m = tmpf[:, x, :].rearrange("p (h n) -> p h n", h=MH)
                    dve(v.tensor_tensor, m, rw_L[:, x], wide(k_("levels")[:, lv * P:(lv + 1) * P]), ALU.mult)
                    for h in range(MH):
                        t_z[x] = mm(bank[x][:, h * P:(h + 1) * P], m[:, h, :], Q[:, x, h, :], True, True,
                                    after=[dve.last], done=h == MH - 1)
                for x in range(2):
                    act(s_.copy, rw_Z[:, x], hb(x), after=[t_z[x]])
                    for h in range(MH):
                        if more:
                            mm(bank[4 + x][:, h * P:(h + 1) * P], rw_Z[:, x, h, :], rw_T[:, x, h, :], True, True,
                               after=[act.last])
                        t_z[x] = mm(bank[2 + x][:, h * P:(h + 1) * P], rw_T[:, x, h, :], rw_Z[:, x, h, :],
                                    True, True, after=[act.last], done=h == MH - 1)
                for x in range(2):
                    dve(v.tensor_tensor, Q[:, x], Q[:, x], hb(2 + x), ALU.add, after=[t_z[x]])
                    if more:
                        dve(v.tensor_tensor, rw_T[:, x], rw_T[:, x], hb(4 + x), ALU.add)
        for c in range(4):
            Q = rw_Q[c // 2][:, c % 2]
            t_in = [dve.last, act.last]
            for j, src in enumerate((aa, k, vv)):
                for i in range(2):
                    n = 2 * j + i
                    prog.transpose(bank[4 + n // 4][:, (n % 4) * P:(n % 4 + 1) * P],
                                   src[:, i, c * P:(c + 1) * P], ident, after=t_in, done=n == 5)
            act(s_.copy, rw_nat[:, 0:2], bank[4][:].rearrange("p (j i n) -> p j i n", j=2, i=2), after=[pe.last])
            t_nat = act(s_.copy, rw_nat[:, 2], bank[5][:, 0:256].rearrange("p (i n) -> p i n", i=2))
            nat = lambda j, h: rw_nat[:, j, h // 2, 64 * (h % 2):64 * (h % 2) + 64]
            for j, (lh, rh) in enumerate(((k, kk), (aa, r), (k, r))):
                prog.by_half(range(MH), lambda h, done: mm(bank[j][:, h * P:(h + 1) * P], hs(lh, h, c), hs(rh, h, c),
                                                           True, True, done=done))
                dve(v.tensor_tensor, rw_M[:, j], hb(j), wide(k_("upper" if j == 0 else "upper_eq")), ALU.mult,
                    after=[pe.last, t_nat])
            pe.wait(dve.last)

            def w_head(h, done):
                o = bank[3][:, 64 * h:64 * h + 64]
                pr = 64 * (h % 2)
                if c:
                    mm(o, hs(kk, h, c), rw_X[pr:pr + 64, h // 2, :], True, False)
                mm(o, rw_M[:, 0, h, :], nat(2, h), c == 0, True, done=done)
            prog.by_half(range(MH), w_head)
            dve(v.tensor_copy, rw_W[:], bank[3][:, 0:256], after=[pe.last])
            for h in range(MH):
                mm(bank[3][:, 256 + 64 * h:320 + 64 * h], Q[:, h, :], rw_W[:, 64 * h:64 * h + 64], True, True,
                   after=[dve.last], done=h == MH - 1)
            dve(v.tensor_scalar, rw_U[:], bank[3][:, 256:512], -1.0, None, ALU.mult, after=[pe.last])
            for h in range(MH):
                pr = 64 * (h % 2)
                o = bank[6 + h % 2][pr:pr + 64, (h // 2) * P:(h // 2 + 1) * P]
                if c:
                    mm(o, rw_X[pr:pr + 64, h // 2, :], hs(r, h, c), True, False)
                mm(o, nat(2, h), rw_M[:, 2, h, :], c == 0, False)
                mm(o, rw_U[:, 64 * h:64 * h + 64], rw_M[:, 1, h, :], False, True, after=[dve.last],
                   done=h == MH - 1)
            for x in range(2):
                pr = 64 * x
                act(s_.copy, lw[pr:pr + 64, :, c * P:(c + 1) * P],
                    bank[6 + x][pr:pr + 64, 0:256].rearrange("p (i n) -> p i n", i=2), after=[pe.last])
            if c < 3:
                for h in range(MH):
                    pr = 64 * (h % 2)
                    o = bank[4 + h % 2][pr:pr + 64, 64 * (h // 2):64 * (h // 2) + 64]
                    mm(o, nat(1, h), nat(2, h), True, False)
                    mm(o, nat(0, h), rw_U[:, 64 * h:64 * h + 64], False, True, done=h == MH - 1)
                for x in range(2):
                    pr = 64 * x
                    for i in range(2):
                        o, ps = rw_X[pr:pr + 64, i, :], bank[4 + x][pr:pr + 64, 64 * i:64 * i + 64]
                        e = e8[pr:pr + 64, i, c:c + 1]
                        if c:
                            dve(v.tensor_tensor, o, o, ps, ALU.add, after=[pe.last])
                            dve(v.tensor_scalar, o, o, e, None, ALU.mult)
                        else:
                            dve(v.tensor_scalar, o, ps, e, None, ALU.mult, after=[pe.last, t_end])
        for i in range(2):
            y, d2, rs = lw[:, i, :], tmpf[:, 0, :], tmpf[:, 1, :]
            mm(bank[0][:], blk, y, True, True, after=[act.last, dve.last], done=True)
            dve(v.scalar_tensor_tensor, y, bank[0][:], -1.0 / HD, y, ALU.mult, ALU.add, after=[pe.last])
            act(s_.activation, d2, y, ACT.Square, after=[dve.last])
            t = mm(bank[1][:], blk, d2, True, True, after=[act.last], done=True)
            rstd(rs, bank[1][:], t, HD, gn_eps_col)
            dve(v.tensor_tensor, y, y, rs, ALU.mult, after=[act.last])
            dve(v.tensor_scalar, y, y, c1("gn_w")[:, i:i + 1], c1("gn_b")[:, i:i + 1], ALU.mult, ALU.add)
            dve(v.tensor_tensor, y, y, bonus[:, i, :], ALU.add)
            dve(v.tensor_tensor, y, y, gg[:, i, :], ALU.mult)
            split_store(H1H[:, 4 + i, :], H1L[:, 4 + i, :], y)

    def mix1(l):
        pe.wait(dve.last)
        with prog.loop("mix_in", NP1 // 4) as i:
            for q in range(4):
                def ev(ps, t, free, q=q):
                    o = PJ[:, ds(i * 4 + q, 1), 2:2 + T].rearrange("p a n -> p (a n)")
                    act(s_.copy, o, ps[0], after=[t], inc=free)
                unit(wmix_in[l][:, :, ds((i * 4 + q) * P, P)], KD, X1, H1H, H1L, ev)
        prog.barrier()
        dve(v.memset, PJ[:, :, 0:2], 0.0)
        attention()
        prog.barrier()
        rwkv_shift()
        prog.barrier()
        rwkv()
        prog.barrier()
        pe.wait(dve.last)
        with prog.loop("mix_out", 2) as i:
            for q in range(4):
                unit(wmix_out[l][:, :, ds((i * 4 + q) * P, P)], KD, X1, H1H, H1L,
                     evict_add(i * 4 + q, small[:, 8:16]))

    with prog.loop("ada_first", 7) as u:
        for j in range(2):
            ada_begin(*ada1(0, u * 2 + j))
            ada_finish(*ada1(0, u * 2 + j))
    for _ in range(AHEAD):
        split_next()

    with prog.loop("layers1", DEPTH) as l:
        prog.dma(act, lora[:], a["lora"][l], in_lora)
        dve(v.tensor_copy, cols1[:], cols1_all[:, ds(l * NC1, NC1)])
        pe.wait(in_lora.now())
        shift = stage_cols(c1("g_ffn1"), 0)
        norm_mod(H1H, H1L, [(TC, 0, T, small[:, 0:8], shift)])
        ffn(l, 0, lambda c, j: ada1(l, j + (14 + 8 * c)), lambda c, j: ada2(l, j + 4 * c))
        prog.barrier()
        shift = stage_cols(c1("g_mix"), 3)
        norm_mod(H1H, H1L, [(TC, 0, T, small[:, 0:8], shift)])
        mix1(l)
        prog.barrier()
        shift = stage_cols(c1("g_ffn2"), 6)
        norm_mod(H1H, H1L, [(TC, 0, T, small[:, 0:8], shift)])

        def ada_in(c, j, q):
            if c == 0:
                return ada2(l, j + 12)
            if c == 1:
                return ada2(l, 20 + j) if q == 0 else ada1(1, j)
            return ada1(1, j + 4)
        ffn(l, 1, ada_in, lambda c, j: ada1(1, j + 10) if c == 0 else None)
        prog.barrier()

    QK = region("QK", G0, [P, 8, TT])
    SO = region("SO", G0 + 6144, [P, MH, TT])
    VN = region("VN", G0 + 9216, [P, TT // P, 512])
    CUW = TT + 4 * 15
    CU = region("CU", G0 + 12288, [P, 2, CUW])
    UT = region("UT", G0 + 12288 + 2 * CUW, [P, 2, TT])
    GR = region("GR", G0 + 15480, [P, TT])
    RAW = region("RAW", G0 + 16248, [P, 2, TT + 4])
    VF = [region("VFa", G0 + 12288, [P, 3, 4, P]), region("VFb", G0 + 16248, [P, 3, 4, P])]
    DFT = [region("DFT_cos", 0, [P, 4, T]), region("DFT_sin", KD * TT, [P, 4, T])]
    DFTC = [region("DFTC_cos", 2048, [P, 2, TC]), region("DFTC_sin", KD * TT + 2048, [P, 2, TC])]
    CA = region("CA", G0 + 17792, [P, 2, TT])
    GI = region("GI", G0 + 16248, [4, 4, TT])
    MC = region("MC", G0 + 12288, [4, 2, TT])
    GS = region("GS", G0 + 13824, [P, TT // P, 2, MH])
    WT = region("WT", G0 + 13944, [P, 2, 2, T])
    WS = region("WS", G0 + 15992, [P, 2, T])
    HA = region("HA", G0 + 17016, [P, T])
    OUT = region("OUT", G0 + 12288, [P, KD, TT])
    POS = region("POS", G0, [P, KD, T])
    assert 16248 + 3072 <= RN - G0

    w_in2 = a["w_in_2"].rearrange("l (k p) n -> l p k n", p=P)
    w_out2 = a["w_out_2"].rearrange("l (k p) n -> l p k n", p=P)
    w_mlp1 = a["w_mlp1_2"].rearrange("l (k p) n -> l p k n", p=P)
    w_mlp2 = a["w_mlp2_2"].rearrange("l (k p) n -> l p k n", p=P)
    
    def m2(l, stream, row):
        o = l * 96 + stream * 48 + row * 8
        return mod2[:, o:o + 8]

    def tile_evict(dst):
        def go(ps, t, free):
            act(s_.copy, dst[:, TC:TT], ps[0], after=[t], inc=None if len(ps) > 1 else free)
            if len(ps) > 1:
                act(s_.copy, dst[:, 0:TC], ps[1], inc=free)
        return go

    def unit_nat(src, tile, nt):
        s = load(src)
        split_next()
        pe.wait(split_done[s].now(), bank_free[s].now())
        for b in range(nt):
            ps = bank[s + 4 * (b // 4)][:, (b % 4) * P:(b % 4 + 1) * P]
            for k in range(KD):
                passes = [(HH, WH), (HL, WH), (HH, WL)]
                for pi, (x, w) in enumerate(passes):
                    mm(ps, x[:, k, b * P:(b + 1) * P], w[:, s, k, :], k == 0 and pi == 0, k == KD - 1 and pi == 2,
                       inc=unit_done[s] if (b, k, pi) == (nt - 1, KD - 1, 2) else None)
        t = pe.last
        act(s_.copy, VN[:, 0:4, tile * P:(tile + 1) * P], bank[s][:].rearrange("p (b n) -> p b n", b=4), after=[t])
        act(s_.copy, VN[:, 4:6, tile * P:(tile + 1) * P], bank[s + 4][:, 0:256].rearrange("p (b n) -> p b n", b=2),
            inc=bank_free[s])
        state["n"] += 1

    def project(l, ctx):
        both = XB if ctx else X0
        pe.wait(dve.last)

        def cols_of(at):
            return w_in2[l][:, :, ds(at, P)]

        dve(v.memset, CU[:], 0.0)
        for i in range(2):
            def ev_gate(ps, t, free):
                act(s_.activation, tmpf[:, 0, :], ps[0], ACT.Sigmoid, after=[t, dve.last],
                    inc=None if len(ps) > 1 else free)
                if len(ps) > 1:
                    act(s_.activation, tmpf[:, 1, 0:TC], ps[1], ACT.Sigmoid, inc=free)

            def ev_a(ps, t, free, i=i):
                dve(v.tensor_tensor, CU[:, i, TC + 45:TC + 45 + T], ps[0], tmpf[:, 0, :], ALU.mult,
                    after=[t, act.last], inc=None if len(ps) > 1 else free)
                if len(ps) > 1:
                    dve(v.tensor_tensor, CU[:, i, 15:15 + TC], ps[1], tmpf[:, 1, 0:TC], ALU.mult, inc=free)
            unit(cols_of(C_OFF + 256 + i * P), KD, both, HH, HL, ev_gate)
            unit(cols_of(C_OFF + i * P), KD, both, HH, HL, ev_a)
        taps = conv31_taps(ctx)

        def some_taps():
            for _ in range(2):
                next(taps, None)
        for i in range(2):
            unit(cols_of(F_OFF + i * P), KD, both, HH, HL, tile_evict(UT[:, i, :]))
            some_taps()
        unit(cols_of(G_OFF), KD, XB, HH, HL, tile_evict(GR[:, :]))
        some_taps()
        for i in range(4):
            unit_nat(cols_of(1024 + i * P), i, TT // P)
            some_taps()
        for q in range(4):
            def ev_o(ps, t, free, q=q):
                act(s_.activation, SO[:, q, TC:TT], ps[0], ACT.Sigmoid, after=[t],
                    inc=None if len(ps) > 1 else free)
                if len(ps) > 1:
                    act(s_.activation, SO[:, q, 0:TC], ps[1], ACT.Sigmoid, inc=free)
            unit(cols_of(1536 + q * P), KD, both, HH, HL, ev_o)
            some_taps()
        dve(v.memset, RAW[:], 0.0)
        wq = cols2[:, COLS2["qk_conv"][0]:COLS2["qk_conv"][0] + 24]
        dve(v.tensor_scalar, wq[:, 12:24], wq[:, 12:24], 128.0 ** -0.5, None, ALU.mult)
        act.wait(dve.last)
        for half in range(2):
            segs = XB if half or ctx else X0
            for q in range(4):
                def ev(ps, t, free, q=q, half=half):
                    r = RAW[:, q % 2, :]
                    act(s_.copy, r[:, TC + 3:TC + 3 + T], ps[0], after=[t, dve.last],
                        inc=None if len(ps) > 1 else free)
                    if len(ps) > 1:
                        act(s_.copy, r[:, 1:1 + TC], ps[1], inc=free)
                    for r0, t0, nt in [(TC + 2, TC, T), (0, 0, TC)][:len(ps)]:
                        o = QK[:, 4 * half + q, t0:t0 + nt]
                        w = wq[:, 12 * half + 3 * q:12 * half + 3 * q + 3]
                        dve(v.tensor_scalar, o, r[:, r0:r0 + nt], w[:, 0:1], None, ALU.mult, after=[act.last])
                        for k in (1, 2):
                            dve(v.scalar_tensor_tensor, o, r[:, r0 + k:r0 + k + nt], w[:, k:k + 1], o,
                                ALU.mult, ALU.add)
                unit(cols_of(half * 512 + q * P), KD, segs, HH, HL, ev)
                some_taps()

    def fourier(ctx):
        t_tab, t_read = None, {}
        for j, n in enumerate(("cos", "sin")):
            t_tab = prog.dma(act, DFT[j][:], a["dft_" + n], in_table)
            t_tab = prog.dma(act, DFTC[j][:], a["dftc_" + n], in_table)
        for b in range(0 if ctx else 2, TT // P):
            for x, m in enumerate((k_("c64"), k_("s64"))):
                for i in range(2):
                    mm(bank[b % 2][:, (2 * x + i) * P:(2 * x + i + 1) * P], UT[:, i, b * P:(b + 1) * P], m,
                       True, True, after=[t_read.get(b - 2)], done=x == 1 and i == 1)
            t_read[b] = act(s_.copy, VF[b // 3][:, b % 3].rearrange("p x n -> p (x n)"), bank[b % 2][:],
                            after=[pe.last])
            yield
        pe.wait(act.last, t_tab)
        for b0, nb, t0, nt, tab in [(2, 4, TC, T, DFT), (0, 2, 0, TC, DFTC)][:2 if ctx else 1]:
            for i in range(2):
                n = 0
                ps = bank[4 + i + (0 if b0 else 2)][:, 0:nt]
                for x in range(2):
                    for b in range(b0, b0 + nb):
                        mm(ps, VF[b // 3][:, b % 3, 2 * x + i, :], tab[x][:, b - b0, :], n == 0, n == 2 * nb - 1,
                           done=n == 2 * nb - 1)
                        n += 1
                y = tmpf[:, i, 0:nt]
                act(s_.copy, y, ps, after=[pe.last, dve.last])
                split_store(HH[:, 4 + i, t0:t0 + nt], HL[:, 4 + i, t0:t0 + nt], y)
                yield

    def conv31_parts(ctx):
        return [(TC, T, TC + 30), (0, TC, 0)][:2 if ctx else 1]

    def conv31_taps(ctx):
        w = c2("w_dw")
        for k in range(K2):
            for i in range(2):
                for t0, nt, u0 in conv31_parts(ctx):
                    o, u, wk = CA[:, i, t0:t0 + nt], CU[:, i, u0 + k:u0 + k + nt], w[:, K2 * i + k:K2 * i + k + 1]
                    if k == 0:
                        dve(v.tensor_scalar, o, u, wk, c2("b_dw")[:, i:i + 1], ALU.mult, ALU.add)
                    else:
                        dve(v.scalar_tensor_tensor, o, u, wk, o, ALU.mult, ALU.add)
            yield

    def conv31_finish(ctx):
        for t0, nt, _ in conv31_parts(ctx):
            tiles = [CA[:, i, t0:t0 + nt] for i in range(2)]
            sq2 = [tmpf[:, 2 + i, 0:nt] for i in range(2)]
            for j, y in enumerate(tiles):
                mm(bank[2][:, 0:nt], ones[:], y, j == 0, j == 1, after=[dve.last, act.last], done=True)
            yield
            for j, y in enumerate(tiles):
                dve(v.scalar_tensor_tensor, y, bank[2][:, 0:nt], -1.0 / 256, y, ALU.mult, ALU.add, after=[pe.last])
                act(s_.activation, sq2[j], y, ACT.Square, after=[dve.last])
            yield
            for j in range(2):
                mm(bank[3][:, 0:nt], ones[:], sq2[j], j == 0, j == 1, after=[act.last], done=True)
            yield
            rs = sq2[0]
            rstd(rs, bank[3][:, 0:nt], pe.last, 256, eps_col)
            yield
            for i, y in enumerate(tiles):
                dve(v.tensor_tensor, y, y, rs, ALU.mult, after=[act.last])
                dve(v.tensor_scalar, y, y, c2("g_ln")[:, i:i + 1], c2("b_ln")[:, i:i + 1], ALU.mult, ALU.add)
                act(s_.activation, y, y, ACT.Silu, after=[dve.last])
                yield
            for i, y in enumerate(tiles):
                split_store(HH[:, 6 + i, t0:t0 + nt], HL[:, 6 + i, t0:t0 + nt], y)
            yield

    def gates():
        g16 = GR[0:16, :]
        dve(v.tensor_scalar, g16, g16, c2("b_gate")[0:16, :], None, ALU.add)
        for j in range(4):
            t = prog.dma(act, GI[:, j // 2 + 2 * (j % 2), :], GR[4 * j:4 * j + 4, :], gates_in, after=[dve.last])
        for d in range(2):
            f, m = GI[:, 2 + d, :], MC[:, d, :]
            act(s_.activation, m, f, ACT.Abs, after=[t])
            act(s_.activation, m, m, ACT.Exp, scale=-1.0)
            act(s_.activation, m, m, ACT.Ln, bias=ones[0:4, 0:1])
            dve(v.scalar_tensor_tensor, f, f, 0.0, m, ALU.min, ALU.subtract, after=[act.last])
            g = GI[:, d, :]
            one = ones[0:4, 0:1].broadcast_to([4, TT])

            def scan(out, inp, op):
                if d == 0:
                    dve(v.tensor_tensor_scan, out, one, inp, 0.0, ALU.mult, op)
                else:
                    dve(v.tensor_tensor_scan, out[:, 0:TC][:, ::-1], one[:, 0:TC], inp[:, 0:TC][:, ::-1], 0.0,
                        ALU.mult, op)
                    dve(v.tensor_tensor_scan, out[:, TC:TT][:, ::-1], one[:, 0:T], inp[:, TC:TT][:, ::-1],
                        out[:, 0:1], ALU.mult, op)
            scan(m, f, ALU.add)
            dve(v.tensor_copy, f, m)
            dve(v.tensor_tensor, g, g, f, ALU.subtract)
            scan(m, g, ALU.max)
            dve(v.tensor_tensor, f, f, m, ALU.add)
        for b in range(TT // P):
            for d in range(2):
                at = (2 * b + d) * MH
                prog.transpose(bank[6][:, at:at + MH], GI[:, d, b * P:(b + 1) * P], ident[0:4, 0:4],
                               after=[dve.last], done=True)
        dve(v.tensor_copy, GS[:].rearrange("p b d h -> p (b d h)"), bank[6][:, 0:TT // P * 2 * MH], after=[pe.last])

    def mlstm_main(h, q0, nt, sources, x, shared):
        sel = k_("sel")[0:4, h * P:(h + 1) * P]
        bc = [tmpf[:, 0, 0:nt], tmpf[:, 1, 0:nt]]
        n = len(sources)
        for d in range(2):
            mm(bank[6 + d][:, 0:nt], sel, MC[:, d, q0:q0 + nt], True, True, after=[act.last], done=True)
            act(s_.copy, bc[d], bank[6 + d][:, 0:nt], after=[pe.last])
        shared["bc_read"] = act.last
        t_s, t_e, s_read, w_read = {}, {}, {}, {}

        def span(ji, d):
            rel = sources[ji][1]
            return (0, nt) if rel is None else ((rel * P, nt) if d == 0 else (0, (rel + 1) * P))

        def ahead(ji):
            j, rel = sources[ji]
            t_s[ji] = mm(bank[4 + ji % 2][:, 0:nt], QK[:, 4 + h, j * P:(j + 1) * P], QK[:, h, q0:q0 + nt], True, True,
                         after=[s_read.get(ji - 2, shared.get("den_read"))], done=True)
            for d in range(2):
                lo, hi_ = span(ji, d)
                t_e[ji, d] = act(s_.activation, WT[:, ji % 2, d, lo:hi_], bc[d][:, lo:hi_], ACT.Exp,
                                 bias=GS[:, j, d, h:h + 1], after=w_read.get((ji - 2, d), ()))
        ahead(0)
        ahead(1)
        yield
        for ji, (j, rel) in enumerate(sources):
            first, last = ji == 0, ji == n - 1
            for d in range(2):
                lo, hi_ = span(ji, d)
                W = WT[:, ji % 2, d]
                if rel is not None:
                    wd = W[:, rel * P:(rel + 1) * P]
                    dve(v.scalar_tensor_tensor, wd, wd, 1.0, k_("upper_eq" if d == 0 else "lower_eq"),
                        ALU.min, ALU.mult, after=[t_e[ji, d]])
                dve(v.tensor_tensor, W[:, lo:hi_], W[:, lo:hi_], bank[4 + ji % 2][:, lo:hi_], ALU.mult,
                    after=[t_e[ji, d], t_s[ji]])
                s_read[ji] = dve.last
                if ji < 2 and hi_ - lo < nt:
                    z0, z1 = (hi_, nt) if lo == 0 else (0, lo)
                    dve(v.memset, W[:, z0:z1], 0.0)
                    lo, hi_ = 0, nt
                t_m = mm(bank[2 * x + d][:, lo:hi_], VN[:, j, h * P:(h + 1) * P], W[:, lo:hi_], first, last,
                         after=[dve.last], done=True)
                if ji == 1:
                    dve(v.tensor_tensor, WS[:, d, 0:nt], WT[:, 0, d, 0:nt], W[:, 0:nt], ALU.add,
                        after=[shared.get("ws_read")])
                elif ji > 1:
                    dve(v.tensor_tensor, WS[:, d, lo:hi_], WS[:, d, lo:hi_], W[:, lo:hi_], ALU.add)
                w_read[ji, d] = (t_m, dve.last)
                if ji == 1:
                    w_read[0, d] = (t_m, dve.last)
            if 0 < ji < n - 1:
                ahead(ji + 1)
            yield

    def mlstm_tail(h, q0, nt, x, shared):
        y = HA[:, 0:nt]
        shared["den_read"] = None
        for d in range(2):
            fl, den = tmpf[:, 2 + d, 0:nt], bank[4 + d][:, 0:nt]
            dve(v.scalar_tensor_tensor, fl, den, -1.0, fl, ALU.mult, ALU.max)
            dve(v.tensor_tensor, fl, fl, den, ALU.max)
        shared["den_read"] = dve.last
        yield
        for d in range(2):
            fl = tmpf[:, 2 + d, 0:nt]
            dve(v.reciprocal, fl, fl)
            dve(v.tensor_tensor, y if d == 0 else fl, fl, bank[2 * x + d][:, 0:nt], ALU.mult)
            yield
        dve(v.tensor_tensor, y, y, tmpf[:, 3, 0:nt], ALU.add)
        mm(bank[6][:, 0:nt], ones[:], y, True, True, after=[dve.last, shared.get("bc_read")], done=True)
        yield
        dve(v.scalar_tensor_tensor, y, bank[6][:, 0:nt], -1.0 / P, y, ALU.mult, ALU.add, after=[pe.last])
        sq2 = tmpf[:, 2, 0:nt]
        act(s_.activation, sq2, y, ACT.Square, after=[dve.last])
        mm(bank[7][:, 0:nt], ones[:], sq2, True, True, after=[act.last], done=True)
        yield
        rstd(sq2, bank[7][:, 0:nt], pe.last, P, eps_col)
        yield
        dve(v.tensor_tensor, y, y, sq2, ALU.mult, after=[act.last])
        dve(v.scalar_tensor_tensor, y, y, c2("g_mlstm")[:, h:h + 1], SO[:, h, q0:q0 + nt], ALU.mult, ALU.mult)
        yield
        split_store(HH[:, h, q0:q0 + nt], HL[:, h, q0:q0 + nt], y)
        yield

    def mlstm(ctx):
        pe.wait(act.last, dve.last)
        act.wait(dve.last)
        shared, tail = {}, None
        x_sources = [(0, None), (1, None)] + [(2 + r, r) for r in range(4)]
        jobs = []
        for h in range(MH):
            jobs.append((h, TC, T, x_sources))
            if ctx:
                jobs.append((h, 0, TC, [(0, 0), (1, 1)]))
        for i, (h, q0, nt, sources) in enumerate(jobs):
            main = mlstm_main(h, q0, nt, sources, i % 2, shared)
            prog.interleave(*([tail] if tail else []), main)
            sel = k_("sel")[0:4, h * P:(h + 1) * P]
            for d in range(2):
                mm(bank[6 + d][:, 0:nt], sel, GI[:, 2 + d, q0:q0 + nt], True, True, after=[dve.last, act.last],
                   done=True)
                act(s_.activation, tmpf[:, 2 + d, 0:nt], bank[6 + d][:, 0:nt], ACT.Exp, after=[pe.last])
            for d in range(2):
                mm(bank[4 + d][:, 0:nt], ones[:], WS[:, d, 0:nt], True, True, after=[dve.last], done=True)
            shared["ws_read"] = pe.last
            dve.wait(pe.last, act.last)
            tail = mlstm_tail(h, q0, nt, i % 2, shared)
        prog.interleave(tail)

    def post_norm_add(l, segs, g, row):
        def chain(stream, t0, nt, bk, buf):
            gg = small[:, 16 + 8 * stream:24 + 8 * stream]
            dve(v.tensor_tensor, gg, g, m2(l, stream, row), ALU.mult)
            yield from norm_sum(lambda k: OUT[:, k, t0:t0 + nt], nt, bk, buf)
            r = buf[2][:, 0:nt]
            t = rstd(r, bank[bk][:, 0:nt], pe.last, D, eps_col, inc=bank_free[bk])
            for k in range(KD):
                o = OUT[:, k, t0:t0 + nt]
                dve(v.scalar_tensor_tensor, o, o, gg[:, k:k + 1], r, ALU.mult, ALU.mult, after=[t])
                dve(v.tensor_tensor, XC[:, k, t0:t0 + nt], XC[:, k, t0:t0 + nt], o, ALU.add)
                yield
        prog.interleave(*[chain(*seg, bk, buf) for seg, bk, buf in zip(segs, (4, 5), (NORM_X, NORM_C))])

    def mod_norm(l, segs, g, row):
        items = []
        for stream, t0, nt in segs:
            gs = small[:, 8 * stream:8 * stream + 8]
            dve(v.tensor_scalar, gs, m2(l, stream, row + 1), 1.0, None, ALU.add)
            dve(v.tensor_tensor, gs, gs, g, ALU.mult)
            items.append((t0, t0, nt, gs, m2(l, stream, row)))
        norm_mod(HH, HL, items)

    def out_evict(n, first):
        def go(ps, t, free):
            for j, (t0, nt) in enumerate([(TC, T), (0, TC)][:len(ps)]):
                inc = free if j == len(ps) - 1 else None
                o = OUT[:, ds(n, 1), t0:t0 + nt].rearrange("p a n -> p (a n)")
                if first:
                    dve(v.tensor_copy, o, ps[j], after=[t], inc=inc)
                else:
                    dve(v.tensor_tensor, o, o, ps[j], ALU.add, after=[t], inc=inc)
        return go

    def mlp(l, ctx, final):
        both = XB if ctx else X0
        for c in range(4):
            pe.wait(dve.last)
            with prog.loop(f"mlp{l}_in{c}", 2) as i:
                for q in range(4):
                    def ev(ps, t, free, q=q):
                        for j, (t0, nt) in enumerate([(TC, T), (0, TC)][:len(ps)]):
                            y = tmpf[:, q % 2 + 2 * j, 0:nt]
                            hi, lo = (g[:, ds(i * 4 + q, 1), t0:t0 + nt].rearrange("p a n -> p (a n)")
                                      for g in (GH, GL))
                            act(s_.activation, y, ps[j], ACT.Relu, after=[t])
                            dve(v.tensor_tensor, y, y, ps[j], ALU.mult, after=[act.last])
                            split_store(hi, lo, y, inc=free if j == len(ps) - 1 else None)
                    unit(w_mlp1[l][:, :, ds((i * 4 + (q + 8 * c)) * P, P)], KD, both, HH, HL, ev)
            pe.wait(*[b.now() for b in bank_free[0:4]])
            with prog.loop(f"mlp{l}_out{c}", 2) as i:
                for q in range(4):
                    unit(w_mlp2[l][:, 8 * c:8 * c + 8, ds((i * 4 + q) * P, P)], KD, both, GH, GL,
                         out_evict(i * 4 + q, c == 0))
        if final:
            for _ in range(AHEAD):
                load(a["const"][:, 0:KD * P].rearrange("p (k n) -> p k n", k=KD))
                state["n"] += 1

    def block2(l):
        ctx = l < DEPTH - 1
        segs = [(0, TC, T), (1, 0, TC)]
        kept = segs if ctx else segs[:1]
        dve(v.tensor_copy, cols2[:], cols2_all[:, l * NC2:(l + 1) * NC2])
        mod_norm(l, segs, c2("g_pre_mix"), 0)
        prog.barrier()
        project(l, ctx)
        prog.barrier()
        prog.interleave(fourier(ctx), conv31_finish(ctx))
        prog.barrier()
        gates()
        prog.barrier()
        mlstm(ctx)
        prog.barrier()
        pe.wait(dve.last)
        with prog.loop(f"out{l}", 2) as i:
            for q in range(4):
                unit(w_out2[l][:, :, ds((i * 4 + q) * P, P)], KD, XB if ctx else X0, HH, HL,
                     out_evict(i * 4 + q, True))
        prog.barrier()
        post_norm_add(l, kept, c2("g_post_mix"), 2)
        mod_norm(l, kept, c2("g_pre_mlp"), 3)
        prog.barrier()
        mlp(l, ctx, not ctx)
        prog.barrier()
        post_norm_add(l, kept, c2("g_post_mlp"), 5)
        prog.barrier()

    t_pos = prog.dma(act, POS[:], a["posT"], in_table)
    dve(v.tensor_tensor, XC[:, :, TC:TT], XC[:, :, TC:TT], POS[:], ALU.add, after=[t_pos])
    prog.barrier()
    for l in range(DEPTH):
        block2(l)
    prog.dma(sp, a["outT"], XC[:, :, TC:TT], out_done, after=[dve.last])
    sp.wait(out_done.now())
    return prog.recorded


def _columns(parts, table, total):
    out = np.zeros((DEPTH, P, total), np.float32)
    for name, (o, w) in table.items():
        out[:, :, o:o + w] = parts[name]
    return np.ascontiguousarray(out.transpose(1, 0, 2).reshape(P, DEPTH * total))


def _vec(x):
    x = np.asarray(x).reshape(DEPTH, -1, P)
    return x.transpose(0, 2, 1)


def _taps(x):
    x = np.asarray(x)
    k = x.shape[1]
    return x.reshape(DEPTH, k, -1, P).transpose(0, 3, 2, 1).reshape(DEPTH, P, -1)


def _shape_constants():
    p, f = np.arange(P)[:, None], np.arange(P)[None, :]
    out = np.zeros((P, NCONST), np.float32)

    def put(name, x):
        o, w = CONST[name]
        out[:x.shape[0], o:o + w] = x

    put("ident", (p == f).astype(np.float32))
    put("blk", (p // HD == f // HD).astype(np.float32))
    q, k = np.arange(P)[:, None], np.arange(2 * P)[None, :] - P
    open_ = (q - k >= 0) & (q - k < P)
    put("attmask", np.concatenate([np.where(open_ & (k >= 0), 0, -1e30), np.where(open_, 0, -1e30)], 1))
    levels = []
    for j in range(RW_LEVELS):
        w = 1 << j
        same = (p // (2 * w)) == (f // (2 * w))
        levels.append(-(same & (p // w % 2 == 1) & (f // w % 2 == 0)).astype(np.float32))
    put("levels", np.concatenate(levels, 1))
    put("level0T", levels[0].T)
    put("upper", (p < f).astype(np.float32))
    put("upper_eq", (p <= f).astype(np.float32))
    put("lower_eq", (p >= f).astype(np.float32))
    ang = 2 * np.pi * ((p % HD) * (f % HD) % HD) / HD
    same = p // HD == f // HD
    put("c64", np.where(same, np.cos(ang), 0))
    put("s64", np.where(same, -np.sin(ang), 0))
    sel = np.zeros((4, 4, P), np.float32)
    for h in range(4):
        sel[h, h] = -1
    put("sel", sel.reshape(4, -1))
    return out


def _dft(n):
    i = np.arange(n)
    ang = 2 * np.pi * (i[:, None] * i[None, :] % n) / n
    scale = 1 / np.sqrt(n * 64)
    lay = lambda x: np.ascontiguousarray((x * scale).astype(np.float32).reshape(n // P, P, n).transpose(1, 0, 2))
    return lay(np.cos(ang)), lay(np.sin(ang))


def _positions():
    quarter = D // 4
    f32 = np.float32
    freq = np.exp(f32(-np.log(10000.0)) * np.arange(quarter, dtype=f32) / f32(quarter))
    r = np.repeat(np.arange(T // 64, dtype=f32), 64)[:, None] * freq
    c = np.tile(np.arange(64, dtype=f32), T // 64)[:, None] * freq
    pos = np.concatenate([np.sin(r), np.cos(r), np.sin(c), np.cos(c)], -1).astype(f32)
    return _transposed(pos)


def _transposed(x):
    return np.ascontiguousarray(x.T.reshape(KD, P, -1).transpose(1, 0, 2))


def host_arrays(i):
    i = {k: np.asarray(x) for k, x in i.items()}
    const = _shape_constants()
    o, w = CONST["cc"]
    for j, n in enumerate(("c", "c_2", "c_ctx_2")):
        const[:, o + 8 * j:o + 8 * j + 8] = i[n].reshape(KD, P).T
    twice = lambda x: np.concatenate([x, x], 1)[:, :, None]
    cols1 = _columns({
        "b_ada": _vec(i["b_ada"]), "g_ffn1": _vec(i["g_ffn1"]), "g_mix": _vec(i["g_mix"]),
        "g_ffn2": _vec(i["g_ffn2"]), "q_gain": twice(i["att_q_gain"]), "k_gain": twice(i["att_k_gain"]),
        "sinks": np.broadcast_to(i["att_sinks"][:, None, :], (DEPTH, P, QH)), "mu": _vec(i["rwkv_mu"]),
        "w0": _vec(i["rwkv_w0"]), "a0": _vec(i["rwkv_a0"]), "k_k": _vec(i["rwkv_k_k"]), "k_a": _vec(i["rwkv_k_a"]),
        "r_k": _vec(i["rwkv_r_k"]), "gn_w": _vec(i["rwkv_gn_w"]), "gn_b": _vec(i["rwkv_gn_b"]),
        "conv": _taps(i["conv_w"])}, COLS1, NC1)
    bg = np.zeros((DEPTH, P, 1), np.float32)
    bg[:, :16, 0] = i["b_gate_2"].reshape(DEPTH, 16)
    cols2 = _columns({
        "b_ada": _vec(i["b_ada_2"]), "g_pre_mix": _vec(i["g_pre_mix_2"]), "g_post_mix": _vec(i["g_post_mix_2"]),
        "g_pre_mlp": _vec(i["g_pre_mlp_2"]), "g_post_mlp": _vec(i["g_post_mlp_2"]),
        "qk_conv": _taps(i["w_qk_conv_2"]), "g_mlstm": _vec(i["g_mlstm_norm_2"]), "w_dw": _taps(i["w_dw_2"]),
        "b_dw": _vec(i["b_dw_2"]), "g_ln": _vec(i["g_conv_ln_2"]), "b_ln": _vec(i["b_conv_ln_2"]),
        "b_gate": bg}, COLS2, NC2)
    lora = np.zeros((DEPTH, P, 2, 256), np.float32)
    lora[:, 0:64, 0] = i["rwkv_w_w2"]
    lora[:, 64:128, 0] = i["rwkv_a_w2"]
    lora[:, :, 1] = i["rwkv_g_w2"]
    dc, dsn = _dft(T)
    cc, cs = _dft(TC)
    arrays = {"const": const, "cols1": cols1, "cols2": cols2, "lora": lora, "xT": _transposed(i["x"][0]),
              "ctxT": _transposed(i["ctx_2"][0]), "posT": _positions(), "dft_cos": dc, "dft_sin": dsn,
              "dftc_cos": cc, "dftc_sin": cs}
    for n in ("w_ada", "w_ffn1_in", "w_ffn1_out", "w_ffn2_in", "w_ffn2_out", "w_mix_in", "w_mix_out", "w_ada_2",
              "w_in_2", "w_out_2", "w_mlp1_2", "w_mlp2_2"):
        arrays[n] = np.ascontiguousarray(i[n])
    return arrays


def kernel(**inputs):
    import concourse.bacc as _bacc
    from concourse.bass_utils import run_bass_kernel_spmd as _run
    arrays = host_arrays(inputs)
    per_loop = {}
    for _ in range(2):
        nc = _bacc.Bacc("TRN2", target_bir_lowering=False, num_devices=1)
        a = {n: nc.dram_tensor("in_" + n, x.shape, F32, kind="ExternalInput").ap() for n, x in arrays.items()}
        a["outT"] = nc.dram_tensor("outT", (P, KD, T), F32, kind="ExternalOutput").ap()
        per_loop = build(nc, a, per_loop)
    r = _run(nc, [{"in_" + n: x for n, x in arrays.items()}], core_ids=[0])
    out = r.results[0]["outT"]
    return np.ascontiguousarray(out.transpose(1, 0, 2).reshape(D, T).T)[None]
```

```python
from contextlib import ExitStack, contextmanager

import numpy as np
import concourse.bass as bass
from concourse import mybir

F32 = mybir.dt.float32
F32R = mybir.dt.float32r
ALU = mybir.AluOpType
ACT = mybir.ActivationFunctionType
AX = mybir.AxisListType
ds = bass.ds

P = 128
D = 1024
T = 512
TC = 256
TT = TC + T
KD = D // P
DEPTH = 2
EPS = 1e-6
D_FF = 2816
FT = D_FF // P
PROJ1 = 2560
NP1 = PROJ1 // P
HD = 64
QH = 8
GN_EPS = 64e-5
DECAY_SCALE = float(np.exp(-0.5))
D_FF2 = 4096
MH = 4
G_OFF = 2048
F_OFF = 2064
C_OFF = F_OFF + 256
K2 = 31
BASE = 16
SLOTS = 4
AHEAD = 2
DEBUG = False

COLS1 = {}
COLS2 = {}


def _layout(table, items):
    at = 0
    for name, n in items:
        table[name] = (at, n)
        at += n
    return at


NC1 = _layout(COLS1, [("b_ada", 72), ("g_ffn1", 8), ("g_mix", 8), ("g_ffn2", 8), ("q_gain", 1), ("k_gain", 1),
                      ("sinks", 8), ("mu", 8), ("w0", 2), ("a0", 2), ("k_k", 2), ("k_a", 2), ("r_k", 2),
                      ("gn_w", 2), ("gn_b", 2), ("conv", 6)])
NC2 = _layout(COLS2, [("b_ada", 48), ("g_pre_mix", 8), ("g_post_mix", 8), ("g_pre_mlp", 8), ("g_post_mlp", 8),
                      ("qk_conv", 24), ("g_mlstm", 4), ("w_dw", 62), ("b_dw", 2), ("g_ln", 2), ("b_ln", 2),
                      ("b_gate", 1)])
CONST = {}
NCONST = _layout(CONST, [("ident", 128), ("blk", 128), ("attmask", 512), ("levels", 7 * 128), ("level0T", 128),
                         ("upper", 128), ("upper_eq", 128), ("lower_eq", 128), ("c64", 128), ("s64", 128),
                         ("sel", 512), ("cc", 24)])
RW_LEVELS = 7


class Counter:

    def __init__(self, sem, name, base):
        self.sem, self.name, self.const, self.terms = sem, name, base, []

    def now(self, more=0):
        return (self, self.const + more, tuple(self.terms))


class Queue:

    def __init__(self, eng, progress, chained):
        self.eng, self.progress, self.chained = eng, progress, chained
        self.last = None
        self.latest = None
        self.seen = {}

    def wait(self, *tokens):
        for t in tokens:
            if t is None:
                continue
            counter, const, terms = t
            key = (counter.name, tuple(id(i) for i, _ in terms))
            if self.seen.get(key, 0) >= const:
                continue
            self.seen[key] = const
            value = const
            for i, k in terms:
                if k:
                    value = i * k + value
            self.eng.wait_ge(counter.sem, value)

    def __call__(self, fn, *args, after=(), inc=None, **kw):
        self.wait(*after)
        if self.chained:
            self.wait(self.last)
        counter = inc or self.progress
        fn(*args, **kw).then_inc(counter.sem, 1)
        counter.const += 1
        self.last = self.latest = counter.now()
        return self.last


def delayed(chain, steps):
    for _ in range(steps):
        yield
    yield from chain


class Program:
    def __init__(self, nc, per_loop):
        self.nc = nc
        self.per_loop = per_loop
        self.recorded = {}
        self.counters = []
        self.pe = Queue(nc.tensor, self.counter("pe"), False)
        self.act = Queue(nc.scalar, self.counter("act"), True)
        self.dve = Queue(nc.vector, self.counter("dve"), True)
        self.pool = Queue(nc.gpsimd, self.counter("pool"), True)
        self.sp = Queue(nc.sync, self.counter("sp"), False)
        self.queues = [self.pe, self.act, self.dve, self.pool, self.sp]
        self.entered = nc.alloc_semaphore("s_entered")

    def counter(self, name, base=BASE):
        c = Counter(self.nc.alloc_semaphore("s_" + name), name, base)
        if base:
            self.nc.sync.sem_inc(c.sem, base)
        self.counters.append(c)
        return c

    def mm(self, out, lhsT, rhs, start, stop, after=(), inc=None, done=False):
        self.pe.wait(*after)
        ins = self.nc.tensor.matmul(out, lhsT, rhs, start=start, stop=stop)
        return self._pe_done(ins, inc, done)

    def transpose(self, out, in_, ident, after=(), inc=None, done=False):
        self.pe.wait(*after)
        return self._pe_done(self.nc.tensor.transpose(out, in_, ident), inc, done)

    def _pe_done(self, ins, inc, done):
        if inc is None and not done:
            return None
        counter = inc or self.pe.progress
        ins.then_inc(counter.sem, 1)
        counter.const += 1
        self.pe.last = self.pe.latest = counter.now()
        return self.pe.last

    def dma(self, queue, out, in_, counter, after=()):
        queue.wait(*after)
        queue.eng.dma_start(out, in_).then_inc(counter.sem, 16)
        counter.const += 16
        return counter.now()

    def by_half(self, heads, one_head):
        for half in range(2):
            mine = [h for h in heads if h % 2 == half]
            for h in mine:
                one_head(h, h == mine[-1])
            self.pe.wait(self.pe.last)
        return self.pe.last

    def interleave(self, *chains):
        last = {c: {q: q.last for q in self.queues} for c in chains}
        live = list(chains)
        while live:
            for c in list(live):
                for q in self.queues:
                    q.last = last[c][q]
                if next(c, self) is self:
                    live.remove(c)
                last[c] = {q: q.last for q in self.queues}
        for q in self.queues:
            q.last = q.latest

    def barrier(self):
        work = [self.pe, self.act, self.dve, self.pool]
        for q in work:
            for other in work:
                if other is not q:
                    q.wait(other.last)

    @contextmanager
    def loop(self, name, n):
        for q in self.queues:
            if q.chained:
                q.wait(q.last)
            q.seen = {}
        outside = {q: q.last for q in self.queues}
        for q in self.queues:
            q.last = None
        for q in (self.pe, self.dve, self.pool):
            q.eng.sem_inc(self.entered, 1)
        start = {c: c.const for c in self.counters}
        per = self.per_loop.get(name, {})
        with self.nc.Fori(0, n) as i:
            for c in self.counters:
                c.terms.append((i, per.get(c.name, 0)))
            yield i
            for q in self.queues:
                if q.chained:
                    q.wait(q.last)
            for c in self.counters:
                c.terms.pop()
        self.recorded[name] = {c.name: c.const - start[c] for c in self.counters}
        for c in self.counters:
            c.const = start[c] + n * (c.const - start[c])
        for q in self.queues:
            q.seen = {}
            q.last = q.latest = q.last[0].now() if q.last else outside[q]


def build(nc, a, per_loop):
    prog = Program(nc, per_loop)
    pe, act, dve, pool, sp = prog.pe, prog.act, prog.dve, prog.pool, prog.sp
    mm = prog.mm
    v, s_, g_ = nc.vector, nc.scalar, nc.gpsimd

    top = [(nc.sbuf_base + 63) // 64 * 64]

    def fixed(name, shape, dt=F32):
        off = top[0]
        top[0] += (int(np.prod(shape[1:])) * 4 + 31) // 32 * 32
        return nc.alloc_sbuf_tensor_at(name, list(shape), dt, offset=off)

    const = fixed("const", [P, NCONST])
    ones = fixed("ones", [P, P])
    cols1_all = fixed("cols1_all", [P, DEPTH * NC1])
    cols2_all = fixed("cols2_all", [P, DEPTH * NC2])
    cols1 = fixed("cols1", [P, NC1])
    cols2 = fixed("cols2", [P, NC2])
    mod1 = fixed("mod1", [P, 72])
    mod2 = fixed("mod2", [P, DEPTH * 2 * 48])
    small = fixed("small", [P, 96])
    csil = fixed("csil", [P, 3, 8])
    csig = fixed("csig", [P, 3, 8])
    lora = fixed("lora", [P, 2, 256])
    XC = fixed("XC", [P, KD, TT])
    stage_at = top[0]
    stage = fixed("stage", [P, SLOTS, 8, P])
    WL = nc.alloc_sbuf_tensor_at("WL", [P, SLOTS, 8, P], F32R, offset=stage_at)
    WH = fixed("WH", [P, SLOTS, 8, P], F32R)
    tmpf_at = top[0]
    tmpf = fixed("tmpf", [P, 4, T])
    R0 = top[0]
    RN = (nc.sbuf_usable_end - R0) // 32 * 8
    print("RN", RN, "free after G0", RN - 2 * KD * TT) if DEBUG else None
    used = set()

    def region(name, off, shape, dt=F32):
        assert off + int(np.prod(shape[1:])) <= RN, (name, off, shape, RN)
        assert name not in used
        used.add(name)
        return nc.alloc_sbuf_tensor_at(name, list(shape), dt, offset=R0 + 4 * off)

    HH = region("HH", 0, [P, KD, TT], F32R)
    HL = region("HL", KD * TT, [P, KD, TT], F32R)
    G0 = 2 * KD * TT
    H1H = region("H1H", 0, [P, KD, T], F32R)
    H1L = region("H1L", KD * TT, [P, KD, T], F32R)
    GH = region("GH", G0, [P, 8, TT], F32R)
    GL = region("GL", G0 + 8 * TT, [P, 8, TT], F32R)
    ADA0 = RN - 2 * 2048 - 512
    ada_w = region("ada_w", ADA0, [P, 2, 8, 256])
    ada_acc = region("ada_acc", ADA0 + 4096, [P, 2, 256])
    bank = [nc.alloc_psum_tensor(f"bank{j}", [P, 512], F32) for j in range(8)]

    def k_(name, n=None):
        o, w = CONST[name]
        return const[:, o:o + (n or w)]

    ident, blk = k_("ident"), k_("blk")

    stage_full = [prog.counter(f"stage_full{i}") for i in range(SLOTS)]
    split_done = [prog.counter(f"split_done{i}") for i in range(SLOTS)]
    unit_done = [prog.counter(f"unit_done{i}") for i in range(SLOTS)]
    bank_free = [prog.counter(f"bank_free{i}") for i in range(8)]
    ada_full = [prog.counter(f"ada_full{i}", 0) for i in range(2)]
    ada_ready = [prog.counter(f"ada_ready{i}") for i in range(2)]
    in_lora = prog.counter("in_lora")
    in_table = prog.counter("in_table")
    gates_in = prog.counter("gates_in")
    out_done = prog.counter("out_done")
    in_misc = prog.counter("in_misc")

    prog.dma(act, const[:], a["const"], in_misc)
    prog.dma(act, cols1_all[:], a["cols1"], in_misc)
    prog.dma(act, cols2_all[:], a["cols2"], in_misc)
    t_const = in_misc.now()
    in_x = prog.counter("in_x")
    prog.dma(act, XC[:, :, TC:TT], a["xT"], in_x)
    t_x = prog.dma(act, XC[:, :, 0:TC], a["ctxT"], in_x)
    dve(v.memset, ones[:], 1.0)
    one_row = ones[:, 0:1]
    eps_col, gn_eps_col = small[:, 46:47], small[:, 47:48]
    dve(v.memset, eps_col, EPS)
    dve(v.memset, gn_eps_col, GN_EPS)

    cc = k_("cc").rearrange("p (a k) -> p a k", a=3)
    act(s_.activation, csig[:], cc, ACT.Sigmoid, after=[t_const])
    t_csil = dve(v.tensor_tensor, csil[:], cc, csig[:], ALU.mult, after=[act.last, t_const])

    state = {"n": 0, "split": 0, "ada": 0}

    def split_next():
        st = state["split"] % SLOTS
        state["split"] += 1
        t = act(s_.copy, WH[:, st], stage[:, st], after=[stage_full[st].now(16)])
        dve(v.tensor_tensor, WL[:, st], stage[:, st], WH[:, st].bitcast(F32), ALU.subtract,
            after=[t, stage_full[st].now(16)], inc=split_done[st])

    def load(src):
        st = state["n"] % SLOTS
        prog.dma(sp, stage[:, st], src, stage_full[st], after=[unit_done[st].now()])
        return st

    def unit(src, kt, segs, hi, lo, evict, ada=None, ready=None):
        s = load(src)
        split_next()
        if ada and ada[0] == "begin":
            ada_begin(*ada[1:])
        outs = []
        pe.wait(split_done[s].now(), bank_free[s].now())
        for gi, (bo, t0, nt) in enumerate(segs):
            ps = bank[s + bo][:, 0:nt]
            for k in range(kt):
                if ready:
                    pe.wait(*ready[gi][k])
                passes = [(WH, hi), (WH, lo), (WL, hi)]
                for pi, (w, x) in enumerate(passes):
                    lastmm = k == kt - 1 and pi == 2
                    end = lastmm and gi == len(segs) - 1
                    mm(ps, w[:, s, KD - kt + k, :], x[:, k, t0:t0 + nt], k == 0 and pi == 0, lastmm,
                       inc=unit_done[s] if end else None)
            outs.append(ps)
        evict(outs, pe.last, bank_free[s])
        if ada and ada[0] == "finish":
            ada_finish(*ada[1:])
        state["n"] += 1

    def ada_begin(src, streams, *_):
        x = state["ada"] % 2
        state["ada"] += 1
        t = prog.dma(pool, ada_w[:, x], src, ada_full[x], after=[ada_ready[x].now()])
        for j, c in enumerate(streams):
            for k in range(KD):
                end = k == KD - 1 and j == len(streams) - 1
                inc = ada_ready[x] if end else None
                if k == 0:
                    dve(v.tensor_scalar, ada_acc[:, j], ada_w[:, x, 0], csil[:, c, 0:1], None, ALU.mult,
                        after=[t, t_csil], inc=inc)
                else:
                    dve(v.scalar_tensor_tensor, ada_acc[:, j], ada_w[:, x, k], csil[:, c, k:k + 1], ada_acc[:, j],
                        ALU.mult, ALU.add, inc=inc)

    def ada_finish(src, streams, out, bias):
        pe.wait(ada_ready[(state["ada"] - 1) % 2].now(), bank_free[7].now())
        for j in range(len(streams)):
            for h in range(2):
                mm(bank[7][:, 2 * j + h:2 * j + h + 1], ada_acc[:, j, h * P:(h + 1) * P], one_row, True, True,
                   done=(j == len(streams) - 1 and h == 1))
        t = pe.last
        for j in range(len(streams)):
            dve(v.tensor_tensor, out[j], bank[7][:, 2 * j:2 * j + 2], bias, ALU.add, after=[t],
                inc=bank_free[7] if j == len(streams) - 1 else None)

    wada1 = a["w_ada"].rearrange("l (k p) n -> l p k n", p=P)
    wada2 = a["w_ada_2"].rearrange("l (k p) n -> l p k n", p=P)

    def ada1(l, u):
        bias = cols1_all[:, ds(u * 2 + (l * NC1 + COLS1["b_ada"][0]), 2)]
        return wada1[l][:, :, ds(u * 256, 256)], (0,), [mod1[:, ds(u * 2, 2)]], bias

    def ada2(l, u):
        bias = cols2_all[:, ds(u * 2 + (l * NC2 + COLS2["b_ada"][0]), 2)]
        return (wada2[l][:, :, ds(u * 256, 256)], (1, 2),
                [mod2[:, ds(u * 2 + (l * 96 + 48 * j), 2)] for j in range(2)], bias)

    sq = tmpf

    NORM_X = [tmpf[:, 0, :], tmpf[:, 1, :], tmpf[:, 3, :]]
    c_buf = tmpf[:, 2, 0:TC]
    NORM_C = [c_buf, c_buf, tmpf[:, 2, TC:2 * TC]]

    def norm_sum(src_of, nt, bk, buf):
        act.wait(dve.last)
        even, odd = (buf[0], buf[2] if buf[0] is not buf[1] else buf[0]), buf[1] if buf[0] is not buf[1] else buf[2]
        read, before = {}, pe.last
        for k in range(0, KD, 2):
            x, y = even[k // 2 % 2][:, 0:nt], odd[:, 0:nt]
            act(s_.activation, x, src_of(k), ACT.Square,
                after=[read.get(k - (4 if even[0] is not even[1] else 2), before)])
            t = act(s_.activation, y, src_of(k + 1), ACT.Square, after=[read.get("odd", before)])
            read["odd"] = dve(v.tensor_tensor, x, x, y, ALU.add, after=[t])
            if k == 0:
                pe.wait(bank_free[bk].now())
            read[k] = mm(bank[bk][:, 0:nt], ones[:], x, k == 0, k == KD - 2, after=[dve.last], done=True)
            yield

    def rstd(out, ps, after, n_mean, eps, inc=None):
        act(s_.activation, out, ps, ACT.Ln, scale=1.0 / n_mean, bias=eps, after=[after, dve.last], inc=inc)
        return act(s_.activation, out, out, ACT.Exp, scale=-0.5)

    def split_store(hi, lo, exact, after=(), inc=None):
        t = act(s_.copy, hi, exact, after=[*after, dve.last])
        return dve(v.tensor_tensor, lo, exact, hi.bitcast(F32), ALU.subtract, after=[t], inc=inc)

    SS = [tmpf[:, 2, :], tmpf[:, 3, 0:TC]]
    SQ = [tmpf[:, 0, :], tmpf[:, 1, 0:TC]]

    def clear_sums(n=1):
        for y in SS[:n]:
            dve(v.memset, y, 0.0)

    def gather(j, tile):
        act(s_.activation, SQ[j], tile, ACT.Square, after=[dve.last])
        dve(v.tensor_tensor, SS[j], SS[j], SQ[j], ALU.add, after=[act.last])

    def sum_gathered(j, nt, bk):
        mm(bank[bk][:, 0:nt], ones[:], SS[j], True, True, after=[dve.last, bank_free[bk].now()], done=True)

    def norm_chain(ready, hi, lo, t0, h0, nt, g, shift, bk, buf, gathered=False):
        if gathered:
            sum_gathered(0, nt, bk)
            yield
        else:
            yield from norm_sum(lambda k: XC[:, k, t0:t0 + nt], nt, bk, buf)
        r = buf[2][:, 0:nt]
        t = rstd(r, bank[bk][:, 0:nt], pe.last, D, eps_col, inc=bank_free[bk])
        ahead = 0 if buf[0] is buf[1] else 1
        t_y = []
        for k in range(KD):
            y = buf[k % 2][:, 0:nt]
            while len(t_y) < min(k + ahead + 1, KD):
                i = len(t_y)
                t_y.append(dve(v.tensor_tensor, buf[i % 2][:, 0:nt], XC[:, i, t0:t0 + nt], r, ALU.mult,
                               after=[t, pe.last]))
            act(s_.activation, y, y, ACT.Identity, scale=g[:, k:k + 1], bias=shift[:, k:k + 1], after=[t_y[k]])
            hi_k = hi[:, k, h0:h0 + nt]
            act(s_.copy, hi_k, y)
            ready.append([dve(v.tensor_tensor, lo[:, k, h0:h0 + nt], y, hi_k.bitcast(F32), ALU.subtract,
                              after=[act.last])])
            yield

    def norm_mod(hi, lo, segs, gathered=False):
        ready = [[] for _ in segs]
        prog.interleave(*[norm_chain(rd, hi, lo, *seg, bk, buf, gathered)
                          for rd, seg, bk, buf in zip(ready, segs, (4, 5), (NORM_X, NORM_C))])
        return ready

    X1 = [(0, 0, T)]
    X0 = [(0, TC, T)]
    XB = [(0, TC, T), (4, 0, TC)]

    wf_in = [a[n].rearrange("l (k p) n -> l p k n", p=P) for n in ("w_ffn1_in", "w_ffn2_in")]
    wf_out = [a[n].rearrange("l (k p) n -> l p k n", p=P) for n in ("w_ffn1_out", "w_ffn2_out")]
    wmix_in = a["w_mix_in"].rearrange("l (k p) n -> l p k n", p=P)
    wmix_out = a["w_mix_out"].rearrange("l (k p) n -> l p k n", p=P)

    def c1(name):
        o, w = COLS1[name]
        return cols1[:, o:o + w]

    def c2(name):
        o, w = COLS2[name]
        return cols2[:, o:o + w]

    def evict_add(n, coef, last):
        def go(ps, t, free):
            xa = XC[:, ds(n, 1), TC:TT].rearrange("p a n -> p (a n)")
            dve(v.scalar_tensor_tensor, xa, ps[0], coef[:, ds(n, 1)], xa, ALU.mult, ALU.add, after=[t], inc=free)
            if last:
                gather(0, xa)
        return go

    def ffn(l, which, ready, ada_in, ada_out, after_first=None):
        w_in, w_out = wf_in[which][l], wf_out[which][l]
        coef = small[:, 8:16]
        for c, (j0, nj) in enumerate([(0, 8), (8, 8), (16, 6)]):
            with prog.loop(f"ffn{which}_in{c}", nj // 2) as i:
                for q in range(2):
                    col = (i * 2 + (j0 + q)) * P

                    def ev_gate(ps, t, free, q=q):
                        act(s_.activation, tmpf[:, q, :], ps[0], ACT.Silu, after=[t], inc=free)

                    def ev_up(ps, t, free, q=q):
                        y = tmpf[:, q, :]
                        dve(v.tensor_tensor, y, y, ps[0], ALU.mult, after=[t, act.last])
                        hi = GH[:, ds(i * 2 + q, 1), 0:T].rearrange("p a n -> p (a n)")
                        lo = GL[:, ds(i * 2 + q, 1), 0:T].rearrange("p a n -> p (a n)")
                        split_store(hi, lo, y, inc=free)

                    job = ada_in(c, i * 2 + q)
                    unit(w_in[:, :, ds(col, P)], KD, X1, H1H, H1L, ev_gate, ada=("begin", *job),
                         ready=ready if c == 0 and q == 0 else None)
                    unit(w_in[:, :, ds(col + D_FF, P)], KD, X1, H1H, H1L, ev_up, ada=("finish", *job))
            if c == 0 and after_first:
                after_first()
            made = [[bank_free[3].now(-1)]] * (nj - 2) + [[bank_free[1].now()], [bank_free[3].now()]]
            if c == 2:
                clear_sums()
            with prog.loop(f"ffn{which}_out{c}", 2) as i:
                for q in range(4):
                    job = ada_out(c, i, q // 2)
                    unit(w_out[:, j0 + nj - KD:j0 + nj, ds((i * 4 + q) * P, P)], nj, X1, GH, GL,
                         evict_add(i * 4 + q, coef, c == 2), ada=job and (("begin", "finish")[q % 2], *job),
                         ready=[made] if q == 0 else None)

    def stage_cols(g, i):
        sc = mod1[:, (i + 1) * 8:(i + 2) * 8]
        dve(v.tensor_scalar, small[:, 0:8], sc, 1.0, None, ALU.add)
        dve(v.tensor_tensor, small[:, 0:8], small[:, 0:8], g, ALU.mult)
        return mod1[:, i * 8:(i + 1) * 8]

    def stage_gate(i):
        gt = mod1[:, (i + 2) * 8:(i + 3) * 8]
        half = 1.0 if i == 3 else 0.5
        dve(v.tensor_scalar, small[:, 8:16], gt, half, half, ALU.mult, ALU.add)

    PJ = region("PJ", G0, [P, NP1, T + 2])
    S_FREE = G0 + NP1 * (T + 2)
    HT, LT = KD * T, KD * TT + KD * T
    kdup = region("kdup", S_FREE, [P, 2, P + T])
    vnat = region("vnat", S_FREE + 1280, [P, 5, P])
    att_s = region("att_s", S_FREE + 1920, [P, 4, 4, 256])
    att_pt3 = region("att_pt", S_FREE + 6016, [P, 3, 8, P])
    att_pt = [att_pt3[:, j] for j in range(3)] + [tmpf[:, 0:2, :].rearrange("p a (b n) -> p (a b) n", b=4)]
    att_y = [tmpf[:, 2 + j // 2, 256 * (j % 2):256 * (j % 2) + 256].rearrange("p (a n) -> p a n", a=2)
             for j in range(4)]
    kd_in = prog.counter("kd_in")

    def heads_rms(tiles):
        act.wait(dve.last, pe.last)
        buf = [tmpf[:, i, :] for i in range(4)] + [att_s[:, 0, 0:2].rearrange("p h n -> p (h n)")]
        t_b = []
        for i, (x, _) in enumerate(tiles):
            act(s_.activation, buf[i], x, ACT.Square)
            t_b.append(mm(bank[i][:], blk, buf[i], True, True, after=[act.last], done=True))
        for i in range(len(tiles)):
            act(s_.activation, buf[i], bank[i][:], ACT.Ln, scale=1.0 / HD, bias=eps_col, after=[t_b[i]])
        for i, (x, gain) in enumerate(tiles):
            act(s_.activation, buf[i], buf[i], ACT.Exp, scale=-0.5)
            dve(v.scalar_tensor_tensor, x, x, gain, buf[i], ALU.mult, ALU.mult, after=[act.last])

    def attention():
        heads_rms([(PJ[:, i, 2:2 + T], c1("q_gain") if i < 4 else c1("k_gain")) for i in (4, 0, 1, 2, 3)])
        dve(v.memset, kdup[:, :, 0:P], 0.0)
        dve(v.memset, vnat[:, 0, :], 0.0)
        for h in range(2):
            for half in range(2):
                t_kd = prog.dma(act, kdup[64 * half:64 * half + 64, h, P:P + T],
                                PJ[64 * h:64 * h + 64, 4, 2:2 + T], kd_in, after=[dve.last])
        for b in range(4):
            prog.transpose(bank[6][:, b * P:(b + 1) * P], PJ[:, 5, 2 + b * P:2 + (b + 1) * P], ident,
                           after=[dve.last], done=b == 3)
        dve(v.tensor_copy, vnat[:, 1:5, :], bank[6][:].rearrange("p (b n) -> p b n", b=4), after=[pe.last])
        t_v = [dve.last, act.last]
        prog.interleave(*[delayed(attention_group(kv, j, t_kd, t_v), 2 * (2 * kv + j))
                          for kv in range(2) for j in range(2)], conv1(), rwkv_shift())

    def attention_group(kv, j, t_kd, t_v):
        chain = 2 * kv + j
        b0 = 2 * chain
        S, PT = att_s[:, chain], att_pt[chain]
        m, e1, den = (small[:, o + 4 * chain:o + 4 * chain + 4] for o in (48, 64, 80))
        sinks = c1("sinks")[:, 4 * kv:4 * kv + 4]
        for b in (j, j + 2):
            pe.wait(t_kd, *t_v, act.last, dve.last)

            for h in range(4):
                pr = 64 * (h % 2)
                mm(bank[b0 + h % 2][:, (h // 2) * 256:(h // 2) * 256 + 256],
                   PJ[pr:pr + 64, 2 * kv + h // 2, 2 + b * P:2 + (b + 1) * P],
                   kdup[pr:pr + 64, kv, b * P:b * P + 256], True, True, done=h >= 2)
            yield
            msk = k_("attmask")[:, (0 if b == 0 else 256):(0 if b == 0 else 256) + 256]
            for h in range(4):
                dve(v.scalar_tensor_tensor, S[:, h, :], bank[b0 + h % 2][:, (h // 2) * 256:(h // 2) * 256 + 256],
                    HD ** -0.5, msk, ALU.mult, ALU.add, after=[pe.last])
            yield
            dve(v.tensor_reduce, m, S, AX.X, ALU.max)
            dve(v.tensor_tensor, m, m, sinks, ALU.max)
            dve(v.tensor_tensor, e1, sinks, m, ALU.subtract)
            dve(v.tensor_scalar, m, m, -1.0, None, ALU.mult)
            yield
            act.wait(dve.last)
            for h in range(4):
                act(s_.activation, S[:, h, :], S[:, h, :], ACT.Exp, bias=m[:, h:h + 1], accum_out=den[:, h:h + 1])
            act(s_.activation, e1, e1, ACT.Exp)
            yield
            dve(v.tensor_tensor, den, den, e1, ALU.add, after=[act.last])
            dve(v.reciprocal, den, den)
            t_p = []
            for h in range(4):
                f = (act, s_.activation, (ACT.Identity,), {"scale": den[:, h:h + 1]}) if h % 2 else \
                    (dve, v.tensor_scalar, (den[:, h:h + 1], None, ALU.mult), {})
                t_p.append(f[0](f[1], S[:, h, :], S[:, h, :], *f[2], after=[dve.last], **f[3]))
            yield
            for q in range(2):
                for i in range(4 * q, 4 * q + 4):
                    prog.transpose(bank[b0 + q][:, (i % 4) * P:(i % 4 + 1) * P],
                                   S[:, i // 2, (i % 2) * P:(i % 2 + 1) * P], ident, after=t_p, done=i % 4 == 3)
                f = (dve, v.tensor_copy) if q else (act, s_.copy)
                f[0](f[1], PT[:, 4 * q:4 * q + 4, :], bank[b0 + q][:].rearrange("p (b n) -> p b n", b=4),
                     after=[pe.last])
            yield
            pe.wait(act.last, dve.last)
            for h in range(4):
                pr = 64 * (h % 2)
                for x in range(2):
                    mm(bank[b0 + h % 2][pr:pr + 64, (h // 2) * P:(h // 2 + 1) * P],
                       vnat[:, b + x, 64 * kv:64 * kv + 64], PT[:, 2 * h + x, :], x == 0, x == 1,
                       done=h == 3 and x == 1)
            yield
            y = att_y[chain]
            src = [bank[b0 + x][64 * x:64 * x + 64, 0:256].rearrange("p (i n) -> p i n", i=2) for x in range(2)]
            act(s_.copy, y[0:64], src[0], after=[pe.last, dve.last])
            dve(v.tensor_copy, y[64:128], src[1], after=[pe.last])
            split_store(H1H[:, 2 * kv:2 * kv + 2, b * P:(b + 1) * P], H1L[:, 2 * kv:2 * kv + 2, b * P:(b + 1) * P],
                        y, after=[act.last])
            yield

    PR = [region("PRa", HT, [P, 4, T]), region("PRb", LT, [P, 4, T])]

    def conv1():
        w = c1("conv")
        for i in range(2):
            u = PJ[:, 18 + i, :]
            dve(v.tensor_tensor, u, u, PJ[:, 16 + i, :], ALU.mult)
            y = PJ[:, 16 + i, 2:2 + T]
            yield
            dve(v.tensor_scalar, y, u[:, 0:T], w[:, 3 * i:3 * i + 1], None, ALU.mult, after=[act.last])
            yield
            for k in (1, 2):
                dve(v.scalar_tensor_tensor, y, u[:, k:k + T], w[:, 3 * i + k:3 * i + k + 1], y, ALU.mult, ALU.add)
            yield
            dve(v.tensor_tensor, y, y, PJ[:, 14 + i, 2:2 + T], ALU.mult)
            split_store(H1H[:, 6 + i, :], H1L[:, 6 + i, :], y)
            yield

    names = ["gg", "lw", "aa", "kk", "cm", "ee", "bonus"]
    rw = {n: region("rw_" + n, G0 + 1024 * i, [P, 2, T]) for i, n in enumerate(names)}
    r1 = G0 + 7 * 1024
    rw_inv = region("rw_inv", r1, [P, 4, 3, MH, P])
    rw_nat = region("rw_nat", r1 + 6144, [P, 2, 3, 2, P])
    rw_M = region("rw_M", r1 + 7680, [P, 2, 3, MH, P])
    rw_W = region("rw_W", r1 + 10752, [P, 256])
    rw_U = region("rw_U", r1 + 11008, [P, 256])
    rw_X = region("rw_X", r1 + 11264, [P, 2, HD])
    rw_Q = [region("rw_Qa", 4 * T, [P, 2, MH, P]), region("rw_Qb", KD * TT + 4 * T, [P, 2, MH, P])]

    def rwkv_shift():
        for i in range(8):
            src = PJ[:, 6 + i, :]
            dst = PR[i // 4][:, i % 4, :]
            dve(v.tensor_tensor, dst, src[:, 1:1 + T], src[:, 2:2 + T], ALU.subtract)
            dve(v.scalar_tensor_tensor, dst, dst, c1("mu")[:, i:i + 1], src[:, 2:2 + T], ALU.mult, ALU.add)
            yield

    def rwkv():
        tile = lambda i: PR[i // 4][:, i % 4, :]
        r, k, vv = PR[0][:, 0:2, :], PR[0][:, 2:4, :], PR[1][:, 0:2, :]
        wad, gd = tile(6), tile(7)
        gg, lw, aa, kk, cm, ee, bonus = (rw[n] for n in names)
        act(s_.activation, wad[0:64, :], wad[0:64, :], ACT.Tanh, after=[dve.last])
        t_in = act(s_.activation, gd, gd, ACT.Sigmoid)
        for i in range(2):
            mm(bank[i][:], lora[0:64, 0, i * P:(i + 1) * P], wad[0:64, :], True, True, after=[t_in, dve.last])
            mm(bank[2 + i][:], lora[64:128, 0, i * P:(i + 1) * P], wad[64:128, :], True, True)
            mm(bank[4 + i][:], lora[:, 1, i * P:(i + 1) * P], gd, True, True, done=True)
        for i in range(2):
            act(s_.activation, lw[:, i, :], bank[i][:], ACT.Sigmoid, bias=c1("w0")[:, i:i + 1], after=[pe.last])
            act(s_.activation, aa[:, i, :], bank[2 + i][:], ACT.Sigmoid, bias=c1("a0")[:, i:i + 1])
            act(s_.copy, gg[:, i, :], bank[4 + i][:])
        dve(v.tensor_scalar, lw[:], lw[:], -DECAY_SCALE, None, ALU.mult, after=[act.last])
        for i in range(2):
            dve(v.tensor_scalar, kk[:, i, :], k[:, i, :], c1("k_k")[:, i:i + 1], None, ALU.mult)
            act(s_.activation, ee[:, i, :], kk[:, i, :], ACT.Square, after=[dve.last])
            mm(bank[6 + i][:], blk, ee[:, i, :], True, True, after=[act.last], done=True)
        for i in range(2):
            act(s_.activation, ee[:, i, :], bank[6 + i][:], ACT.Sqrt, after=[pe.last])
        dve(v.tensor_scalar, ee[:], ee[:], 1e-12, None, ALU.max, after=[act.last])
        dve(v.reciprocal, ee[:], ee[:])
        dve(v.tensor_tensor, kk[:], kk[:], ee[:], ALU.mult)
        for i in range(2):
            dve(v.tensor_scalar, ee[:, i, :], aa[:, i, :], -1.0, c1("k_a")[:, i:i + 1], ALU.add, ALU.mult)
            dve(v.scalar_tensor_tensor, k[:, i, :], ee[:, i, :], 1.0, k[:, i, :], ALU.add, ALU.mult)
            dve(v.scalar_tensor_tensor, ee[:, i, :], r[:, i, :], c1("r_k")[:, i:i + 1], k[:, i, :],
                ALU.mult, ALU.mult)
            mm(bank[6 + i][:], blk, ee[:, i, :], True, True, after=[dve.last], done=True)
            dve(v.tensor_tensor, bonus[:, i, :], bank[6 + i][:], vv[:, i, :], ALU.mult, after=[pe.last])
        dve(v.tensor_tensor, aa[:], aa[:], kk[:], ALU.mult)
        for i in range(2):
            for c in range(4):
                dve(v.tensor_tensor_scan, cm[:, i, c * P:(c + 1) * P], ones[:], lw[:, i, c * P:(c + 1) * P], 0.0,
                    ALU.mult, ALU.add)
        mid, end = small[:, 16:24], small[:, 24:32]
        cm4 = cm[:].rearrange("p i (c n) -> p (i c) n", c=4)
        dve(v.tensor_copy, mid, cm4[:, :, 63])
        dve(v.tensor_tensor, cm4, cm4, mid.unsqueeze(2).broadcast_to([P, 8, P]), ALU.subtract)
        dve(v.tensor_copy, end, cm4[:, :, P - 1])
        m8, e8 = mid.rearrange("p (i c) -> p i c", i=2), end.rearrange("p (i c) -> p i c", i=2)
        dve(v.tensor_tensor, e8[:, :, 0:3], e8[:, :, 0:3], m8[:, :, 1:4], ALU.add)
        t_end = act(s_.activation, end, end, ACT.Exp, after=[dve.last])
        act(s_.activation, ee[:], cm[:], ACT.Exp)
        dve(v.tensor_tensor, r, r, ee[:], ALU.mult, after=[act.last])
        dve(v.tensor_tensor, lw[:], cm[:], lw[:], ALU.subtract)
        act(s_.activation, lw[:], lw[:], ACT.Exp, after=[dve.last])
        dve(v.tensor_tensor, kk[:], kk[:], lw[:], ALU.mult, after=[act.last])
        act(s_.activation, ee[:], cm[:], ACT.Exp, scale=-1.0, after=[dve.last])
        dve(v.tensor_tensor, aa[:], aa[:], ee[:], ALU.mult, after=[act.last])
        dve(v.tensor_tensor, k, k, ee[:], ALU.mult)

        def hs(x, h, c):
            return x[64 * (h % 2):64 * (h % 2) + 64, h // 2, c * P:(c + 1) * P]

        def hb(j):
            return bank[j][:].rearrange("p (h n) -> p h n", h=MH)

        def wide(m, n=MH):
            return m.unsqueeze(1).broadcast_to([P, n, P])

        def odd_even(x, odd):
            return x.rearrange("p (a b) n -> p b a n", b=2)[:, odd]

        def inverse(c):
            L, Tm, Z = (rw_inv[:, c, j] for j in range(3))
            Q, m = rw_Q[c // 2][:, c % 2], tmpf[:, c, :].rearrange("p (h n) -> p h n", h=MH)
            b0, b1 = 2 * c, 2 * c + 1
            pe.wait(dve.last, act.last)

            for j, (lh, rh) in enumerate(((kk, aa), (aa, kk))):
                for h in range(MH):
                    mm(bank[b0 + h % 2][:, (2 * j + h // 2) * P:(2 * j + h // 2 + 1) * P], hs(lh, h, c), hs(rh, h, c),
                       True, True, done=j == 1 and h >= 2)
            yield
            for x in range(2):
                dve(v.tensor_copy, odd_even(L, x), hb(b0 + x)[:, 0:2], after=[pe.last])
            dve(v.tensor_tensor, Tm, L, wide(k_("levels")[:, 0:P]), ALU.mult)
            dve(v.tensor_tensor, Tm, Tm, wide(ident), ALU.add)
            for x in range(2):
                dve(v.tensor_tensor, odd_even(Q, x), hb(b0 + x)[:, 2:4], wide(k_("level0T"), 2), ALU.mult)
            dve(v.tensor_tensor, Q, Q, wide(ident), ALU.add)
            yield
            def level(lv):
                dve(v.tensor_tensor, m, L, wide(k_("levels")[:, lv * P:(lv + 1) * P]), ALU.mult, after=[pe.last])
            level(1)
            for lv in range(1, RW_LEVELS):
                more = lv < RW_LEVELS - 1
                for h in range(MH):
                    mm(bank[b0][:, h * P:(h + 1) * P], m[:, h, :], Q[:, h, :], True, True, after=[dve.last],
                       done=h == MH - 1)
                yield
                act(s_.copy, Z, hb(b0), after=[pe.last])
                if more:
                    level(lv + 1)
                for h in range(MH):
                    if more:
                        mm(bank[b1][:, h * P:(h + 1) * P], Z[:, h, :], Tm[:, h, :], True, True, after=[act.last])
                    mm(bank[b0][:, h * P:(h + 1) * P], Tm[:, h, :], Z[:, h, :], True, True, after=[act.last],
                       done=h == MH - 1)
                yield
                dve(v.tensor_tensor, Q, Q, hb(b0), ALU.add, after=[pe.last])
                if more:
                    dve(v.tensor_tensor, Tm, Tm, hb(b1), ALU.add)
                yield

        def prepare(c):
            nat, M = rw_nat[:, c % 2], rw_M[:, c % 2]
            t_in = [dve.last, act.last]
            for j, src in enumerate((aa, k, vv)):
                for i in range(2):
                    n = 2 * j + i
                    prog.transpose(bank[n // 4][:, (n % 4) * P:(n % 4 + 1) * P],
                                   src[:, i, c * P:(c + 1) * P], ident, after=t_in, done=n == 5)
            act(s_.copy, nat[:, 0:2], bank[0][:].rearrange("p (j i n) -> p j i n", j=2, i=2), after=[pe.last])
            act(s_.copy, nat[:, 2], bank[1][:, 0:256].rearrange("p (i n) -> p i n", i=2))
            t_nat = act.last
            yield
            pe.wait(t_nat)
            for j, (lh, rh) in enumerate(((k, kk), (aa, r), (k, r))):
                banks, at = ((2, 0), (2, 0), (1, 2))[j], (0, 2, 0)[j]
                if j == 2:
                    pe.wait(dve.last)
                for h in range(MH):
                    n = at + h // 2
                    mm(bank[banks[h % 2]][:, n * P:(n + 1) * P], hs(lh, h, c), hs(rh, h, c), True, True, done=h >= 2)
                if j == 0:
                    continue
                for i in (0, 1) if j == 1 else (2,):
                    for x in range(2):
                        dve(v.tensor_tensor, odd_even(M[:, i], x), hb(banks[x])[:, (0, 2, 0)[i]:(0, 2, 0)[i] + 2],
                            wide(k_("upper" if i == 0 else "upper_eq"), 2), ALU.mult, after=[pe.last])
                yield

        def run_state(c):
            Q, M = rw_Q[c // 2][:, c % 2], rw_M[:, c % 2]
            nat = lambda j, h: rw_nat[:, c % 2, j, h // 2, 64 * (h % 2):64 * (h % 2) + 64]
            pe.wait(dve.last, act.last)

            def w_head(h, done):
                o = bank[3][:, 64 * h:64 * h + 64]
                pr = 64 * (h % 2)
                if c:
                    mm(o, hs(kk, h, c), rw_X[pr:pr + 64, h // 2, :], True, False)
                mm(o, M[:, 0, h, :], nat(2, h), c == 0, True, done=done)
            prog.by_half(range(MH), w_head)
            dve(v.tensor_copy, rw_W[:], bank[3][:, 0:256], after=[pe.last])
            yield
            for h in range(MH):
                mm(bank[3][:, 256 + 64 * h:320 + 64 * h], Q[:, h, :], rw_W[:, 64 * h:64 * h + 64], True, True,
                   after=[dve.last], done=h == MH - 1)
            dve(v.tensor_scalar, rw_U[:], bank[3][:, 256:512], -1.0, None, ALU.mult, after=[pe.last])
            t_u = dve.last
            yield
            if c < 3:
                for h in range(MH):
                    pr = 64 * (h % 2)
                    o = bank[4 + h % 2][pr:pr + 64, 64 * (h // 2):64 * (h // 2) + 64]
                    mm(o, nat(1, h), nat(2, h), True, False)
                    mm(o, nat(0, h), rw_U[:, 64 * h:64 * h + 64], False, True, after=[t_u], done=h == MH - 1)
            for h in range(MH):
                pr = 64 * (h % 2)
                o = bank[6 + h % 2][pr:pr + 64, (h // 2) * P:(h // 2 + 1) * P]
                if c:
                    mm(o, rw_X[pr:pr + 64, h // 2, :], hs(r, h, c), True, False)
                mm(o, nat(2, h), M[:, 2, h, :], c == 0, False)
                mm(o, rw_U[:, 64 * h:64 * h + 64], M[:, 1, h, :], False, True, after=[t_u], done=h == MH - 1)
            yield
            for x in range(2):
                pr = 64 * x
                act(s_.copy, lw[pr:pr + 64, :, c * P:(c + 1) * P],
                    bank[6 + x][pr:pr + 64, 0:256].rearrange("p (i n) -> p i n", i=2), after=[pe.last])
            if c < 3:
                for x in range(2):
                    pr = 64 * x
                    for i in range(2):
                        o, ps = rw_X[pr:pr + 64, i, :], bank[4 + x][pr:pr + 64, 64 * i:64 * i + 64]
                        e = e8[pr:pr + 64, i, c:c + 1]
                        if c:
                            dve(v.tensor_tensor, o, o, ps, ALU.add, after=[pe.last])
                            dve(v.tensor_scalar, o, o, e, None, ALU.mult)
                        else:
                            dve(v.tensor_scalar, o, ps, e, None, ALU.mult, after=[pe.last, t_end])
            yield

        prog.interleave(*[inverse(c) for c in range(4)])
        prog.interleave(prepare(0))
        for c in range(4):
            prog.interleave(run_state(c), *([prepare(c + 1)] if c < 3 else []))

        def group_norm(i):
            y, d2, rs = lw[:, i, :], tmpf[:, 2 * i, :], tmpf[:, 2 * i + 1, :]
            mm(bank[2 * i][:], blk, y, True, True, after=[act.last, dve.last], done=True)
            yield
            dve(v.scalar_tensor_tensor, y, bank[2 * i][:], -1.0 / HD, y, ALU.mult, ALU.add, after=[pe.last])
            yield
            act(s_.activation, d2, y, ACT.Square, after=[dve.last])
            mm(bank[2 * i + 1][:], blk, d2, True, True, after=[act.last], done=True)
            yield
            rstd(rs, bank[2 * i + 1][:], pe.last, HD, gn_eps_col)
            yield
            dve(v.tensor_tensor, y, y, rs, ALU.mult, after=[act.last])
            dve(v.tensor_scalar, y, y, c1("gn_w")[:, i:i + 1], c1("gn_b")[:, i:i + 1], ALU.mult, ALU.add)
            dve(v.tensor_tensor, y, y, bonus[:, i, :], ALU.add)
            dve(v.tensor_tensor, y, y, gg[:, i, :], ALU.mult)
            yield
            split_store(H1H[:, 4 + i, :], H1L[:, 4 + i, :], y)
            yield
        prog.interleave(group_norm(0), group_norm(1))

    def mix1(l, ready):
        with prog.loop("mix_in", NP1 // 4) as i:
            for q in range(4):
                def ev(ps, t, free, q=q):
                    o = PJ[:, ds(i * 4 + q, 1), 2:2 + T].rearrange("p a n -> p (a n)")
                    act(s_.copy, o, ps[0], after=[t], inc=free)
                unit(wmix_in[l][:, :, ds((i * 4 + q) * P, P)], KD, X1, H1H, H1L, ev, ready=ready if q == 0 else None)
        prog.barrier()
        dve(v.memset, PJ[:, :, 0:2], 0.0)
        attention()
        prog.barrier()
        rwkv()
        prog.barrier()
        pe.wait(dve.last)
        clear_sums()
        with prog.loop("mix_out", 2) as i:
            for q in range(4):
                unit(wmix_out[l][:, :, ds((i * 4 + q) * P, P)], KD, X1, H1H, H1L,
                     evict_add(i * 4 + q, small[:, 8:16], True))

    clear_sums()
    with prog.loop("ada_first", 4) as u:
        for j in range(2):
            ada_begin(*ada1(0, u * 2 + j))
            ada_finish(*ada1(0, u * 2 + j))
            act.wait(t_x)
            gather(0, XC[:, ds(u * 2 + j, 1), TC:TT].rearrange("p a n -> p (a n)"))
    for _ in range(AHEAD):
        split_next()

    with prog.loop("layers1", DEPTH) as l:
        prog.dma(act, lora[:], a["lora"][l], in_lora)
        dve(v.tensor_copy, cols1[:], cols1_all[:, ds(l * NC1, NC1)])
        pe.wait(in_lora.now())
        shift = stage_cols(c1("g_ffn1"), 0)
        ready = norm_mod(H1H, H1L, [(TC, 0, T, small[:, 0:8], shift)], True)

        def out_0(c, i, x):
            if c == 0:
                return ada1(l, i * 2 + (30 + x))
            if c == 1:
                return ada2(l, i) if x else ada1(l, i + 34)
            return None
        ffn(l, 0, ready, lambda c, j: ada1(l, j + (8 + 8 * c)), out_0, lambda: stage_gate(0))
        prog.barrier()
        shift = stage_cols(c1("g_mix"), 3)
        stage_gate(3)
        mix1(l, norm_mod(H1H, H1L, [(TC, 0, T, small[:, 0:8], shift)], True))
        prog.barrier()
        shift = stage_cols(c1("g_ffn2"), 6)
        stage_gate(6)
        ready = norm_mod(H1H, H1L, [(TC, 0, T, small[:, 0:8], shift)], True)

        def out_1(c, i, x):
            if c == 0:
                return ada2(l, i + 22) if x else ada1(1, i + 6)
            return ada2(l, i * 2 + (2 + x)) if c == 1 else None
        ffn(l, 1, ready, lambda c, j: ada1(1, j) if c == 2 else ada2(l, j + (6 + 8 * c)), out_1)
        prog.barrier()

    QK = region("QK", G0, [P, 8, TT])
    SO = region("SO", G0 + 6144, [P, MH, TT])
    VN = region("VN", G0 + 9216, [P, TT // P, 512])
    CUW = TT + 4 * 15
    CU = region("CU", G0 + 12288, [P, 2, CUW])
    UT = region("UT", G0 + 12288 + 2 * CUW, [P, 2, TT])
    GR = region("GR", G0 + 15480, [P, TT])
    RAW = region("RAW", G0 + 16248, [P, 2, TT + 4])
    VF = [region("VFa", G0 + 12288, [P, 3, 4, P]), region("VFb", G0 + 16248, [P, 3, 4, P])]
    DFT = [region("DFT_cos", 0, [P, 4, T]), region("DFT_sin", KD * TT, [P, 4, T])]
    DFTC = [region("DFTC_cos", 2048, [P, 2, TC]), region("DFTC_sin", KD * TT + 2048, [P, 2, TC])]
    CA = region("CA", G0 + 17792, [P, 2, TT])
    VT = nc.alloc_sbuf_tensor_at("VT", [P, 2, TT], F32, offset=tmpf_at)
    vt_read = {}
    GI = region("GI", G0 + 16248, [4, 4, TT])
    MC = region("MC", G0 + 12288, [4, 2, TT])
    GS = region("GS", G0 + 13824, [P, TT // P, 2, MH])
    WT = region("WT", G0 + 13944, [P, 2, 2, T])
    WS = region("WS", G0 + 15992, [P, 2, T])
    HA = region("HA", G0 + 17016, [P, T])
    OUT = region("OUT", G0 + 12288, [P, KD, TT])
    POS = region("POS", G0, [P, KD, T])
    assert 16248 + 3072 <= RN - G0

    w_in2 = a["w_in_2"].rearrange("l (k p) n -> l p k n", p=P)
    w_out2 = a["w_out_2"].rearrange("l (k p) n -> l p k n", p=P)
    w_mlp1 = a["w_mlp1_2"].rearrange("l (k p) n -> l p k n", p=P)
    w_mlp2 = a["w_mlp2_2"].rearrange("l (k p) n -> l p k n", p=P)
    
    def m2(l, stream, row):
        o = l * 96 + stream * 48 + row * 8
        return mod2[:, o:o + 8]

    def tile_evict(dst):
        def go(ps, t, free):
            act(s_.copy, dst[:, TC:TT], ps[0], after=[t], inc=None if len(ps) > 1 else free)
            if len(ps) > 1:
                act(s_.copy, dst[:, 0:TC], ps[1], inc=free)
        return go

    def value_tile(src, tile):
        parts = []

        def ev(ps, t, free):
            y = VT[:, tile % 2, :]
            act(s_.copy, y[:, TC:TT], ps[0], after=[t, *vt_read.get(tile - 2, ())])
            act(s_.copy, y[:, 0:TC], ps[1])
            parts.append((y, act.last, free))
        s = state["n"] % SLOTS
        unit(src, KD, XB, HH, HL, ev)
        yield
        y, t, free = parts[0]
        for b in range(TT // P):
            prog.transpose(bank[s + 4 * (b // 4)][:, (b % 4) * P:(b % 4 + 1) * P], y[:, b * P:(b + 1) * P], ident,
                           after=[t], done=b == TT // P - 1)
        vt_read[tile] = [pe.last]
        act(s_.copy, VN[:, 0:4, tile * P:(tile + 1) * P], bank[s][:].rearrange("p (b n) -> p b n", b=4),
            after=[pe.last])
        act(s_.copy, VN[:, 4:6, tile * P:(tile + 1) * P], bank[s + 4][:, 0:256].rearrange("p (b n) -> p b n", b=2),
            inc=free)
        yield

    def project(l, ctx, ready):
        both = XB if ctx else X0

        def cols_of(at):
            return w_in2[l][:, :, ds(at, P)]

        dve(v.memset, CU[:], 0.0)
        for i in range(2):
            def ev_gate(ps, t, free):
                act(s_.activation, tmpf[:, 0, :], ps[0], ACT.Sigmoid, after=[t, dve.last],
                    inc=None if len(ps) > 1 else free)
                if len(ps) > 1:
                    act(s_.activation, tmpf[:, 1, 0:TC], ps[1], ACT.Sigmoid, inc=free)

            def ev_a(ps, t, free, i=i):
                dve(v.tensor_tensor, CU[:, i, TC + 45:TC + 45 + T], ps[0], tmpf[:, 0, :], ALU.mult,
                    after=[t, act.last], inc=None if len(ps) > 1 else free)
                if len(ps) > 1:
                    dve(v.tensor_tensor, CU[:, i, 15:15 + TC], ps[1], tmpf[:, 1, 0:TC], ALU.mult, inc=free)
            unit(cols_of(C_OFF + 256 + i * P), KD, both, HH, HL, ev_gate, ready=ready if i == 0 else None)
            unit(cols_of(C_OFF + i * P), KD, both, HH, HL, ev_a)
        pe.wait(*ready[1][KD - 1])
        taps = conv31_taps(ctx)

        def some_taps():
            for _ in range(2):
                next(taps, None)
        for i in range(2):
            unit(cols_of(F_OFF + i * P), KD, both, HH, HL, tile_evict(UT[:, i, :]))
            some_taps()
        unit(cols_of(G_OFF), KD, XB, HH, HL, tile_evict(GR[:, :]))
        some_taps()
        values = []
        for i in range(4):
            values.append(value_tile(cols_of(1024 + i * P), i))
            next(values[i])
            if i:
                next(values[i - 1])
            some_taps()
        for q in range(4):
            def ev_o(ps, t, free, q=q):
                act(s_.activation, SO[:, q, TC:TT], ps[0], ACT.Sigmoid, after=[t],
                    inc=None if len(ps) > 1 else free)
                if len(ps) > 1:
                    act(s_.activation, SO[:, q, 0:TC], ps[1], ACT.Sigmoid, inc=free)
            unit(cols_of(1536 + q * P), KD, both, HH, HL, ev_o)
            if q == 0:
                next(values[3])
            some_taps()
        dve(v.memset, RAW[:], 0.0)
        wq = cols2[:, COLS2["qk_conv"][0]:COLS2["qk_conv"][0] + 24]
        dve(v.tensor_scalar, wq[:, 12:24], wq[:, 12:24], 128.0 ** -0.5, None, ALU.mult)
        act.wait(dve.last)
        for half in range(2):
            segs = XB if half or ctx else X0
            for q in range(4):
                def ev(ps, t, free, q=q, half=half):
                    r = RAW[:, q % 2, :]
                    act(s_.copy, r[:, TC + 3:TC + 3 + T], ps[0], after=[t, dve.last],
                        inc=None if len(ps) > 1 else free)
                    if len(ps) > 1:
                        act(s_.copy, r[:, 1:1 + TC], ps[1], inc=free)
                    for r0, t0, nt in [(TC + 2, TC, T), (0, 0, TC)][:len(ps)]:
                        o = QK[:, 4 * half + q, t0:t0 + nt]
                        w = wq[:, 12 * half + 3 * q:12 * half + 3 * q + 3]
                        dve(v.tensor_scalar, o, r[:, r0:r0 + nt], w[:, 0:1], None, ALU.mult, after=[act.last])
                        for k in (1, 2):
                            dve(v.scalar_tensor_tensor, o, r[:, r0 + k:r0 + k + nt], w[:, k:k + 1], o,
                                ALU.mult, ALU.add)
                unit(cols_of(half * 512 + q * P), KD, segs, HH, HL, ev)
                some_taps()

    def fourier(ctx):
        t_tab, t_read = None, {}
        for j, n in enumerate(("cos", "sin")):
            t_tab = prog.dma(act, DFT[j][:], a["dft_" + n], in_table)
            t_tab = prog.dma(act, DFTC[j][:], a["dftc_" + n], in_table)
        for b in range(0 if ctx else 2, TT // P):
            for x, m in enumerate((k_("c64"), k_("s64"))):
                for i in range(2):
                    mm(bank[b % 2][:, (2 * x + i) * P:(2 * x + i + 1) * P], UT[:, i, b * P:(b + 1) * P], m,
                       True, True, after=[t_read.get(b - 2)], done=x == 1 and i == 1)
            t_read[b] = act(s_.copy, VF[b // 3][:, b % 3].rearrange("p x n -> p (x n)"), bank[b % 2][:],
                            after=[pe.last])
            yield
        pe.wait(act.last, t_tab)
        for b0, nb, t0, nt, tab in [(2, 4, TC, T, DFT), (0, 2, 0, TC, DFTC)][:2 if ctx else 1]:
            for i in range(2):
                n = 0
                ps = bank[4 + i + (0 if b0 else 2)][:, 0:nt]
                for x in range(2):
                    for b in range(b0, b0 + nb):
                        mm(ps, VF[b // 3][:, b % 3, 2 * x + i, :], tab[x][:, b - b0, :], n == 0, n == 2 * nb - 1,
                           done=n == 2 * nb - 1)
                        n += 1
                y = tmpf[:, i, 0:nt]
                act(s_.copy, y, ps, after=[pe.last, dve.last])
                split_store(HH[:, 4 + i, t0:t0 + nt], HL[:, 4 + i, t0:t0 + nt], y)
                yield

    def conv31_parts(ctx):
        return [(TC, T, TC + 30), (0, TC, 0)][:2 if ctx else 1]

    def conv31_taps(ctx):
        w = c2("w_dw")
        for k in range(K2):
            for i in range(2):
                for t0, nt, u0 in conv31_parts(ctx):
                    o, u, wk = CA[:, i, t0:t0 + nt], CU[:, i, u0 + k:u0 + k + nt], w[:, K2 * i + k:K2 * i + k + 1]
                    if k == 0:
                        dve(v.tensor_scalar, o, u, wk, c2("b_dw")[:, i:i + 1], ALU.mult, ALU.add)
                    else:
                        dve(v.scalar_tensor_tensor, o, u, wk, o, ALU.mult, ALU.add)
            yield

    def conv31_finish(ctx):
        for t0, nt, _ in conv31_parts(ctx):
            tiles = [CA[:, i, t0:t0 + nt] for i in range(2)]
            sq2 = [tmpf[:, 2 + i, 0:nt] for i in range(2)]
            for j, y in enumerate(tiles):
                mm(bank[2][:, 0:nt], ones[:], y, j == 0, j == 1, after=[dve.last, act.last], done=True)
            yield
            for j, y in enumerate(tiles):
                dve(v.scalar_tensor_tensor, y, bank[2][:, 0:nt], -1.0 / 256, y, ALU.mult, ALU.add, after=[pe.last])
                act(s_.activation, sq2[j], y, ACT.Square, after=[dve.last])
            yield
            for j in range(2):
                mm(bank[3][:, 0:nt], ones[:], sq2[j], j == 0, j == 1, after=[act.last], done=True)
            yield
            rs = sq2[0]
            rstd(rs, bank[3][:, 0:nt], pe.last, 256, eps_col)
            yield
            for i, y in enumerate(tiles):
                dve(v.tensor_tensor, y, y, rs, ALU.mult, after=[act.last])
                dve(v.tensor_scalar, y, y, c2("g_ln")[:, i:i + 1], c2("b_ln")[:, i:i + 1], ALU.mult, ALU.add)
                act(s_.activation, y, y, ACT.Silu, after=[dve.last])
                yield
            for i, y in enumerate(tiles):
                split_store(HH[:, 6 + i, t0:t0 + nt], HL[:, 6 + i, t0:t0 + nt], y)
            yield

    def gates():
        g16 = GR[0:16, :]
        dve(v.tensor_scalar, g16, g16, c2("b_gate")[0:16, :], None, ALU.add)
        for j in range(4):
            t = prog.dma(act, GI[:, j // 2 + 2 * (j % 2), :], GR[4 * j:4 * j + 4, :], gates_in, after=[dve.last])
        def direction(d):
            f, m = GI[:, 2 + d, :], MC[:, d, :]
            act(s_.activation, m, f, ACT.Abs, after=[t])
            yield
            act(s_.activation, m, m, ACT.Exp, scale=-1.0)
            yield
            act(s_.activation, m, m, ACT.Ln, bias=ones[0:4, 0:1])
            dve(v.scalar_tensor_tensor, f, f, 0.0, m, ALU.min, ALU.subtract, after=[act.last])
            yield
            g = GI[:, d, :]
            one = ones[0:4, 0:1].broadcast_to([4, TT])

            def scan(out, inp, op):
                if d == 0:
                    dve(v.tensor_tensor_scan, out, one, inp, 0.0, ALU.mult, op)
                else:
                    dve(v.tensor_tensor_scan, out[:, 0:TC][:, ::-1], one[:, 0:TC], inp[:, 0:TC][:, ::-1], 0.0,
                        ALU.mult, op)
                    dve(v.tensor_tensor_scan, out[:, TC:TT][:, ::-1], one[:, 0:T], inp[:, TC:TT][:, ::-1],
                        out[:, 0:1], ALU.mult, op)
            scan(m, f, ALU.add)
            dve(v.tensor_copy, f, m)
            dve(v.tensor_tensor, g, g, f, ALU.subtract)
            scan(m, g, ALU.max)
            dve(v.tensor_tensor, f, f, m, ALU.add)
        prog.interleave(direction(0), direction(1))
        for b in range(TT // P):
            for d in range(2):
                at = (2 * b + d) * MH
                prog.transpose(bank[6][:, at:at + MH], GI[:, d, b * P:(b + 1) * P], ident[0:4, 0:4],
                               after=[dve.last], done=True)
        dve(v.tensor_copy, GS[:].rearrange("p b d h -> p (b d h)"), bank[6][:, 0:TT // P * 2 * MH], after=[pe.last])

    def mlstm_main(h, q0, nt, sources, x, shared):
        sel = k_("sel")[0:4, h * P:(h + 1) * P]
        bc = [tmpf[:, 0, 0:nt], tmpf[:, 1, 0:nt]]
        n = len(sources)
        for d in range(2):
            mm(bank[6 + d][:, 0:nt], sel, MC[:, d, q0:q0 + nt], True, True, after=[act.last], done=True)
            act(s_.copy, bc[d], bank[6 + d][:, 0:nt], after=[pe.last])
        shared["bc_read"] = act.last
        t_s, t_e, s_read, w_read = {}, {}, {}, {}

        def span(ji, d):
            rel = sources[ji][1]
            return (0, nt) if rel is None else ((rel * P, nt) if d == 0 else (0, (rel + 1) * P))

        def ahead(ji):
            j, rel = sources[ji]
            t_s[ji] = mm(bank[4 + ji % 2][:, 0:nt], QK[:, 4 + h, j * P:(j + 1) * P], QK[:, h, q0:q0 + nt], True, True,
                         after=[s_read.get(ji - 2, shared.get("den_read"))], done=True)
            for d in range(2):
                lo, hi_ = span(ji, d)
                t_e[ji, d] = act(s_.activation, WT[:, ji % 2, d, lo:hi_], bc[d][:, lo:hi_], ACT.Exp,
                                 bias=GS[:, j, d, h:h + 1], after=w_read.get((ji - 2, d), ()))
        ahead(0)
        ahead(1)
        yield
        for ji, (j, rel) in enumerate(sources):
            first, last = ji == 0, ji == n - 1
            for d in range(2):
                lo, hi_ = span(ji, d)
                W = WT[:, ji % 2, d]
                if rel is not None:
                    wd = W[:, rel * P:(rel + 1) * P]
                    dve(v.scalar_tensor_tensor, wd, wd, 1.0, k_("upper_eq" if d == 0 else "lower_eq"),
                        ALU.min, ALU.mult, after=[t_e[ji, d]])
                dve(v.tensor_tensor, W[:, lo:hi_], W[:, lo:hi_], bank[4 + ji % 2][:, lo:hi_], ALU.mult,
                    after=[t_e[ji, d], t_s[ji]])
                s_read[ji] = dve.last
                if ji < 2 and hi_ - lo < nt:
                    z0, z1 = (hi_, nt) if lo == 0 else (0, lo)
                    dve(v.memset, W[:, z0:z1], 0.0)
                    lo, hi_ = 0, nt
                t_m = mm(bank[2 * x + d][:, lo:hi_], VN[:, j, h * P:(h + 1) * P], W[:, lo:hi_], first, last,
                         after=[dve.last], done=True)
                if ji == 1:
                    dve(v.tensor_tensor, WS[:, d, 0:nt], WT[:, 0, d, 0:nt], W[:, 0:nt], ALU.add,
                        after=[shared.get("ws_read")])
                elif ji > 1:
                    dve(v.tensor_tensor, WS[:, d, lo:hi_], WS[:, d, lo:hi_], W[:, lo:hi_], ALU.add)
                w_read[ji, d] = (t_m, dve.last)
                if ji == 1:
                    w_read[0, d] = (t_m, dve.last)
            if 0 < ji < n - 1:
                ahead(ji + 1)
            yield

    def mlstm_tail(h, q0, nt, x, shared):
        y = HA[:, 0:nt]
        shared["den_read"] = None
        for d in range(2):
            fl, den = tmpf[:, 2 + d, 0:nt], bank[4 + d][:, 0:nt]
            dve(v.scalar_tensor_tensor, fl, den, -1.0, fl, ALU.mult, ALU.max)
            dve(v.tensor_tensor, fl, fl, den, ALU.max)
        shared["den_read"] = dve.last
        yield
        for d in range(2):
            fl = tmpf[:, 2 + d, 0:nt]
            dve(v.reciprocal, fl, fl)
            dve(v.tensor_tensor, y if d == 0 else fl, fl, bank[2 * x + d][:, 0:nt], ALU.mult)
            yield
        dve(v.tensor_tensor, y, y, tmpf[:, 3, 0:nt], ALU.add)
        mm(bank[6][:, 0:nt], ones[:], y, True, True, after=[dve.last, shared.get("bc_read")], done=True)
        yield
        dve(v.scalar_tensor_tensor, y, bank[6][:, 0:nt], -1.0 / P, y, ALU.mult, ALU.add, after=[pe.last])
        sq2 = tmpf[:, 2, 0:nt]
        act(s_.activation, sq2, y, ACT.Square, after=[dve.last])
        mm(bank[7][:, 0:nt], ones[:], sq2, True, True, after=[act.last], done=True)
        yield
        rstd(sq2, bank[7][:, 0:nt], pe.last, P, eps_col)
        yield
        dve(v.tensor_tensor, y, y, sq2, ALU.mult, after=[act.last])
        dve(v.scalar_tensor_tensor, y, y, c2("g_mlstm")[:, h:h + 1], SO[:, h, q0:q0 + nt], ALU.mult, ALU.mult)
        yield
        split_store(HH[:, h, q0:q0 + nt], HL[:, h, q0:q0 + nt], y)
        yield

    def mlstm(ctx):
        pe.wait(act.last, dve.last)
        act.wait(dve.last)
        shared, tail = {}, None
        x_sources = [(0, None), (1, None)] + [(2 + r, r) for r in range(4)]
        jobs = [(h, TC, T, x_sources) for h in range(MH)]
        if ctx:
            jobs += [(h, 0, TC, [(0, 0), (1, 1)]) for h in range(MH)]
        for i, (h, q0, nt, sources) in enumerate(jobs):
            main = mlstm_main(h, q0, nt, sources, i % 2, shared)
            prog.interleave(*([tail] if tail else []), main)
            sel = k_("sel")[0:4, h * P:(h + 1) * P]
            for d in range(2):
                mm(bank[6 + d][:, 0:nt], sel, GI[:, 2 + d, q0:q0 + nt], True, True, after=[dve.last, act.last],
                   done=True)
                act(s_.activation, tmpf[:, 2 + d, 0:nt], bank[6 + d][:, 0:nt], ACT.Exp, after=[pe.last])
            for d in range(2):
                mm(bank[4 + d][:, 0:nt], ones[:], WS[:, d, 0:nt], True, True, after=[dve.last], done=True)
            shared["ws_read"] = pe.last
            dve.wait(pe.last, act.last)
            tail = mlstm_tail(h, q0, nt, i % 2, shared)
        prog.interleave(tail)

    def post_norm_add(l, segs, g, row):
        def chain(stream, t0, nt, bk):
            gg = small[:, 16 + 8 * stream:24 + 8 * stream]
            dve(v.tensor_tensor, gg, g, m2(l, stream, row), ALU.mult)
            sum_gathered(stream, nt, bk)
            yield
            r = SQ[stream]
            t = rstd(r, bank[bk][:, 0:nt], pe.last, D, eps_col, inc=bank_free[bk])
            for k in range(KD):
                o = OUT[:, k, t0:t0 + nt]
                dve(v.scalar_tensor_tensor, o, o, gg[:, k:k + 1], r, ALU.mult, ALU.mult, after=[t])
                dve(v.tensor_tensor, XC[:, k, t0:t0 + nt], XC[:, k, t0:t0 + nt], o, ALU.add)
                yield
        prog.interleave(*[chain(*seg, bk) for seg, bk in zip(segs, (4, 5))])

    def mod_norm(l, segs, g, row):
        items = []
        for stream, t0, nt in segs:
            gs = small[:, 8 * stream:8 * stream + 8]
            dve(v.tensor_scalar, gs, m2(l, stream, row + 1), 1.0, None, ALU.add)
            dve(v.tensor_tensor, gs, gs, g, ALU.mult)
            items.append((t0, t0, nt, gs, m2(l, stream, row)))
        return norm_mod(HH, HL, items)

    def out_evict(n, first, last):
        def go(ps, t, free):
            for j, (t0, nt) in enumerate([(TC, T), (0, TC)][:len(ps)]):
                inc = free if j == len(ps) - 1 else None
                o = OUT[:, ds(n, 1), t0:t0 + nt].rearrange("p a n -> p (a n)")
                if first:
                    dve(v.tensor_copy, o, ps[j], after=[t], inc=inc)
                else:
                    dve(v.tensor_tensor, o, o, ps[j], ALU.add, after=[t], inc=inc)
            if last:
                for j, (t0, nt) in enumerate([(TC, T), (0, TC)][:len(ps)]):
                    gather(j, OUT[:, ds(n, 1), t0:t0 + nt].rearrange("p a n -> p (a n)"))
        return go

    def mlp(l, ctx, final, ready):
        both = XB if ctx else X0
        for c in range(4):
            with prog.loop(f"mlp{l}_in{c}", 2) as i:
                for q in range(4):
                    def ev(ps, t, free, q=q):
                        for j, (t0, nt) in enumerate([(TC, T), (0, TC)][:len(ps)]):
                            y = tmpf[:, q % 2 + 2 * j, 0:nt]
                            hi, lo = (g[:, ds(i * 4 + q, 1), t0:t0 + nt].rearrange("p a n -> p (a n)")
                                      for g in (GH, GL))
                            act(s_.activation, y, ps[j], ACT.Relu, after=[t])
                            dve(v.tensor_tensor, y, y, ps[j], ALU.mult, after=[act.last])
                            split_store(hi, lo, y, inc=free if j == len(ps) - 1 else None)
                    unit(w_mlp1[l][:, :, ds((i * 4 + (q + 8 * c)) * P, P)], KD, both, HH, HL, ev,
                         ready=ready if c == 0 and q == 0 else None)
            made = [[bank_free[max(k - 4, 0)].now()] for k in range(KD)]
            if c == 3:
                clear_sums(2)
            with prog.loop(f"mlp{l}_out{c}", 2) as i:
                for q in range(4):
                    unit(w_mlp2[l][:, 8 * c:8 * c + 8, ds((i * 4 + q) * P, P)], KD, both, GH, GL,
                         out_evict(i * 4 + q, c == 0, c == 3), ready=[made] * len(both) if q == 0 else None)
        if final:
            for _ in range(AHEAD):
                load(a["const"][:, 0:KD * P].rearrange("p (k n) -> p k n", k=KD))
                state["n"] += 1

    def block2(l):
        ctx = l < DEPTH - 1
        segs = [(0, TC, T), (1, 0, TC)]
        kept = segs if ctx else segs[:1]
        dve(v.tensor_copy, cols2[:], cols2_all[:, l * NC2:(l + 1) * NC2])
        project(l, ctx, mod_norm(l, segs, c2("g_pre_mix"), 0))
        prog.barrier()
        prog.interleave(fourier(ctx), conv31_finish(ctx))
        prog.barrier()
        gates()
        prog.barrier()
        mlstm(ctx)
        prog.barrier()
        pe.wait(dve.last)
        clear_sums(2)
        with prog.loop(f"out{l}", 2) as i:
            for q in range(4):
                unit(w_out2[l][:, :, ds((i * 4 + q) * P, P)], KD, XB if ctx else X0, HH, HL,
                     out_evict(i * 4 + q, True, True))
        prog.barrier()
        post_norm_add(l, kept, c2("g_post_mix"), 2)
        mlp(l, ctx, not ctx, mod_norm(l, kept, c2("g_pre_mlp"), 3))
        prog.barrier()
        post_norm_add(l, kept, c2("g_post_mlp"), 5)
        prog.barrier()

    t_pos = prog.dma(act, POS[:], a["posT"], in_table)
    dve(v.tensor_tensor, XC[:, :, TC:TT], XC[:, :, TC:TT], POS[:], ALU.add, after=[t_pos])
    prog.barrier()
    for l in range(DEPTH):
        block2(l)
    prog.dma(sp, a["outT"], XC[:, :, TC:TT], out_done, after=[dve.last])
    sp.wait(out_done.now())
    return prog.recorded


def _columns(parts, table, total):
    out = np.zeros((DEPTH, P, total), np.float32)
    for name, (o, w) in table.items():
        out[:, :, o:o + w] = parts[name]
    return np.ascontiguousarray(out.transpose(1, 0, 2).reshape(P, DEPTH * total))


def _vec(x):
    x = np.asarray(x).reshape(DEPTH, -1, P)
    return x.transpose(0, 2, 1)


def _taps(x):
    x = np.asarray(x)
    k = x.shape[1]
    return x.reshape(DEPTH, k, -1, P).transpose(0, 3, 2, 1).reshape(DEPTH, P, -1)


def _shape_constants():
    p, f = np.arange(P)[:, None], np.arange(P)[None, :]
    out = np.zeros((P, NCONST), np.float32)

    def put(name, x):
        o, w = CONST[name]
        out[:x.shape[0], o:o + w] = x

    put("ident", (p == f).astype(np.float32))
    put("blk", (p // HD == f // HD).astype(np.float32))
    q, k = np.arange(P)[:, None], np.arange(2 * P)[None, :] - P
    open_ = (q - k >= 0) & (q - k < P)
    put("attmask", np.concatenate([np.where(open_ & (k >= 0), 0, -1e30), np.where(open_, 0, -1e30)], 1))
    levels = []
    for j in range(RW_LEVELS):
        w = 1 << j
        same = (p // (2 * w)) == (f // (2 * w))
        levels.append(-(same & (p // w % 2 == 1) & (f // w % 2 == 0)).astype(np.float32))
    put("levels", np.concatenate(levels, 1))
    put("level0T", levels[0].T)
    put("upper", (p < f).astype(np.float32))
    put("upper_eq", (p <= f).astype(np.float32))
    put("lower_eq", (p >= f).astype(np.float32))
    ang = 2 * np.pi * ((p % HD) * (f % HD) % HD) / HD
    same = p // HD == f // HD
    put("c64", np.where(same, np.cos(ang), 0))
    put("s64", np.where(same, -np.sin(ang), 0))
    sel = np.zeros((4, 4, P), np.float32)
    for h in range(4):
        sel[h, h] = -1
    put("sel", sel.reshape(4, -1))
    return out


def _dft(n):
    i = np.arange(n)
    ang = 2 * np.pi * (i[:, None] * i[None, :] % n) / n
    scale = 1 / np.sqrt(n * 64)
    lay = lambda x: np.ascontiguousarray((x * scale).astype(np.float32).reshape(n // P, P, n).transpose(1, 0, 2))
    return lay(np.cos(ang)), lay(np.sin(ang))


def _positions():
    quarter = D // 4
    f32 = np.float32
    freq = np.exp(f32(-np.log(10000.0)) * np.arange(quarter, dtype=f32) / f32(quarter))
    r = np.repeat(np.arange(T // 64, dtype=f32), 64)[:, None] * freq
    c = np.tile(np.arange(64, dtype=f32), T // 64)[:, None] * freq
    pos = np.concatenate([np.sin(r), np.cos(r), np.sin(c), np.cos(c)], -1).astype(f32)
    return _transposed(pos)


def _transposed(x):
    return np.ascontiguousarray(x.T.reshape(KD, P, -1).transpose(1, 0, 2))


def host_arrays(i):
    i = {k: np.asarray(x) for k, x in i.items()}
    const = _shape_constants()
    o, w = CONST["cc"]
    for j, n in enumerate(("c", "c_2", "c_ctx_2")):
        const[:, o + 8 * j:o + 8 * j + 8] = i[n].reshape(KD, P).T
    twice = lambda x: np.concatenate([x, x], 1)[:, :, None]
    cols1 = _columns({
        "b_ada": _vec(i["b_ada"]), "g_ffn1": _vec(i["g_ffn1"]), "g_mix": _vec(i["g_mix"]),
        "g_ffn2": _vec(i["g_ffn2"]), "q_gain": twice(i["att_q_gain"]), "k_gain": twice(i["att_k_gain"]),
        "sinks": np.broadcast_to(i["att_sinks"][:, None, :], (DEPTH, P, QH)), "mu": _vec(i["rwkv_mu"]),
        "w0": _vec(i["rwkv_w0"]), "a0": _vec(i["rwkv_a0"]), "k_k": _vec(i["rwkv_k_k"]), "k_a": _vec(i["rwkv_k_a"]),
        "r_k": _vec(i["rwkv_r_k"]), "gn_w": _vec(i["rwkv_gn_w"]), "gn_b": _vec(i["rwkv_gn_b"]),
        "conv": _taps(i["conv_w"])}, COLS1, NC1)
    bg = np.zeros((DEPTH, P, 1), np.float32)
    bg[:, :16, 0] = i["b_gate_2"].reshape(DEPTH, 16)
    cols2 = _columns({
        "b_ada": _vec(i["b_ada_2"]), "g_pre_mix": _vec(i["g_pre_mix_2"]), "g_post_mix": _vec(i["g_post_mix_2"]),
        "g_pre_mlp": _vec(i["g_pre_mlp_2"]), "g_post_mlp": _vec(i["g_post_mlp_2"]),
        "qk_conv": _taps(i["w_qk_conv_2"]), "g_mlstm": _vec(i["g_mlstm_norm_2"]), "w_dw": _taps(i["w_dw_2"]),
        "b_dw": _vec(i["b_dw_2"]), "g_ln": _vec(i["g_conv_ln_2"]), "b_ln": _vec(i["b_conv_ln_2"]),
        "b_gate": bg}, COLS2, NC2)
    lora = np.zeros((DEPTH, P, 2, 256), np.float32)
    lora[:, 0:64, 0] = i["rwkv_w_w2"]
    lora[:, 64:128, 0] = i["rwkv_a_w2"]
    lora[:, :, 1] = i["rwkv_g_w2"]
    dc, dsn = _dft(T)
    cc, cs = _dft(TC)
    arrays = {"const": const, "cols1": cols1, "cols2": cols2, "lora": lora, "xT": _transposed(i["x"][0]),
              "ctxT": _transposed(i["ctx_2"][0]), "posT": _positions(), "dft_cos": dc, "dft_sin": dsn,
              "dftc_cos": cc, "dftc_sin": cs}
    for n in ("w_ada", "w_ffn1_in", "w_ffn1_out", "w_ffn2_in", "w_ffn2_out", "w_mix_in", "w_mix_out", "w_ada_2",
              "w_in_2", "w_out_2", "w_mlp1_2", "w_mlp2_2"):
        arrays[n] = np.ascontiguousarray(i[n])
    return arrays


def kernel(**inputs):
    import concourse.bacc as _bacc
    from concourse.bass_utils import run_bass_kernel_spmd as _run
    arrays = host_arrays(inputs)
    per_loop = {}
    for _ in range(2):
        nc = _bacc.Bacc("TRN2", target_bir_lowering=False, num_devices=1)
        a = {n: nc.dram_tensor("in_" + n, x.shape, F32, kind="ExternalInput").ap() for n, x in arrays.items()}
        a["outT"] = nc.dram_tensor("outT", (P, KD, T), F32, kind="ExternalOutput").ap()
        per_loop = build(nc, a, per_loop)
    r = _run(nc, [{"in_" + n: x for n, x in arrays.items()}], core_ids=[0])
    out = r.results[0]["outT"]
    return np.ascontiguousarray(out.transpose(1, 0, 2).reshape(D, T).T)[None]
```
